# Optimizing a Trainium2 kernel written in Bass

```python
import jax
import jax.numpy as jnp
from jax import lax
import numpy as np

D_MODEL = 2048
BATCH = 1
SEQ = 512
DEPTH = 1

GRID_W = 64
CTX_LEN = 256
D_POOL = 1024
POOL_WINDOWS = (2, 4, 8, 16)
N_POOL_GROUPS = 4
POOL_GROUP = D_POOL // N_POOL_GROUPS
HG_HEADS = 8
HG_DK = 128
HG_DV = 128
HG_WIDTH = HG_HEADS * HG_DK
CHUNK = 64
N_BRANCH = 2
IN_COLS = D_POOL + 5 * HG_WIDTH + N_BRANCH * D_MODEL
N_EXPERTS = 16
N_EXPERT_GROUPS = 4
EXPERTS_PER_GROUP = N_EXPERTS // N_EXPERT_GROUPS
TOP_K = 2
D_EXPERT = 512
MOE_BLOCK = 128
EPS = 1e-6

kernel_name = 'hybrid_pool_hgrn2_moe_dit'

def rmsnorm(x, w):
    x32 = x.astype(jnp.float32)
    y = x32 * lax.rsqrt(jnp.mean(x32 * x32, axis=-1, keepdims=True) + EPS)
    return (y * w.astype(jnp.float32)).astype(x.dtype)

def window_mean(u, w):
    L = u.shape[2]
    u32 = u.astype(jnp.float32)
    cs = jnp.concatenate([jnp.zeros_like(u32[:, :, :1]), jnp.cumsum(u32, axis=2)], axis=2)
    t = jnp.arange(L)
    lo = jnp.maximum(t - w // 2, 0)
    hi = jnp.minimum(t + w // 2 - 1, L - 1)
    s = jnp.take(cs, hi + 1, axis=2) - jnp.take(cs, lo, axis=2)
    cnt = (hi - lo + 1).astype(jnp.float32)
    return (s / cnt[:, None]).astype(u.dtype)

def pool_mixer(u, w_pg, pool_scale):
    outs = []
    for g, w in enumerate(POOL_WINDOWS):
        ug = u[..., g * POOL_GROUP:(g + 1) * POOL_GROUP]
        outs.append(jnp.einsum('brlc,cd->brld', window_mean(ug, w) - ug, w_pg[g]))
    return jnp.concatenate(outs, axis=-1) * pool_scale

def heads(a):
    b, t = a.shape[:2]
    return a.reshape(b, t, HG_HEADS, -1).transpose(0, 2, 1, 3).astype(jnp.float32)

def hgrn2_inputs(zq, zf_fwd, zf_bwd, zi, lb_fwd, lb_bwd):
    q = heads(jax.nn.silu(zq.astype(jnp.float32)))
    v = heads(zi)

    def gate(zf, lb):
        f = lb + (1.0 - lb) * jax.nn.sigmoid(zf.astype(jnp.float32))
        return heads(1.0 - f), heads(jnp.log(f))

    k_f, lf_f = gate(zf_fwd, lb_fwd)
    k_b, lf_b = gate(zf_bwd, lb_bwd)
    stack = lambda a, b: jnp.stack([a, jnp.flip(b, axis=2)])
    return stack(q, q), stack(k_f, k_b), stack(lf_f, lf_b), stack(v, v)

def hgrn2_scan(q, k, log_f, v, s0):
    T = q.shape[3]
    n = T // CHUNK

    def to_chunks(a):
        return jnp.moveaxis(a.reshape(a.shape[:3] + (n, CHUNK, a.shape[-1])), 3, 0)

    lower = jnp.tril(jnp.ones((CHUNK, CHUNK), dtype=bool))

    def step(S, inp):
        qc, kc, lfc, vc = inp
        b = jnp.cumsum(lfc, axis=-2)
        diff = b[..., :, None, :] - b[..., None, :, :]
        dec = jnp.exp(jnp.where(lower[:, :, None], diff, -jnp.inf))
        attn = jnp.einsum('dbhtk,dbhtsk,dbhsk->dbhts', qc, dec, kc)
        o = (jnp.einsum('dbhtk,dbhkv->dbhtv', qc * jnp.exp(b), S)
             + jnp.einsum('dbhts,dbhsv->dbhtv', attn, vc))
        bl = b[..., -1:, :]
        S = (jnp.exp(bl[..., 0, :])[..., None] * S
             + jnp.einsum('dbhsk,dbhsv->dbhkv', kc * jnp.exp(bl - b), vc))
        return S, o

    sT, o = lax.scan(step, s0, (to_chunks(q), to_chunks(k), to_chunks(log_f), to_chunks(v)))
    o = jnp.moveaxis(o, 0, 3).reshape(v.shape)
    return o, sT

def hgrn2_readout(o2, og, w_norm):
    o = o2[0] + jnp.flip(o2[1], axis=2)
    o = o * lax.rsqrt(jnp.mean(o * o, axis=-1, keepdims=True) + EPS)
    b, _, t, _ = o.shape
    o = o.transpose(0, 2, 1, 3).reshape(b, t, HG_WIDTH)
    return (o * w_norm.astype(jnp.float32) * jax.nn.silu(og.astype(jnp.float32))).astype(og.dtype)

def split_in(z):
    cuts = [D_POOL + j * HG_WIDTH for j in range(6)] + [D_POOL + 5 * HG_WIDTH + D_MODEL]
    return jnp.split(z, cuts, axis=-1)

def branch_merge(p, o2, og, gp, gh, grid, w_pg, pool_scale, hg_norm_w, w_bp, w_bh, w_out):
    b, t, _ = p.shape
    pool = pool_mixer(p.reshape((b,) + grid + (D_POOL,)), w_pg, pool_scale).reshape(b, t, D_POOL)
    hg = hgrn2_readout(o2, og, hg_norm_w)
    m = jax.nn.sigmoid(gp) * (pool @ w_bp) + jax.nn.sigmoid(gh) * (hg @ w_bh)
    return m @ w_out

def token_mixers(hl, hc, w_in, w_pg, pool_scale, hg_norm_w, lb_fwd, lb_bwd, w_bp, w_bh, w_out, need_ctx):
    b, n, _ = hl.shape
    rows = n // GRID_W
    pl, ql, ffl, fbl, il, ogl, gpl, ghl = split_in(hl @ w_in)
    pc, qc, ffc, fbc, ic, ogc, gpc, ghc = split_in(hc @ w_in)
    s0 = jnp.zeros((2, b, HG_HEADS, HG_DK, HG_DV), jnp.float32)
    o_ctx, s_ctx = hgrn2_scan(*hgrn2_inputs(qc, ffc, fbc, ic, lb_fwd, lb_bwd), s0)
    o_lat, _ = hgrn2_scan(*hgrn2_inputs(ql, ffl, fbl, il, lb_fwd, lb_bwd), s_ctx)
    yl = branch_merge(pl, o_lat, ogl, gpl, ghl, (rows, GRID_W), w_pg, pool_scale, hg_norm_w, w_bp, w_bh, w_out)
    if not need_ctx:
        return yl, None
    yc = branch_merge(pc, o_ctx, ogc, gpc, ghc, (1, hc.shape[1]), w_pg, pool_scale, hg_norm_w, w_bp, w_bh, w_out)
    return yl, yc

def moe_ffn(h, w_router, router_bias, w1, w3, w2):
    T, D = h.shape
    scores = jax.nn.sigmoid(h.astype(jnp.float32) @ w_router.astype(jnp.float32))
    sel = scores + router_bias.astype(jnp.float32)
    grp = sel.reshape(T, N_EXPERT_GROUPS, EXPERTS_PER_GROUP)
    grp_score = lax.top_k(grp, 2)[0].sum(-1)
    g_idx = jnp.argmax(grp_score, axis=-1)
    in_grp = jnp.take_along_axis(grp, g_idx[:, None, None], axis=1)[:, 0]
    _, loc = lax.top_k(in_grp, TOP_K)
    e_idx = (g_idx[:, None] * EXPERTS_PER_GROUP + loc).astype(jnp.int32)
    gate = jnp.take_along_axis(scores, e_idx, axis=1)
    gate = gate / jnp.sum(gate, axis=-1, keepdims=True)
    n_assign = T * TOP_K
    flat_e = e_idx.reshape(-1)
    flat_tok = jnp.repeat(jnp.arange(T, dtype=jnp.int32), TOP_K)
    order = jnp.argsort(flat_e)
    se, stok, sgate = flat_e[order], flat_tok[order], gate.reshape(-1)[order]
    counts = jnp.bincount(flat_e, length=N_EXPERTS)
    starts = jnp.cumsum(counts) - counts
    pcounts = (counts + MOE_BLOCK - 1) // MOE_BLOCK * MOE_BLOCK
    pends = jnp.cumsum(pcounts)
    dest = (pends - pcounts)[se] + jnp.arange(n_assign) - starts[se]
    n_blocks = -(-n_assign // MOE_BLOCK) + N_EXPERTS
    buf_tok = jnp.zeros((n_blocks * MOE_BLOCK,), jnp.int32).at[dest].set(stok)
    blk_e = jnp.minimum(jnp.searchsorted(pends, jnp.arange(n_blocks) * MOE_BLOCK, side='right'), N_EXPERTS - 1)
    xb = h[buf_tok].reshape(n_blocks, MOE_BLOCK, D)

    def expert_block(args):
        xblk, e = args
        return (jax.nn.silu(xblk @ w1[e]) * (xblk @ w3[e])) @ w2[e]

    yb = lax.map(expert_block, (xb, blk_e)).reshape(n_blocks * MOE_BLOCK, D)
    return jnp.zeros_like(h).at[stok].add(yb[dest] * sgate[:, None].astype(h.dtype))

def setup_inputs(seed: int = 0) -> dict:
    key = jax.random.key(seed)
    ks = jax.random.split(key, 22)
    D = D_MODEL
    nrm = lambda k, shape, s: jax.random.normal(k, shape, jnp.float32) * s
    return {
        'x': nrm(ks[0], (BATCH, SEQ, D), 1.0),
        'c': nrm(ks[1], (BATCH, D), 1.0),
        'ctx': nrm(ks[2], (BATCH, CTX_LEN, D), 1.0),
        'c_ctx': nrm(ks[3], (D,), 1.0),
        'w_ada': nrm(ks[4], (DEPTH, D, 6 * D), 0.5 * D ** -0.5),
        'b_ada': nrm(ks[5], (DEPTH, 6 * D), 0.01),
        'norm1_w': 1.0 + nrm(ks[6], (DEPTH, D), 0.02),
        'norm2_w': 1.0 + nrm(ks[7], (DEPTH, D), 0.02),
        'w_in': nrm(ks[8], (DEPTH, D, IN_COLS), D ** -0.5),
        'w_pool_group': nrm(ks[9], (DEPTH, N_POOL_GROUPS, POOL_GROUP, POOL_GROUP), POOL_GROUP ** -0.5),
        'pool_scale': 1.0 + nrm(ks[10], (DEPTH, D_POOL), 0.02),
        'hg_norm_w': 1.0 + nrm(ks[11], (DEPTH, HG_WIDTH), 0.02),
        'lb_logits': nrm(ks[12], (2, DEPTH, HG_WIDTH), 0.1),
        'w_branch_pool': nrm(ks[13], (DEPTH, D_POOL, D), D_POOL ** -0.5),
        'w_branch_hgrn': nrm(ks[14], (DEPTH, HG_WIDTH, D), HG_WIDTH ** -0.5),
        'w_out': nrm(ks[15], (DEPTH, D, D), D ** -0.5),
        'w_router': nrm(ks[16], (D, N_EXPERTS), D ** -0.5),
        'router_bias': nrm(ks[17], (N_EXPERTS,), 0.01),
        'w_e1': nrm(ks[18], (DEPTH, N_EXPERTS, D, D_EXPERT), D ** -0.5),
        'w_e3': nrm(ks[19], (DEPTH, N_EXPERTS, D, D_EXPERT), D ** -0.5),
        'w_e2': nrm(ks[20], (DEPTH, N_EXPERTS, D_EXPERT, D), D_EXPERT ** -0.5),
        'final_norm_w': 1.0 + nrm(ks[21], (D,), 0.02),
    }

def reference(x, c, ctx, c_ctx, w_ada, b_ada, norm1_w, norm2_w, w_in, w_pool_group, pool_scale,
              hg_norm_w, lb_logits, w_branch_pool, w_branch_hgrn, w_out, w_router, router_bias,
              w_e1, w_e3, w_e2, final_norm_w):
    b, n, d = x.shape
    sc = jax.nn.silu(c)
    scc = jax.nn.silu(c_ctx)
    lbw = jax.nn.softmax(lb_logits.astype(jnp.float32), axis=1)
    lb = jnp.cumsum(lbw, axis=1) - lbw[:, :1]
    xl, xc = x, ctx
    for i in range(DEPTH):
        last = i == DEPTH - 1
        mod_l = jnp.split((sc @ w_ada[i] + b_ada[i])[:, None, :], 6, axis=-1)
        mod_c = jnp.split(scc @ w_ada[i] + b_ada[i], 6, axis=-1)
        hl = rmsnorm(xl, norm1_w[i]) * (1 + mod_l[1]) + mod_l[0]
        hc = rmsnorm(xc, norm1_w[i]) * (1 + mod_c[1]) + mod_c[0]
        yl, yc = token_mixers(hl, hc, w_in[i], w_pool_group[i], pool_scale[i], hg_norm_w[i],
                              lb[0, i], lb[1, i], w_branch_pool[i], w_branch_hgrn[i], w_out[i], not last)
        xl = xl + mod_l[2] * yl
        hl2 = rmsnorm(xl, norm2_w[i]) * (1 + mod_l[4]) + mod_l[3]
        if last:
            f = moe_ffn(hl2.reshape(-1, d), w_router, router_bias, w_e1[i], w_e3[i], w_e2[i])
            xl = xl + mod_l[5] * f.reshape(xl.shape)
        else:
            xc = xc + mod_c[2] * yc
            hc2 = rmsnorm(xc, norm2_w[i]) * (1 + mod_c[4]) + mod_c[3]
            tokens = jnp.concatenate([hl2.reshape(-1, d), hc2.reshape(-1, d)], axis=0)
            f = moe_ffn(tokens, w_router, router_bias, w_e1[i], w_e3[i], w_e2[i])
            xl = xl + mod_l[5] * f[:b * n].reshape(xl.shape)
            xc = xc + mod_c[5] * f[b * n:].reshape(xc.shape)
    return rmsnorm(xl, final_norm_w)


_drawn_inputs = setup_inputs


def setup_inputs(seed=0):
    import zlib

    import numpy as np

    out = dict(_drawn_inputs(seed))
    spreads = {}
    factors = {'ctx': 8.0,
     'c_ctx': 7.549,
     'b_ada': 3.031,
     'norm1_w': 3.857,
     'norm2_w': 2.689,
     'pool_scale': 7.662,
     'hg_norm_w': 4.297,
     'final_norm_w': 2.759}
    for name, (base, spread) in spreads.items():
        noise = np.random.default_rng([zlib.crc32(name.encode()), seed]).standard_normal(out[name].shape)
        drawn = base * np.exp(spread * noise) if base else spread * noise
        out[name] = jnp.asarray(drawn.astype(out[name].dtype))
    for name, factor in factors.items():
        out[name] = (out[name] * factor).astype(out[name].dtype)
    return out
```

```python
from contextlib import ExitStack

import numpy as np

import concourse.bass as bass
from concourse import mybir

F32 = mybir.dt.float32
F32R = mybir.dt.float32r
I32 = mybir.dt.int32
U8 = mybir.dt.uint8
ALU = mybir.AluOpType
ACT = mybir.ActivationFunctionType
AX = mybir.AxisListType
ds = bass.ds

P = 128
D = 2048
KT = D // P
SEQ = 512
CTX = 256
NTOK = SEQ // P
NCTX = CTX // P
HEADS = 8
D_POOL = 1024
WINDOWS = (2, 4, 8, 16)
GRID_W = 64
ROWS = SEQ // GRID_W
HALO = 8
PADW = GRID_W + 2 * HALO
LEVELS = 7
NCH = SEQ // P
CTX_LEVELS = 8
E = 16
GROUPS = 4
DX = 512
BLK = 128
NXTRA = 7
NBLK = E + NXTRA
EPS = 1e-6
UNIT = 1024
SLOTS = 6
KB = 1024
BIG = 1 << 20

COL = dict(p=0, q=1024, ff=2048, fb=3072, i=4096, og=5120, gp=6144, gh=8192)
V_C, V_CC, V_N1, V_B, V_PS, V_HG, V_LB, V_ROWS = 0, 16, 32, 48, 80, 88, 96, 112


class Chain:

    def __init__(self, eng, sem):
        self.eng, self.sem, self.start, self.k = eng, sem, 0, 0

    def did(self, ins):
        ins.then_inc(self.sem, 1)
        self.k += 1

    def wait(self):
        self.eng.wait_ge(self.sem, self.start + self.k)

    def pass_waits(self):
        self.eng.sem_inc(self.sem, 1)
        self.k += 1

    def loop(self, turn, per):
        self.entry = (self.start, self.k, per)
        self.start, self.k = self.start + self.k + turn * per, 0

    def end(self, turns):
        start, k, per = self.entry
        assert self.k == per, f"{self.sem}: {self.k} instructions in a turn, {per} stated"
        self.start, self.k = start, k + turns * per


class Room:

    def __init__(self, nc, base, start_kb, end_kb):
        self.nc, self.at, self.end = nc, base + int(start_kb * KB), base + int(end_kb * KB)

    def new(self, name, shape, dtype):
        size = int(np.prod(shape[1:])) * {F32: 4, F32R: 4, I32: 4, U8: 1}[dtype]
        at = self.at
        self.at += (size + 31) // 32 * 32
        assert self.at <= self.end, f"{name} does not fit: {self.at - self.end} bytes over"
        return self.nc.alloc_sbuf_tensor_at(name, shape, dtype, offset=at)


def grow(eng, chain, QF, KG, T, T_next, half, forward, width):
    n = width // (2 * half)
    t = T.rearrange("p (n two) -> p n two", two=2)
    a, b = (1, 0) if forward else (0, 1)
    k = KG.rearrange("p (n two h) -> p n two h", two=2, h=half)
    if QF is not None:
        q = QF.rearrange("p (n two h) -> p n two h", two=2, h=half)
        chain.did(eng.tensor_tensor(q[:, :, a, :], q[:, :, a, :],
                                    t[:, :, b].unsqueeze(2).to_broadcast([P, n, half]), ALU.mult))
    last = eng.tensor_tensor(k[:, :, b, :], k[:, :, b, :],
                             t[:, :, a].unsqueeze(2).to_broadcast([P, n, half]), ALU.mult)
    if T_next is not None:
        chain.did(last)
        last = eng.tensor_tensor(T_next, t[:, :, 0], t[:, :, 1], ALU.mult)
    return last


def build(nc, x, c, ctx_tokens, c_ctx, w_ada, b_ada, norm1_w, norm2_w, w_in, w_pool_group, pool_scale,
          hg_norm_w, lb_logits, w_branch_pool, w_branch_hgrn, w_out, w_router, router_bias, w_e1, w_e3,
          w_e2, final_norm_w, consts, level_masks, pool_coefs, out):
    x_d = x[0].rearrange("(i p) d -> i p d", p=P)
    ctx_d = ctx_tokens[0].rearrange("(i p) d -> i p d", p=P)
    out_d = out[0].rearrange("(i p) d -> i p d", p=P)
    w_in_d = w_in[0].rearrange("(k p) n -> p k n", p=P)
    w_ada_d = w_ada[0].rearrange("(k p) n -> p k n", p=P)
    w_bp_d = w_branch_pool[0].rearrange("(k p) n -> p k n", p=P)
    w_bh_d = w_branch_hgrn[0].rearrange("(k p) n -> p k n", p=P)
    w_out_d = w_out[0].rearrange("(k p) n -> p k n", p=P)
    w_pg_d = w_pool_group[0].rearrange("g (k p) n -> p g k n", p=P)
    w_e1_d = w_e1[0].rearrange("e (k p) n -> e p k n", p=P)
    w_e3_d = w_e3[0].rearrange("e (k p) n -> e p k n", p=P)
    w_e2_d = w_e2[0].rearrange("e (k p) n -> e p k n", p=P)
    w_r_d = w_router.rearrange("(k p) n -> p k n", p=P)

    mod_d = nc.dram_tensor("mod_rows", [1, 4 * D], F32).ap()
    h2_d = nc.dram_tensor("h2_rows", [SEQ, D], F32).ap()
    tok_d = nc.dram_tensor("block_tokens", [NBLK * BLK, 1], F32).ap()
    y_d = nc.dram_tensor("block_outputs", [NBLK * BLK, D], F32).ap()

    stack = ExitStack()
    with stack:
        base = (nc.sbuf_base + 63) // 64 * 64
        top = (nc.sbuf_usable_end - base) / KB

        def sem(name):
            return stack.enter_context(nc.semaphore(name))

        def psum(name, shape):
            return stack.enter_context(nc.psum_tensor(name, shape, F32))

        small = Room(nc, base, 0, 10)
        ident = small.new("ident", [P, P], F32)
        upper = small.new("strict_upper", [P, P], F32)
        iota_e = small.new("iota_e", [P, E], F32)
        tok_ids = small.new("tok_ids", [P, NTOK], F32)
        ones = small.new("ones", [P, P], F32)
        masks = small.new("level_masks_sb", [P, 2, LEVELS, P], U8)
        vecT = small.new("vecT", [P, V_ROWS], F32)
        cs = small.new("silu_c", [P, 2, KT], F32)
        modT = small.new("modT", [P, 2 * KT, 2], F32)
        scale1 = small.new("scale1", [P, KT, 2], F32)
        lb_all = small.new("lb_all", [P, HEADS, 4], F32)
        lb_tmp = small.new("lb_tmp", [P, 4, 16], F32)
        stat = small.new("stat", [P, 4, 8], F32)
        lb_v = small.new("lb_v", [P, 4], F32)
        lb_p = small.new("lb_p", [P, 4], F32)
        mod_row = small.new("mod_row", [P, 512], F32)

        ada_ring = Room(nc, base, 10, 74).new("ada_ring", [P, 4, 4096], F32)
        ring_start = Room(nc, base, 74, 98)
        x_tok = ring_start.new("x_tok", [P, 3, D], F32)
        prep = Room(nc, base, 98, 114)
        vec_rows = prep.new("vec_rows", [P, P], F32)
        square_junk = prep.new("square_junk", [P, D], F32)
        mod01_row = Room(nc, base, 98, 114).new("mod01_row", [P, 4096], F32)
        masks_in = Room(nc, base, 194, 201).new("masks_in", [P, 2, LEVELS, P], F32)
        xT_ctx = Room(nc, base, 114, 130).new("xT_ctx", [P, KT, CTX], F32)
        xT_lat = Room(nc, base, 130, 162).new("xT_lat", [P, KT, SEQ], F32)
        hc_room = Room(nc, base, 162, 194)
        hc_hi = hc_room.new("hc_hi", [P, KT, CTX], F32R)
        hc_lo = hc_room.new("hc_lo", [P, KT, CTX], F32R)
        hl_room = Room(nc, base, 10, 74)
        hl_hi = hl_room.new("hl_hi", [P, KT, SEQ], F32R)
        hl_lo = hl_room.new("hl_lo", [P, KT, SEQ], F32R)
        ring = Room(nc, base, 74, 114)
        raw = ring.new("raw", [P, SLOTS, UNIT], F32)
        w_hi = ring.new("w_hi", [P, 2, UNIT], F32R)
        w_lo = ring.new("w_lo", [P, 2, UNIT], F32R)
        cw = Room(nc, base, 114, 130)
        c_sig = cw.new("c_sig", [P, 2, CTX], F32)
        c_f = cw.new("c_f", [P, 2, CTX], F32)
        c_kg = cw.new("c_kg", [P, 2, CTX], F32)
        c_T = cw.new("c_T", [P, 2, CTX], F32)
        c_vT = cw.new("c_vT", [P, CTX], F32)
        c_v = cw.new("c_v", [P, NCTX, P], F32)
        c_kgT = cw.new("c_kgT", [P, 2, NCTX, P], F32)
        s_ctx = Room(nc, base, 194, 202).new("s_ctx", [P, 2, HEADS, P], F32)
        hg = Room(nc, base, 130, 146).new("hg", [P, HEADS, SEQ], F32)
        delta = Room(nc, base, 162, 178).new("delta", [P, HEADS, SEQ], F32)
        ra = Room(nc, base, 114, 130)
        rb = Room(nc, base, 146, 162)
        rc = Room(nc, base, 178, 194)
        rd = Room(nc, base, 202, top)
        QF = [ra.new("QF_f", [P, SEQ], F32), ra.new("QF_b", [P, SEQ], F32)]
        KG = [ra.new("KG_f", [P, SEQ], F32), ra.new("KG_b", [P, SEQ], F32)]
        TT = [ra.new("T_f", [P, SEQ], F32), ra.new("T_b", [P, SEQ], F32)]
        A = [ra.new("A_f", [P, NCH, P], F32), ra.new("A_b", [P, NCH, P], F32)]
        S = [rb.new("S_f", [P, NCH, P], F32), rb.new("S_b", [P, NCH, P], F32)]
        q_sb = rb.new("q_sb", [P, SEQ], F32)
        f_sb = [rb.new("f_f", [P, SEQ], F32), rb.new("f_b", [P, SEQ], F32)]
        vT_sb = rb.new("vT_sb", [P, SEQ], F32)
        v_sb = rb.new("v_sb", [P, NCH, P], F32)
        gate_sb = rb.new("gate_sb", [P, SEQ], F32)
        up = rc.new("up", [P, ROWS, PADW], F32)
        win = [rc.new("win_a", [P, ROWS, PADW], F32), rc.new("win_b", [P, ROWS, PADW], F32)]
        pool_t = rc.new("pool_t", [P, ROWS, GRID_W], F32)
        pool_acc = rc.new("pool_acc", [P, ROWS, GRID_W], F32)
        sig_a = rc.new("sig_a", [P, SEQ], F32)
        sig_b = rc.new("sig_b", [P, SEQ], F32)
        coef = rd.new("coef", [P, 4, GRID_W], F32)
        kgT = [rd.new("kgT_f", [P, NCH - 1, P], F32), rd.new("kgT_b", [P, NCH - 1, P], F32)]
        osq = small.new("osq", [P, SEQ], F32)
        w_pg = Room(nc, base, 114, 122).new("w_pg", [P, 4, 2, 256], F32)
        ada2 = Room(nc, base, 114, 130).new("ada2", [P, 2, 4, 512], F32)
        poolT = Room(nc, base, 146, 162).new("poolT", [P, HEADS, SEQ], F32)
        m_sb = Room(nc, base, 162, 194).new("m_sb", [P, KT, SEQ], F32)
        mw = Room(nc, base, 194, top)
        acc = mw.new("ada_acc", [P, 512], F32)
        sig_gp = mw.new("sig_gp", [P, SEQ], F32)
        sig_gh = mw.new("sig_gh", [P, SEQ], F32)
        part_p = mw.new("part_p", [P, SEQ], F32)
        part_h = mw.new("part_h", [P, SEQ], F32)
        b_row = mw.new("b_row", [P, 512], F32)
        m_room = Room(nc, base, 10, 74)
        m_hi = m_room.new("m_hi", [P, KT, SEQ], F32R)
        m_lo = m_room.new("m_lo", [P, KT, SEQ], F32R)
        x2 = Room(nc, base, 114, 146).new("x2", [P, NTOK, D], F32)
        ow = Room(nc, base, 146, 162)
        x_part = ow.new("x_part", [P, NTOK, 512], F32)
        m2_part = ow.new("m2_part", [P, 512], F32)
        y_part = ow.new("y_part", [P, 2, 512], F32)
        h2 = Room(nc, base, 162, 194).new("h2", [P, NTOK, D], F32)
        nw = Room(nc, base, 42, 74)
        n2_row = nw.new("n2_row", [P, D], F32)
        m4_row = nw.new("m4_row", [P, D], F32)
        m3_row = nw.new("m3_row", [P, D], F32)
        junk2 = nw.new("junk2", [P, D], F32)
        h2T = Room(nc, base, 10, 42).new("h2T", [P, KT, SEQ], F32)
        rt_room = Room(nc, base, 194, 206)
        w_r = rt_room.new("w_r", [P, KT, E], F32)
        bias_row = rt_room.new("bias_row", [P, E], F32)
        rt = rt_room.new("rt", [P, 20, NTOK * E], F32)
        rt_small = rt_room.new("rt_small", [P, 16, E], F32)
        keep = Room(nc, base, 206, top)
        dest_i = keep.new("dest_i", [P, 2, NTOK], I32)
        gate_w = keep.new("gate_w", [P, 2, NTOK], F32)
        table_i = keep.new("table_i", [P, NBLK + 1], I32)
        idx_now = keep.new("idx_now", [P, 1], I32)
        route_i = keep.new("route_i", [P, 8], I32)
        stat2 = keep.new("stat2", [P, 4, NTOK], F32)
        table_rows = Room(nc, base, 146, 147).new("table_rows", [P, P], F32)
        e_raw = Room(nc, base, 74, 106).new("e_raw", [P, 8, UNIT], F32)
        act_room = Room(nc, base, 106, 114)
        act_sig = act_room.new("act_sig", [P, DX], F32)
        act_u = act_room.new("act_u", [P, DX], F32)
        act = act_room.new("act", [P, DX], F32)
        eh = Room(nc, base, 42, 74)
        e_hi = eh.new("e_hi", [P, 4, UNIT], F32R)
        e_lo = eh.new("e_lo", [P, 4, UNIT], F32R)
        ex = Room(nc, base, 10, 42)
        xe_hi = ex.new("xe_hi", [P, KT, BLK], F32R)
        xe_lo = ex.new("xe_lo", [P, KT, BLK], F32R)
        actT_hi = ex.new("actT_hi", [P, 4, BLK], F32R)
        actT_lo = ex.new("actT_lo", [P, 4, BLK], F32R)
        xe = Room(nc, base, 148, 156).new("xe", [P, D], F32)
        y_sb = Room(nc, base, 162, 170).new("y_sb", [P, D], F32)
        m5_row = Room(nc, base, 170, 178).new("m5_row", [P, D], F32)
        fn_row = Room(nc, base, 178, 186).new("fn_row", [P, D], F32)
        y0 = Room(nc, base, 10, 26).new("y0", [P, 2, D], F32)
        y1 = Room(nc, base, 42, 58).new("y1", [P, 2, D], F32)
        f_junk = Room(nc, base, 26, 34).new("f_junk", [P, D], F32)
        o_sb = Room(nc, base, 74, 90).new("o_sb", [P, 2, D], F32)

        T_AT = [0] + [sum(SEQ >> k for k in range(1, l)) for l in range(1, LEVELS + 1)]

        def level_T(z, l):
            return f_sb[z][:] if l == 0 else TT[z][:, T_AT[l]:T_AT[l] + (SEQ >> l)]

        def ctx_decays(eng, own, z):
            at = 0
            total = c_f[:, z, :]
            for l in range(1, CTX_LEVELS + 1):
                nxt = c_T[:, z, at:at + (CTX >> l)] if l < CTX_LEVELS else None
                own.wait()
                last = grow(eng, own, None, c_kg[:, z, :], total, nxt, 1 << (l - 1), z == 0, CTX)
                if l < CTX_LEVELS:
                    own.did(last)
                at += CTX >> l
                total = nxt
            return last

        ps = psum("ps", [P, 8, 512])
        ZA, ZB, BF, BB, BD, TR, OB, UB = range(8)

        def bank(b, n=512):
            return ps[:, b, 0:n]

        consts_in = sem("consts_in")
        vec_in = sem("vec_in")
        x_in = [sem(f"x_in{i}") for i in range(3)]
        ada_in = [sem(f"ada_in{i}") for i in range(4)]
        vec_T, vecT_rdy, cs_rdy = sem("vec_T"), sem("vecT_rdy"), sem("cs_rdy")
        c_sg = sem("c_sg")
        ssq_rdy, var_rdy, std_rdy, xn_rdy = sem("ssq_rdy"), sem("var_rdy"), sem("std_rdy"), sem("xn_rdy")
        x_T, xT_act, xT_dve = sem("x_T"), sem("xT_act"), sem("xT_dve")
        ada_mm, mod_act, mod_dve, mod_T = sem("ada_mm"), sem("mod_act"), sem("mod_dve"), sem("mod_T")
        lb_exp, lb_in = sem("lb_exp"), sem("lb_in")
        h_rdy, h_hi, h_split = sem("h_rdy"), sem("h_hi"), sem("h_split")
        raw_in = [sem(f"raw_in{i}") for i in range(SLOTS)]
        hi_done, split_done, units_done = sem("hi_done"), sem("split_done"), sem("units_done")
        v_own, a_own, p_own, sp_own = sem("v_own"), sem("a_own"), sem("p_own"), sem("sp_own")
        c_sig_f, c_sig_b, c_v_ev = sem("c_sig_f"), sem("c_sig_b"), sem("c_v_ev")
        c_kg_f, c_kg_b = sem("c_kg_f"), sem("c_kg_b")
        c_v_T, c_kg_T, c_v_rdy, c_kgT_rdy = sem("c_v_T"), sem("c_kg_T"), sem("c_v_rdy"), sem("c_kgT_rdy")
        c_s_mm, ctx_state = sem("c_s_mm"), sem("ctx_state")
        sig_q, q_rdy, sig_f, f_rdy, v_ev, v_T, v_rdy = (sem(s) for s in (
            "sig_q", "q_rdy", "sig_f", "f_rdy", "v_ev", "v_T", "v_rdy"))
        sig_bw, fb_rdy, sig_og, gate_rdy, p_ev, pool_rdy, coef_in = (sem(s) for s in (
            "sig_bw", "fb_rdy", "sig_og", "gate_rdy", "p_ev", "pool_rdy", "coef_in"))
        lv_mm = [sem("lv_mm_f"), sem("lv_mm_b")]
        lv_up = [sem("lv_up_f"), sem("lv_up_b")]
        lv_sel = [sem("lv_sel_f"), sem("lv_sel_b")]
        kg_T = [sem("kg_T_f"), sem("kg_T_b")]
        kgT_rdy = [sem("kgT_f_rdy"), sem("kgT_b_rdy")]
        u_mm = [sem("u_mm_f"), sem("u_mm_b")]
        s_rdy = [sem("s_f_rdy"), sem("s_b_rdy")]
        o_mm = [sem("o_mm_f"), sem("o_mm_b")]
        osq_rdy, n_mm, nv_rdy, rt_rdy, hg_rdy = (sem(s) for s in (
            "osq_rdy", "n_mm", "nv_rdy", "rt_rdy", "hg_rdy"))
        pad_rdy = sem("pad_rdy")
        pg_mm, pg_ev, hgw_rdy, branch_free = (sem(s) for s in (
            "pg_mm", "pg_ev", "hgw_rdy", "branch_free"))
        gp_rdy, gh_rdy, pp_rdy, m_rdy, row_mm, row_rdy, row_out, b_in = (sem(s) for s in (
            "gp_rdy", "gh_rdy", "pp_rdy", "m_rdy", "row_mm", "row_rdy", "row_out", "b_in"))
        ada2_in = [sem("ada2_in0"), sem("ada2_in1")]
        ada2_free = sem("ada2_free")
        xp_in, w_ev, x2_rdy = sem("xp_in"), sem("w_ev"), sem("x2_rdy")
        rows_in, h2_rdy, h2_T, h2T_ev, lg_mm = (sem(s) for s in (
            "rows_in", "h2_rdy", "h2_T", "h2T_ev", "lg_mm"))
        score_rdy, sel_rdy, pos_mm, dest_rdy, tok_out, tab_in, tab_T, table_rdy = (sem(s) for s in (
            "score_rdy", "sel_rdy", "pos_mm", "dest_rdy", "tok_out", "tab_in", "tab_T", "table_rdy"))
        e_in = raw_in + [sem("e_in6"), sem("e_in7")]
        e_hi_done, e_split, e_units = sem("e_hi_done"), sem("e_split"), sem("e_units")
        idx_rdy, xe_in, xe_T, xe_hi_rdy, xe_rdy = (sem(s) for s in (
            "idx_rdy", "xe_in", "xe_T", "xe_hi_rdy", "xe_rdy"))
        sg_rdy, u_rdy, act_rdy, act_T, actT_hi_rdy, actT_rdy = (sem(s) for s in (
            "sg_rdy", "u_rdy", "act_rdy", "act_T", "actT_hi_rdy", "actT_rdy"))
        y_ev, y_out = sem("y_ev"), sem("y_out")
        y_in, f_sum, o_rdy, o_out = (
            [sem("y_in0"), sem("y_in1")], sem("f_sum"), sem("o_rdy"), [sem("o_out0"), sem("o_out1")])

        block = stack.enter_context(nc.Block())

        N_NORMS, H_PIECES = NTOK + NCTX, 24
        C_U, H_U, M_U = 6, 12, 6
        U_H = HEADS * C_U
        U_M = U_H + HEADS * H_U
        S_W = U_M + KT * 4
        C_TILES = ("ff", "fb", "i")
        H_TILES = ("q", "ff", "i", "fb", "og", "p")

        def split_value(s):
            return SLOTS + s + 1

        E_BASE = [16 * (U_M // SLOTS + KT + 8)] * 4 + [16 * (U_M // SLOTS + KT)] * 2 + [0] * 2

        def unit_value(s):
            return 2 + s + 1

        @block.sync
        def _(sp):
            sp.dma_start(ident[:], consts[:, 0:P]).then_inc(consts_in, 16)
            sp.dma_start(upper[:], consts[:, P:2 * P]).then_inc(consts_in, 16)
            sp.dma_start(iota_e[:], consts[:, 2 * P:2 * P + E]).then_inc(consts_in, 16)
            sp.dma_start(tok_ids[:], consts[:, 2 * P + E:2 * P + E + NTOK]).then_inc(consts_in, 16)
            sp.dma_start(masks_in[:], level_masks).then_inc(consts_in, 16)
            for v, r in ((c.rearrange("a (r n) -> (a r) n", n=P), V_C),
                         (c_ctx.rearrange("(r n) -> r n", n=P), V_CC),
                         (norm1_w.rearrange("a (r n) -> (a r) n", n=P), V_N1),
                         (b_ada[:, 0:2 * D].rearrange("a (r n) -> (a r) n", n=P), V_B),
                         (pool_scale.rearrange("a (r n) -> (a r) n", n=P), V_PS),
                         (hg_norm_w.rearrange("a (r n) -> (a r) n", n=P), V_HG),
                         (lb_logits.rearrange("z a (r n) -> (z a r) n", n=P), V_LB)):
                sp.dma_start(vec_rows[r:r + v.shape[0], :], v).then_inc(vec_in, 16)

            def load_x(n):
                if n >= 3:
                    sp.wait_ge(x_T, n - 2)
                src = ctx_d[n] if n < NCTX else x_d[n - NCTX]
                sp.dma_start(x_tok[:, n % 3, :], src).then_inc(x_in[n % 3], 16)

            def load_ada(k):
                if k >= 4:
                    sp.wait_ge(ada_mm, k - 3)
                sp.dma_start(ada_ring[:, k % 4, :], w_ada_d[:, k, 0:2 * D]).then_inc(ada_in[k % 4], 16)

            for n in range(3):
                load_x(n)
            for k in range(2):
                load_ada(k)
            for n in range(3, NTOK + NCTX):
                load_x(n)
            for k in range(2, KT):
                load_ada(k)

            def load_unit(slot, src):
                sp.sem_inc(sp_own, 1)
                sp.dma_start(raw[:, slot, :].rearrange("p (k n) -> p k n", k=src.shape[1]), src
                             ).then_inc(raw_in[slot], 16)

            with sp.Fori(0, HEADS) as h:
                for u in range(C_U):
                    col = COL[C_TILES[u // 2]]
                    sp.wait_ge(split_done, h * C_U + u + 1)
                    load_unit(u, w_in_d[:, 8 * (u % 2):8 * (u % 2) + 8, ds(h * P + col, P)])
            with sp.Fori(0, HEADS) as h:
                for u in range(H_U):
                    col = COL[H_TILES[u // 2]]
                    sp.wait_ge(split_done, h * H_U + (U_H + u + 1))
                    load_unit(u % SLOTS, w_in_d[:, 8 * (u % 2):8 * (u % 2) + 8, ds(h * P + col, P)])
            with sp.Fori(0, KT) as j:
                for u in range(4):
                    col = COL["gp" if u < 2 else "gh"]
                    sp.wait_ge(split_done, j * 4 + (U_M + SLOTS - 4 + u + 1))
                    load_unit(u, w_in_d[:, 8 * (u % 2):8 * (u % 2) + 8, ds(j * P + col, P)])
                for u, w in ((4, w_bp_d), (5, w_bh_d)):
                    sp.wait_ge(split_done, SLOTS + U_M)
                    sp.wait_ge(branch_free, j * 2 + (u - 3))
                    load_unit(u, w[:, 0:8, ds(j * P, P)])
            with sp.Fori(0, 4) as cb:
                for u in range(8):
                    sp.wait_ge(split_done, cb * 8 + (SLOTS + S_W - 4 + u + 1))
                    load_unit(u % 4, w_out_d[:, 2 * u:2 * u + 2, ds(cb * 512, 512)])

            sp.wait_ge(units_done, 2 + S_W + 32)

            def load_e(g, slot, src):
                sp.wait_ge(e_split, g + 1)
                sp.sem_inc(sp_own, 1)
                sp.dma_start(e_raw[:, slot, :].rearrange("p (k n) -> p k n", k=src.shape[1]), src
                             ).then_inc(e_in[slot], 16)

            def w13(w, e, q):
                return w[ds(e, 1), :, 2 * q:2 * q + 2, :].rearrange("o p k n -> (o p) k n")

            def w2(e, q):
                return w_e2_d[ds(e, 1), :, q // 2:q // 2 + 1, 1024 * (q % 2):1024 * (q % 2) + 1024
                              ].rearrange("o p k n -> (o p) k n")

            for q in range(16):
                load_e(q, q % 8, w13(w_e1_d if q < 8 else w_e3_d, 0, q % 8))
            with sp.Fori(1, E) as e:
                for q in range(24):
                    src = w13(w_e1_d, e, q) if q < 8 else w13(w_e3_d, e, q - 8) if q < 16 else w2(e - 1, q - 16)
                    load_e(e * 24 + (q - 8), q % 8, src)
            for q in range(8):
                load_e(E * 24 - 8 + q, q, w2(E - 1, q))
            sp.wait_ge(table_rdy, 1)
            n_extra = sp.value_load(route_i[0:1, 7:8], min_val=0, max_val=NXTRA)
            with sp.Fori(0, NXTRA) as b:
                with sp.If(b < n_extra):
                    e = sp.value_load(route_i[0:1, ds(b, 1)], min_val=0, max_val=E - 1)
                    for q in range(24):
                        src = w13(w_e1_d, e, q) if q < 8 else w13(w_e3_d, e, q - 8) if q < 16 else w2(e, q - 16)
                        load_e(b * 24 + (E * 24 + q), q % 8, src)
                sp.nop()

            for i in range(NTOK):
                sp.wait_ge(o_rdy, i + 1)
                sp.dma_start(out_d[i], o_sb[:, i % 2, :]).then_inc(o_out[i % 2], 16)
            for i in range(2):
                sp.wait_ge(o_out[i], 16 * NTOK // 2)

        @block.tensor
        def _(pe):
            mm = pe.matmul
            pe.sem_inc(units_done, 2)
            pe.sem_inc(branch_free, 2)
            pe.sem_inc(e_units, 4)
            for s in (u_mm[0], u_mm[1], o_mm[0], row_mm):
                pe.sem_inc(s, 1)

            pe.wait_ge(consts_in, 80)
            pe.wait_ge(vec_in, 7 * 16)
            pe.transpose(bank(BD, V_ROWS), vec_rows[0:V_ROWS, :], ident[0:V_ROWS, 0:V_ROWS]).then_inc(vec_T, 1)
            for n in range(NTOK + NCTX):
                pe.wait_ge(xn_rdy, n + 1)
                for g in range(4):
                    b = (n % 2) * 4 + g
                    if n == 0 and b == BD or n == 1 and g == 0:
                        pe.wait_ge(vecT_rdy, 1)
                    if n >= 2:
                        pe.wait_ge(xT_act if g % 2 == 0 else xT_dve, 2 * (n - 2) + g // 2 + 1)
                    for j in range(4):
                        last = pe.transpose(ps[:, b, j * P:(j + 1) * P],
                                            x_tok[:, n % 3, (4 * g + j) * P:(4 * g + j + 1) * P], ident[:])
                last.then_inc(x_T, 1)
            pe.wait_ge(cs_rdy, 1)
            pe.wait_ge(xT_act, 2 * (NTOK + NCTX))
            pe.wait_ge(xT_dve, 2 * (NTOK + NCTX))
            for k in range(KT):
                pe.wait_ge(ada_in[k % 4], 16 * (k // 4 + 1))
                for b in range(8):
                    last = mm(ps[0:2, b, :], cs[:, :, k], ada_ring[:, k % 4, b * 512:(b + 1) * 512],
                              start=(k == 0), stop=(k == KT - 1))
                last.then_inc(ada_mm, 1)
            pe.wait_ge(mod_act, 4)
            pe.wait_ge(mod_dve, 4)
            for j in range(2 * KT):
                last = pe.transpose(ps[:, 0, 2 * j:2 * j + 2], mod01_row[0:2, j * P:(j + 1) * P], ident[0:2, 0:2])
            last.then_inc(mod_T, 1)
            pe.wait_ge(mod_T, 1)
            pe.sem_inc(split_done, SLOTS)

            def unit(s, slot, half, rhs_hi, rhs_lo, dst):
                pe.wait_ge(split_done, split_value(s))
                for kk in range(8):
                    k = 8 * half + kk
                    hi, lo = (w[:, slot, kk * P:(kk + 1) * P] for w in (w_hi, w_lo))
                    mm(dst, hi, rhs_hi[:, k, :], start=(k == 0), stop=False)
                    mm(dst, hi, rhs_lo[:, k, :], start=False, stop=False)
                    last = mm(dst, lo, rhs_hi[:, k, :], start=False, stop=(k == KT - 1))
                last.then_inc(units_done, 1)

            pe.wait_ge(h_split, 24)

            def ctx_scan(h, own, lag):
                hd = h - 1
                for u in range(C_U if own else 4):
                    if own:
                        if lag and u % 2 == 0:
                            pe.wait_ge((c_sig_f, c_sig_b, c_v_ev)[u // 2], h)
                        unit(h * C_U + u, u % 2, u % 2, hc_hi, hc_lo, bank((ZA, ZB, BF)[u // 2], CTX))
                    if lag and u == 1:
                        pe.wait_ge(c_v_ev, hd + 1)
                        for t in range(NCTX):
                            last = pe.transpose(ps[:, TR, t * P:(t + 1) * P], c_vT[:, t * P:(t + 1) * P], ident[:])
                        last.then_inc(c_v_T, 1)
                        pe.wait_ge(c_kg_f, hd + 1)
                        pe.wait_ge(c_kg_b, hd + 1)
                        for z in range(2):
                            for t in range(NCTX):
                                o = (z * NCTX + t) * P
                                last = pe.transpose(ps[:, UB, o:o + P], c_kg[:, z, t * P:(t + 1) * P], ident[:])
                        last.then_inc(c_kg_T, 1)
                    if lag and u == 3:
                        pe.wait_ge(c_v_rdy, hd + 1)
                        pe.wait_ge(c_kgT_rdy, hd + 1)
                        pe.wait_ge(ctx_state, hd + 1)
                        for z in range(2):
                            for t in range(NCTX):
                                last = mm(ps[:, OB, z * P:(z + 1) * P], c_kgT[:, z, t, :], c_v[:, t, :],
                                          start=(t == 0), stop=(t == NCTX - 1))
                        last.then_inc(c_s_mm, 1)

            ctx_scan(0, True, False)
            with pe.Fori(1, HEADS) as h:
                ctx_scan(h, True, True)
            ctx_scan(HEADS, False, True)

            def level(z, hd, idx):
                Bk = BD if idx == 0 else (BF, BB)[z]
                lhs, rhs = KG[z], (q_sb if idx == 0 else QF[z])
                if idx >= 2:
                    pe.wait_ge(lv_up[z], hd * LEVELS + (idx - 1))
                    pe.wait_ge(lv_sel[z], hd * 8 + idx)
                for ch in range(NCH):
                    last = mm(ps[:, Bk, ch * P:(ch + 1) * P], lhs[:, ch * P:(ch + 1) * P],
                              rhs[:, ch * P:(ch + 1) * P], start=True, stop=True)
                last.then_inc(lv_mm[z], 1)

            def turn_kg(z, hd):
                pe.wait_ge(lv_up[z], hd * LEVELS + LEVELS)
                for t in range(NCH - 1):
                    ch = t if z == 0 else t + 1
                    last = pe.transpose(ps[:, TR, t * P:(t + 1) * P], KG[z][:, ch * P:(ch + 1) * P], ident[:])
                last.then_inc(kg_T[z], 1)

            def chunk_sums(z, hd):
                pe.wait_ge(kgT_rdy[z], hd + 1)
                for t in range(NCH - 1):
                    ch = t if z == 0 else t + 1
                    last = mm(ps[:, UB, t * P:(t + 1) * P], kgT[z][:, t, :], v_sb[:, ch, :], start=True, stop=True)
                last.then_inc(u_mm[z], 1)

            def outputs(z, hd):
                pe.wait_ge(s_rdy[z], hd + 1)
                pe.wait_ge(lv_sel[z], hd * 8 + 8)
                for ch in range(NCH):
                    o = ps[:, OB, ch * P:(ch + 1) * P]
                    mm(o, v_sb[:, ch, :], A[z][:, ch, :], start=(z == 0 and ch == 0), stop=False,
                       skip_group_check=True)
                    last = mm(o, S[z][:, ch, :], QF[z][:, ch * P:(ch + 1) * P], start=False,
                              stop=(z == 1 and ch == NCH - 1), skip_group_check=True)
                last.then_inc(o_mm[z], 1)

            pe.wait_ge(ctx_state, HEADS + 1)

            def lat_scan(h, own, lag):
                hd = h - 1
                for u in range(H_U if own else 8):
                    if own:
                        if lag and u % 2 == 0:
                            pe.wait_ge(*((gate_rdy, h), (p_ev, h), (q_rdy, h + 1), (f_rdy, h + 1), (v_ev, h + 1),
                                         (sig_bw, h + 1))[u // 2])
                        elif u % 2 == 0 and u >= 4:
                            pe.wait_ge(*((q_rdy, h + 1), (f_rdy, h + 1), (v_ev, h + 1), (sig_bw, h + 1))[u // 2 - 2])
                        unit(h * H_U + (U_H + u), u % 2, u % 2, hl_hi, hl_lo, bank((ZA, ZB)[u // 2 % 2]))
                        if u == 4:
                            pe.wait_ge(f_rdy, h + 1)
                            if lag:
                                pe.wait_ge(lv_sel[1], hd * 8 + 1)
                            level(0, h, 0)
                            if lag:
                                pe.wait_ge(lv_sel[0], h * 8)
                            level(0, h, 1)
                        if 5 <= u <= 10:
                            level(0, h, u - 3)
                        if u == 7:
                            pe.wait_ge(v_ev, h + 1)
                            if lag:
                                pe.wait_ge(kgT_rdy[1], h)
                            for t in range(NCH):
                                last = pe.transpose(ps[:, TR, t * P:(t + 1) * P], vT_sb[:, t * P:(t + 1) * P],
                                                    ident[:])
                            last.then_inc(v_T, 1)
                        if u == 8:
                            pe.wait_ge(fb_rdy, h + 1)
                            pe.wait_ge(lv_sel[0], h * 8 + 1)
                            level(1, h, 0)
                            if lag:
                                pe.wait_ge(lv_sel[1], h * 8)
                            level(1, h, 1)
                        if 9 <= u <= 11:
                            level(1, h, u - 7)
                        if u == 11:
                            pe.wait_ge(v_rdy, h + 1)
                            turn_kg(0, h)
                    if lag:
                        if u <= 2:
                            level(1, hd, u + 5)
                        if u == 1:
                            pe.wait_ge(hg_rdy, hd + 1)
                            chunk_sums(0, hd)
                        if u == 2:
                            outputs(0, hd)
                        if u == 3:
                            pe.wait_ge(kgT_rdy[0], hd + 1)
                            turn_kg(1, hd)
                        if u == 4:
                            pe.wait_ge(s_rdy[0], hd + 1)
                            chunk_sums(1, hd)
                        if u == 5:
                            outputs(1, hd)
                        if u == 7:
                            pe.wait_ge(osq_rdy, hd + 1)
                            pe.wait_ge(s_rdy[1], hd + 1)
                            mm(bank(UB), ones[:], osq[:], start=True, stop=True).then_inc(n_mm, 1)

            lat_scan(0, True, False)
            with pe.Fori(1, HEADS) as h:
                lat_scan(h, True, True)
            lat_scan(HEADS, False, True)

            pe.wait_ge(pool_rdy, HEADS)
            pe.wait_ge(coef_in, 16 * (HEADS + 1))
            pe.wait_ge(lv_sel[1], HEADS * 8)
            pe.wait_ge(gate_rdy, HEADS)
            pe.wait_ge(p_ev, HEADS)
            for t in range(HEADS):
                g, half = t // 2, t % 2
                if t >= 2:
                    pe.wait_ge(pg_ev, t - 1)
                for k in range(2):
                    last = mm(bank((BF, BB)[t % 2]), w_pg[:, g, k, half * P:(half + 1) * P], delta[:, 2 * g + k, :],
                              start=(k == 0), stop=(k == 1))
                last.then_inc(pg_mm, 1)
            pe.wait_ge(pg_ev, HEADS)
            pe.wait_ge(hgw_rdy, 1)

            with pe.Fori(0, KT) as j:
                pe.wait_ge(gp_rdy, j + 1)
                for u in range(4):
                    if u == 2:
                        pe.wait_ge(gh_rdy, j + 1)
                    unit(j * 4 + (U_M + u), u % 2, u % 2, hl_hi, hl_lo, bank((ZA, ZB)[u // 2]))
                pe.wait_ge(m_rdy, j + 1)
                for u, src, b in ((4, poolT, BF), (5, hg, BB)):
                    pe.wait_ge(raw_in[u], j * 16 + 16 * (U_M // SLOTS + 1))
                    for k in range(8):
                        last = mm(bank(b), raw[:, u, k * P:(k + 1) * P], src[:, k, :], start=(k == 0), stop=(k == 7))
                    last.then_inc(branch_free, 1)
                pe.wait_ge(ada2_free, j * 4 + 6)
                pe.wait_ge(row_rdy, j + 1)
                mm(ps[0:1, UB, :], ones[:, 0:1], acc[:], start=True, stop=True).then_inc(row_mm, 1)

            pe.wait_ge(m_rdy, KT + 1)
            pe.wait_ge(h_split, H_PIECES + 8)
            with pe.Fori(0, 4) as cb:
                for u in range(8):
                    s = cb * 8 + (S_W + u)
                    pe.wait_ge(split_done, split_value(s))
                    for t in range(NTOK):
                        if u == 0:
                            pe.wait_ge(w_ev, cb * 4 + (t + 1))
                        for kk in range(2):
                            k = 2 * u + kk
                            hi, lo = (w[:, u % 2, kk * 512:(kk + 1) * 512] for w in (w_hi, w_lo))
                            a_hi, a_lo = (m[:, k, t * P:(t + 1) * P] for m in (m_hi, m_lo))
                            mm(bank(t), a_hi, hi, start=(k == 0), stop=False)
                            mm(bank(t), a_hi, lo, start=False, stop=False)
                            last = mm(bank(t), a_lo, hi, start=False, stop=(k == KT - 1))
                    last.then_inc(units_done, 1)

            for k in range(KT):
                if k == 0:
                    pe.wait_ge(w_ev, 20)
                    pe.wait_ge(h2_rdy, NTOK)
                if k >= 2:
                    pe.wait_ge(h2T_ev, k - 1)
                for t in range(NTOK):
                    last = pe.transpose(ps[:, 4 + k % 2, t * P:(t + 1) * P], h2[:, t, k * P:(k + 1) * P], ident[:])
                last.then_inc(h2_T, 1)
            pe.wait_ge(rows_in, 5 * 16)
            for t in range(NTOK):
                for k in range(KT):
                    if t == 0:
                        pe.wait_ge(h2T_ev, k + 1)
                    last = mm(ps[:, 0, t * E:(t + 1) * E], h2T[:, k, t * P:(t + 1) * P], w_r[:, k, :],
                              start=(k == 0), stop=(k == KT - 1))
            last.then_inc(lg_mm, 1)
            pe.wait_ge(sel_rdy, 1)
            chosen = rt[:, 8, :].rearrange("p (t e) -> p t e", e=E)
            for t in range(NTOK):
                for s in range(t + 1):
                    mm(ps[:, 1, t * E:(t + 1) * E], upper[:] if s == t else ones[:], chosen[:, s, :],
                       start=(s == 0), stop=(s == t))
            for s in range(NTOK):
                last = mm(ps[:, 2, 0:E], ones[:], chosen[:, s, :], start=(s == 0), stop=(s == NTOK - 1))
            last.then_inc(pos_mm, 1)
            pe.wait_ge(tab_in, 16)
            pe.transpose(ps[:, 3, 0:NBLK], table_rows[0:NBLK, :], ident[0:NBLK, 0:NBLK]).then_inc(tab_T, 1)
            pe.wait_ge(table_rdy, 1)

            def e_unit(g, slot, parts):
                pe.wait_ge(e_split, g + 9)
                for b, n, a_hi, a_lo, start, stop in parts:
                    hi, lo = (w[:, slot, n * 512:(n + 1) * 512] for w in (e_hi, e_lo))
                    mm(bank(b), a_hi, hi, start=start, stop=False)
                    mm(bank(b), a_hi, lo, start=False, stop=False)
                    last = mm(bank(b), a_lo, hi, start=False, stop=stop)
                last.then_inc(e_units, 1)

            def up_unit(g, q, b):
                e_unit(g, q % 4, [(b, kk, xe_hi[:, 2 * q + kk, :], xe_lo[:, 2 * q + kk, :],
                                   2 * q + kk == 0, 2 * q + kk == KT - 1) for kk in range(2)])

            def down_unit(g, q):
                k = q // 2
                e_unit(g, q % 4, [(2 + 2 * (q % 2) + n, n, actT_hi[:, k, :], actT_lo[:, k, :], k == 0, k == 3)
                                  for n in range(2)])

            def turn_x(b, part):
                if part == 0:
                    pe.wait_ge(xe_in, b * 16 + 16)
                pe.wait_ge(xe_rdy, b * 4 + (part + 1))
                pe.wait_ge(actT_rdy, b + 1)
                for j in range(4):
                    last = pe.transpose(ps[:, 6 + part % 2, j * P:(j + 1) * P],
                                        xe[:, (4 * part + j) * P:(4 * part + j + 1) * P], ident[:])
                last.then_inc(xe_T, 1)

            def turn_act(b):
                pe.wait_ge(act_rdy, b + 1)
                for j in range(4):
                    last = pe.transpose(ps[:, 6, j * P:(j + 1) * P], act[:, j * P:(j + 1) * P], ident[:])
                last.then_inc(act_T, 1)

            def x_ready(b):
                pe.wait_ge(xe_rdy, b * 4 + 6)

            for part in range(4):
                turn_x(0, part)
            x_ready(0)
            for q in range(16):
                up_unit(q, q % 8, q // 8)
            for part in range(4):
                if part == 0:
                    pe.wait_ge(e_units, 4 + 16)
                turn_x(1, part)
            with pe.Fori(1, E) as e:
                x_ready(e)
                for q in range(24):
                    g = e * 24 + (q - 8)
                    if q == 0:
                        pe.wait_ge(u_rdy, e)
                    if q == 8:
                        pe.wait_ge(act_rdy, e)
                    if q == 16:
                        pe.wait_ge(actT_rdy, e + 2)
                        pe.wait_ge(y_ev, e * 4)
                    if q < 16:
                        up_unit(g, q % 8, q // 8)
                    else:
                        down_unit(g, q - 16)
                    if q == 2:
                        turn_act(e - 1)
                    if 17 <= q <= 20:
                        turn_x(e + 1, q - 17)
            x_ready(E)
            turn_act(E - 1)
            pe.wait_ge(actT_rdy, E + 2)
            pe.wait_ge(y_ev, 4 * E)
            for q in range(8):
                down_unit(E * 24 - 8 + q, q)
            n_extra = pe.value_load(route_i[0:1, 7:8], min_val=0, max_val=NXTRA)
            with pe.Fori(0, NXTRA) as b:
                with pe.If(b < n_extra):
                    for part in range(4):
                        turn_x(b + (E + 1), part)
                    x_ready(b + (E + 1))
                    pe.wait_ge(u_rdy, b + E)
                    pe.wait_ge(act_rdy, b + E)
                    for q in range(16):
                        up_unit(b * 24 + (E * 24 + q), q % 8, q // 8)
                    turn_act(b + E)
                    pe.wait_ge(actT_rdy, b + (E + 3))
                    pe.wait_ge(y_ev, b * 4 + 4 * (E + 1))
                    for q in range(8):
                        down_unit(b * 24 + (E * 24 + 16 + q), q)
                pe.nop()

        @block.scalar
        def _(act_e):
            own = Chain(act_e, a_own)
            activate = act_e.activation
            act_e.sem_inc(gp_rdy, 1)
            act_e.sem_inc(gh_rdy, 1)
            act_e.sem_inc(y_ev, 4)

            act_e.wait_ge(vecT_rdy, 1)
            activate(cs[:], vecT[:, 0:2 * KT].rearrange("p (z k) -> p z k", z=2), ACT.Sigmoid).then_inc(c_sg, 1)
            act_e.wait_ge(lb_in, 1)
            activate(lb_tmp[:, 1, :], lb_tmp[:, 0, :], ACT.Exp).then_inc(lb_exp, 1)
            for n in range(NTOK + NCTX):
                act_e.wait_ge(x_in[n % 3], 16 * (n // 3 + 1))
                own.wait()
                own.did(activate(square_junk[:], x_tok[:, n % 3, :], ACT.Square, accum_out=stat[:, 0, n:n + 1]))
                own.wait()
                act_e.nop().then_inc(ssq_rdy, 1)
                act_e.wait_ge(var_rdy, n + 1)
                activate(stat[:, 2, n:n + 1], stat[:, 1, n:n + 1], ACT.Sqrt).then_inc(std_rdy, 1)
                act_e.wait_ge(x_T, n + 1)
                for g in (0, 2):
                    dst = xT_ctx[:, 4 * g:4 * g + 4, n * P:(n + 1) * P] if n < NCTX else \
                        xT_lat[:, 4 * g:4 * g + 4, (n - NCTX) * P:(n - NCTX + 1) * P]
                    act_e.copy(dst, bank((n % 2) * 4 + g).rearrange("p (j t) -> p j t", j=4)).then_inc(xT_act, 1)
            act_e.wait_ge(ada_mm, KT)
            for b in range(0, 8, 2):
                act_e.copy(mod01_row[0:2, b * 512:(b + 1) * 512], ps[0:2, b, :]).then_inc(mod_act, 1)
            for n in range(24):
                act_e.wait_ge(h_rdy, n + 1)
                if n < 8:
                    dst, src = hc_hi[:, 2 * n:2 * n + 2, :], xT_ctx[:, 2 * n:2 * n + 2, :]
                else:
                    dst, src = hl_hi[:, n - 8:n - 7, :], xT_lat[:, n - 8:n - 7, :]
                act_e.copy(dst, src).then_inc(h_hi, 1)

            def hi(s, slot, hslot, uses):
                act_e.wait_ge(raw_in[slot], uses)
                act_e.wait_ge(units_done, s + 1)
                act_e.copy(w_hi[:, hslot, :], raw[:, slot, :]).then_inc(hi_done, 1)

            act_e.wait_ge(split_done, SLOTS)
            hi(0, 0, 0, 16)

            def ctx_scan(h, main, lag):
                hd = h - 1
                for u in range(C_U if main else 4):
                    if main:
                        hi(h * C_U + (u + 1), (u + 1) % SLOTS, (u + 1) % 2, h * 16 + 16 * ((u + 1) // SLOTS + 1))
                        done = h * C_U + (2 + u + 1)
                        if u == 1:
                            act_e.wait_ge(units_done, done)
                            if lag:
                                act_e.wait_ge(c_kg_f, h)
                            activate(c_sig[:, 0, :], bank(ZA, CTX), ACT.Sigmoid).then_inc(c_sig_f, 1)
                        if u == 3:
                            act_e.wait_ge(units_done, done)
                            if lag:
                                act_e.wait_ge(c_kg_b, h)
                            activate(c_sig[:, 1, :], bank(ZB, CTX), ACT.Sigmoid).then_inc(c_sig_b, 1)
                        if u == 5:
                            act_e.wait_ge(units_done, done)
                            if lag:
                                act_e.wait_ge(c_v_T, h)
                            act_e.copy(c_vT[:], bank(BF, CTX)).then_inc(c_v_ev, 1)
                    if lag and u == 2:
                        act_e.wait_ge(ctx_state, hd + 1)
                        act_e.wait_ge(c_v_T, hd + 1)
                        act_e.copy(c_v[:].rearrange("p t v -> p (t v)"), bank(TR, CTX)).then_inc(c_v_rdy, 1)
                        act_e.wait_ge(c_kg_T, hd + 1)
                        act_e.copy(c_kgT[:].rearrange("p z t k -> p (z t k)"), bank(UB)).then_inc(c_kgT_rdy, 1)

            ctx_scan(0, True, False)
            with act_e.Fori(1, HEADS) as h:
                ctx_scan(h, True, True)
            ctx_scan(HEADS, False, True)

            act_e.wait_ge(ctx_state, HEADS + 1)
            act_e.wait_ge(pad_rdy, 1)

            def kgT_copy(z, hd):
                act_e.wait_ge(kg_T[z], hd + 1)
                act_e.wait_ge(u_mm[z], hd + 1)
                act_e.copy(kgT[z][:].rearrange("p t k -> p (t k)"), bank(TR, (NCH - 1) * P)).then_inc(kgT_rdy[z], 1)

            def lat_scan(h, main, lag):
                hd = h - 1
                for u in range(H_U if main else 9):
                    if main:
                        hi(h * H_U + (U_H + u + 1), (u + 1) % SLOTS, (u + 1) % 2,
                           h * 32 + 16 * (U_H // SLOTS + (u + 1) // SLOTS + 1))
                        done = h * H_U + (2 + U_H + u + 1)
                        if u == 1:
                            act_e.wait_ge(units_done, done)
                            if lag:
                                act_e.wait_ge(gate_rdy, h)
                            activate(sig_a[:], bank(ZA), ACT.Sigmoid).then_inc(sig_q, 1)
                        if u == 3:
                            act_e.wait_ge(units_done, done)
                            act_e.wait_ge(q_rdy, h + 1)
                            activate(sig_a[:], bank(ZB), ACT.Sigmoid).then_inc(sig_f, 1)
                        if u == 5:
                            act_e.wait_ge(units_done, done)
                            if lag:
                                act_e.wait_ge(v_T, h)
                            act_e.copy(vT_sb[:], bank(ZA)).then_inc(v_ev, 1)
                        if u == 7:
                            act_e.wait_ge(units_done, done)
                            if lag:
                                act_e.wait_ge(fb_rdy, h)
                            activate(sig_b[:], bank(ZB), ACT.Sigmoid).then_inc(sig_bw, 1)
                            act_e.wait_ge(v_T, h + 1)
                            if lag:
                                act_e.wait_ge(o_mm[1], h)
                            act_e.copy(v_sb[:].rearrange("p t v -> p (t v)"), bank(TR)).then_inc(v_rdy, 1)
                        if u == 9:
                            act_e.wait_ge(units_done, done)
                            act_e.wait_ge(f_rdy, h + 1)
                            activate(sig_a[:], bank(ZA), ACT.Sigmoid).then_inc(sig_og, 1)
                        if u == 11:
                            act_e.wait_ge(units_done, done)
                            if lag:
                                act_e.wait_ge(pool_rdy, h)
                            act_e.copy(up[:, :, HALO:HALO + GRID_W], bank(ZB).rearrange("p (r w) -> p r w", w=GRID_W)
                                       ).then_inc(p_ev, 1)
                    if lag:
                        if u == 0:
                            kgT_copy(0, hd)
                        if u == 3:
                            kgT_copy(1, hd)
                        if u == 5:
                            act_e.wait_ge(o_mm[1], hd + 1)
                            act_e.wait_ge(hg_rdy, hd + 1)
                            activate(osq[:], bank(OB), ACT.Square).then_inc(osq_rdy, 1)
                        if u == 8:
                            act_e.wait_ge(nv_rdy, hd + 1)
                            activate(osq[:], osq[:], ACT.Sqrt).then_inc(rt_rdy, 1)

            lat_scan(0, True, False)
            with act_e.Fori(1, HEADS) as h:
                lat_scan(h, True, True)
            lat_scan(HEADS, False, True)

            for t in range(HEADS):
                act_e.wait_ge(pg_mm, t + 1)
                activate(poolT[:, t, :], bank((BF, BB)[t % 2]), ACT.Copy, scale=vecT[:, V_PS + t:V_PS + t + 1]
                         ).then_inc(pg_ev, 1)

            with act_e.Fori(0, KT) as j:
                for u in range(4):
                    nxt = u + 1
                    slot = nxt if nxt < 4 else 0
                    hi(j * 4 + (U_M + nxt), slot, nxt % 2, j * 16 + 16 * (U_M // SLOTS + 1 + (nxt == 4)))
                    done = j * 4 + (2 + U_M + u + 1)
                    if u == 1:
                        act_e.wait_ge(units_done, done)
                        act_e.wait_ge(pp_rdy, j + 1)
                        activate(sig_gp[:], bank(ZA), ACT.Sigmoid).then_inc(gp_rdy, 1)
                    if u == 3:
                        act_e.wait_ge(units_done, done)
                        act_e.wait_ge(m_rdy, j + 1)
                        activate(sig_gh[:], bank(ZB), ACT.Sigmoid).then_inc(gh_rdy, 1)

            act_e.wait_ge(units_done, 2 + S_W)
            act_e.wait_ge(m_rdy, KT + 1)
            for n in range(8):
                act_e.copy(m_hi[:, 2 * n:2 * n + 2, :], m_sb[:, 2 * n:2 * n + 2, :]).then_inc(h_hi, 1)

            def out_hi(cb, last):
                for u in range(7 if last else 8):
                    nxt = u + 1
                    hi(cb * 8 + (S_W + nxt), nxt % 4, nxt % 2,
                       cb * 32 + 16 * ((U_M + 6 * KT) // SLOTS + nxt // 4 + 1))

            with act_e.Fori(0, 3) as cb:
                out_hi(cb, False)
            out_hi(3, True)

            act_e.wait_ge(x2_rdy, 20)
            act_e.wait_ge(units_done, 2 + S_W + 32)
            for t in range(NTOK):
                own.wait()
                own.did(activate(junk2[:], x2[:, t, :], ACT.Square, accum_out=stat2[:, 0, t:t + 1]))
            own.wait()
            act_e.nop().then_inc(ssq_rdy, 1)
            act_e.wait_ge(var_rdy, N_NORMS + 1)
            activate(stat2[:, 2, :], stat2[:, 1, :], ACT.Sqrt).then_inc(std_rdy, 1)
            for k in range(0, KT, 2):
                act_e.wait_ge(h2_T, k + 1)
                if k:
                    act_e.wait_ge(h2T_ev, k)
                act_e.copy(h2T[:, k, :], bank(4 + k % 2)).then_inc(h2T_ev, 1)
            act_e.wait_ge(lg_mm, 1)
            activate(rt[:, 0, :], bank(0, NTOK * E), ACT.Sigmoid).then_inc(score_rdy, 1)

            def e_hi_unit(g, slot, hslot, uses):
                act_e.wait_ge(e_in[slot], uses + E_BASE[slot])
                act_e.wait_ge(e_units, g + 1)
                act_e.copy(e_hi[:, hslot, :], e_raw[:, slot, :]).then_inc(e_hi_done, 1)

            def x_hi(b, part):
                act_e.wait_ge(xe_T, b * 4 + (part + 1))
                act_e.copy(xe_hi[:, 4 * part:4 * part + 4, :].rearrange("p k t -> p (k t)"), bank(6 + part % 2)
                           ).then_inc(xe_hi_rdy, 1)

            def sig1(b):
                act_e.wait_ge(u_rdy, b)
                activate(act_sig[:], bank(0), ACT.Sigmoid).then_inc(sg_rdy, 1)

            def act_hi(b):
                act_e.wait_ge(act_T, b + 1)
                act_e.copy(actT_hi[:].rearrange("p k t -> p (k t)"), bank(6)).then_inc(actT_hi_rdy, 1)

            def y_copy(b, units):
                act_e.wait_ge(e_units, units)
                act_e.wait_ge(y_out, b * 16 + 16 * NTOK)
                for part in range(4):
                    act_e.copy(y_sb[:, part * 512:(part + 1) * 512], bank(2 + part)).then_inc(y_ev, 1)

            AHEAD = 3
            act_e.wait_ge(table_rdy, 1)
            for q in range(AHEAD):
                e_hi_unit(q, q, q, 16)
            for part in range(4):
                x_hi(0, part)
            for q in range(16):
                n = q + AHEAD
                e_hi_unit(n, n % 8, n % 4, 16 * (n // 8 + 1))
                if q == 8:
                    act_e.wait_ge(e_units, 4 + 8)
                    activate(act_sig[:], bank(0), ACT.Sigmoid).then_inc(sg_rdy, 1)
            act_e.wait_ge(e_units, 4 + 16)
            for part in range(4):
                x_hi(1, part)
            with act_e.Fori(1, E) as e:
                for q in range(24):
                    n = q + AHEAD
                    e_hi_unit(e * 24 + (n - 8), n % 8, n % 4, e * 48 + 16 * (n // 8))
                    if q == 3:
                        act_hi(e - 1)
                    if q == 9:
                        act_e.wait_ge(e_units, e * 24 + 4)
                        sig1(e)
                    if q == 17:
                        act_e.wait_ge(e_units, e * 24 + 12)
                    if 18 <= q <= 21:
                        x_hi(e + 1, q - 18)
                y_copy(e - 1, e * 24 + 20)
            act_hi(E - 1)
            for q in range(AHEAD, 8):
                n = E * 24 - 8 + q
                e_hi_unit(n, n % 8, n % 4, 16 * (n // 8 + 1))
            y_copy(E - 1, E * 24 + 4)
            n_extra = act_e.value_load(route_i[0:1, 7:8], min_val=0, max_val=NXTRA)
            with act_e.Fori(0, NXTRA) as b:
                with act_e.If(b < n_extra):
                    for part in range(4):
                        x_hi(b + (E + 1), part)
                    for q in range(24):
                        e_hi_unit(b * 24 + (24 * E + q), q % 8, q % 4, b * 48 + 16 * (3 * E + q // 8 + 1))
                        if q == 10:
                            act_e.wait_ge(e_units, b * 24 + (24 * E + 12))
                            sig1(b + E)
                        if q == 16:
                            act_hi(b + E)
                    y_copy(b + E, b * 24 + (E * 24 + 28))
                act_e.nop()

            for i in range(NTOK):
                act_e.wait_ge(f_sum, i + 1)
                own.wait()
                own.did(activate(f_junk[:], o_sb[:, i % 2, :], ACT.Square, accum_out=stat2[:, 0, i:i + 1]))
                own.wait()
                act_e.nop().then_inc(ssq_rdy, 1)
                act_e.wait_ge(var_rdy, N_NORMS + 1 + i + 1)
                activate(stat2[:, 2, i:i + 1], stat2[:, 1, i:i + 1], ACT.Sqrt).then_inc(std_rdy, 1)

        @block.vector
        def _(dve):
            own = Chain(dve, v_own)
            tt, ts, stt = dve.tensor_tensor, dve.tensor_scalar, dve.scalar_tensor_tensor
            for s, n in ((ctx_state, 1), (hg_rdy, 1), (pp_rdy, 1), (m_rdy, 1), (row_rdy, 1), (ada2_free, 2),
                         (w_ev, 4), (x2_rdy, 4), (e_split, 8), (xe_rdy, 2), (actT_rdy, 2)):
                dve.sem_inc(s, n)

            own.did(dve.memset(ones[:], 1.0))
            dve.wait_ge(consts_in, 80)
            own.did(dve.tensor_copy(masks[:], masks_in[:]))
            dve.wait_ge(vec_T, 1)
            dve.tensor_copy(vecT[:], bank(BD, V_ROWS)).then_inc(vecT_rdy, 1)
            dve.wait_ge(vecT_rdy, 1)
            dve.wait_ge(c_sg, 1)
            tt(cs[:], vecT[:, 0:2 * KT].rearrange("p (z k) -> p z k", z=2), cs[:], ALU.mult).then_inc(cs_rdy, 1)
            lb = vecT[:, V_LB:V_LB + 16]
            tt(lb_tmp[:, 0, :], lb, lb, ALU.subtract).then_inc(lb_in, 1)
            dve.wait_ge(lb_exp, 1)
            own.did(dve.reciprocal(lb_tmp[:, 2, :], lb_tmp[:, 1, :]))
            own.wait()
            own.did(tt(lb_tmp[:, 3, :], lb_tmp[:, 1, :], lb_tmp[:, 2, :], ALU.mult))
            own.wait()
            prob = lb_tmp[:, 3, :].rearrange("p (z h) -> p z h", z=2)
            lbv = lb_all[:].rearrange("p h (z w) -> p w z h", z=2)
            own.did(tt(lbv[:, 0], prob, prob, ALU.subtract))
            own.wait()
            own.did(ts(lbv[:, 1], lbv[:, 0], -1.0, 1.0, ALU.mult, ALU.add))
            for n in range(NTOK + NCTX):
                dve.wait_ge(ssq_rdy, n + 1)
                ts(stat[:, 1, n:n + 1], stat[:, 0, n:n + 1], 1.0 / D, EPS, ALU.mult, ALU.add).then_inc(var_rdy, 1)
                dve.wait_ge(std_rdy, n + 1)
                own.did(dve.reciprocal(stat[:, 3, n:n + 1], stat[:, 2, n:n + 1]))
                own.wait()
                ts(x_tok[:, n % 3, :], x_tok[:, n % 3, :], stat[:, 3, n:n + 1], None, ALU.mult).then_inc(xn_rdy, 1)
                dve.wait_ge(x_T, n + 1)
                for g in (1, 3):
                    dst = xT_ctx[:, 4 * g:4 * g + 4, n * P:(n + 1) * P] if n < NCTX else \
                        xT_lat[:, 4 * g:4 * g + 4, (n - NCTX) * P:(n - NCTX + 1) * P]
                    dve.tensor_copy(dst, bank((n % 2) * 4 + g).rearrange("p (j t) -> p j t", j=4)
                                    ).then_inc(xT_dve, 1)
            dve.wait_ge(ada_mm, KT)
            for b in range(1, 8, 2):
                dve.tensor_copy(mod01_row[0:2, b * 512:(b + 1) * 512], ps[0:2, b, :]).then_inc(mod_dve, 1)
            dve.wait_ge(mod_T, 1)
            own.did(tt(modT[:], ps[:, 0, 0:4 * KT].rearrange("p (j z) -> p j z", z=2),
                       vecT[:, V_B:V_B + 2 * KT].unsqueeze(2).to_broadcast([P, 2 * KT, 2]), ALU.add))
            own.wait()
            own.did(stt(out=scale1[:], in0=modT[:, KT:2 * KT, :], scalar=1.0,
                        in1=vecT[:, V_N1:V_N1 + KT].unsqueeze(2).to_broadcast([P, KT, 2]),
                        op0=ALU.add, op1=ALU.mult))
            own.wait()
            dve.wait_ge(xT_act, 2 * (NTOK + NCTX))
            dve.wait_ge(xT_dve, 2 * (NTOK + NCTX))

            def modulate(n):
                if n < 8:
                    for j in (2 * n, 2 * n + 1):
                        last = ts(xT_ctx[:, j, :], xT_ctx[:, j, :], scale1[:, j, 1:2], modT[:, j, 1:2],
                                  ALU.mult, ALU.add)
                else:
                    j = n - 8
                    last = ts(xT_lat[:, j, :], xT_lat[:, j, :], scale1[:, j, 0:1], modT[:, j, 0:1],
                              ALU.mult, ALU.add)
                last.then_inc(h_rdy, 1)

            modulate(0)
            for n in range(24):
                if n + 1 < 24:
                    modulate(n + 1)
                dve.wait_ge(h_hi, n + 1)
                if n < 8:
                    dst, hi_, src = (a[:, 2 * n:2 * n + 2, :] for a in (hc_lo, hc_hi, xT_ctx))
                else:
                    dst, hi_, src = (a[:, n - 8:n - 7, :] for a in (hl_lo, hl_hi, xT_lat))
                tt(dst, src, hi_.bitcast(F32), ALU.subtract).then_inc(h_split, 1)

            def lo(s, slot, hslot):
                dve.wait_ge(hi_done, s + 1)
                tt(w_lo[:, hslot, :], raw[:, slot, :], w_hi[:, hslot, :].bitcast(F32), ALU.subtract
                   ).then_inc(split_done, 1)

            lo(0, 0, 0)

            def ctx_scan(h, main, lag):
                hd = h - 1
                for u in range(C_U if main else 4):
                    if main:
                        lo(h * C_U + (u + 1), (u + 1) % SLOTS, (u + 1) % 2)
                        if u == 1:
                            own.wait()
                            own.did(dve.tensor_copy(lb_v[:], lb_all[:, ds(h, 1), :].rearrange("p o w -> p (o w)")))
                            own.wait()
                            dve.wait_ge(c_sig_f, h + 1)
                            if lag:
                                dve.wait_ge(c_kg_T, h)
                                dve.wait_ge(c_kg_f, h)
                            own.did(ts(c_f[:, 0, :], c_sig[:, 0, :], lb_v[:, 1:2], lb_v[:, 0:1], ALU.mult, ALU.add))
                            own.wait()
                            own.did(ts(c_kg[:, 0, :], c_f[:, 0, :], -1.0, 1.0, ALU.mult, ALU.add))
                            ctx_decays(dve, own, 0).then_inc(c_kg_f, 1)
                    if lag and u == 3:
                        dve.wait_ge(c_s_mm, hd + 1)
                        dve.tensor_copy(s_ctx[:, :, ds(hd, 1), :],
                                        bank(OB, 2 * P).rearrange("p (z o v) -> p z o v", z=2, o=1)
                                        ).then_inc(ctx_state, 1)

            ctx_scan(0, True, False)
            with dve.Fori(1, HEADS) as h:
                own.loop(h - 1, PER["ctx_v"])
                ctx_scan(h, True, True)
                own.end(HEADS - 1)
            ctx_scan(HEADS, False, True)

            def select(z, hd, idx):
                dve.wait_ge(lv_mm[z], hd * 8 + (idx + 1))
                if idx == 0:
                    tt(A[z][:], bank(BD).rearrange("p (c t) -> p c t", c=NCH),
                       ident[:].unsqueeze(1).to_broadcast([P, NCH, P]), ALU.mult).then_inc(lv_sel[z], 1)
                else:
                    dve.wait_ge(lv_sel[z], hd * 8 + idx)
                    own.pass_waits()
                    dve.copy_predicated(A[z][:], masks[:, z, idx - 1, :].unsqueeze(1).to_broadcast([P, NCH, P]),
                                        bank((BF, BB)[z]).rearrange("p (c t) -> p c t", c=NCH)
                                        ).then_inc(lv_sel[z], 1)

            def states(z, hd):
                order = range(NCH) if z == 0 else range(NCH - 1, -1, -1)
                dve.wait_ge(u_mm[z], hd + 2)
                if z == 0:
                    dve.wait_ge(o_mm[0], hd + 1)
                T_chunk = TT[z][:, T_AT[LEVELS]:T_AT[LEVELS] + NCH]
                prev = order[0]
                dve.wait_ge(ctx_state, HEADS + 1)
                own.did(dve.tensor_copy(S[z][:, prev, :], s_ctx[:, z, ds(hd, 1), :].rearrange("p o v -> p (o v)")))
                for n, ch in enumerate(order[1:]):
                    own.wait()
                    t = prev if z == 0 else prev - 1
                    ins = stt(out=S[z][:, ch, :], in0=S[z][:, prev, :], scalar=T_chunk[:, prev:prev + 1],
                              in1=ps[:, UB, t * P:(t + 1) * P], op0=ALU.mult, op1=ALU.add)
                    if n < NCH - 2:
                        own.did(ins)
                    else:
                        ins.then_inc(s_rdy[z], 1)
                    prev = ch

            def lat_scan(h, main, lag):
                hd = h - 1
                for u in range(H_U if main else 11):
                    if main:
                        lo(h * H_U + (U_H + u + 1), (u + 1) % SLOTS, (u + 1) % 2)
                        if u == 1:
                            dve.wait_ge(sig_q, h + 1)
                            if lag:
                                dve.wait_ge(fb_rdy, h)
                            tt(q_sb[:], bank(ZA), sig_a[:], ALU.mult).then_inc(q_rdy, 1)
                        if u == 3:
                            own.wait()
                            own.did(dve.tensor_copy(lb_v[:], lb_all[:, ds(h, 1), :].rearrange("p o w -> p (o w)")))
                            own.wait()
                            dve.wait_ge(sig_f, h + 1)
                            own.did(ts(f_sb[0][:], sig_a[:], lb_v[:, 1:2], lb_v[:, 0:1], ALU.mult, ALU.add))
                            if lag:
                                dve.wait_ge(o_mm[0], h + 1)
                                dve.wait_ge(lv_up[0], h * LEVELS)
                            own.wait()
                            own.did(ts(KG[0][:], f_sb[0][:], -1.0, 1.0, ALU.mult, ALU.add))
                            dve.wait_ge(q_rdy, h + 1)
                            tt(QF[0][:], q_sb[:], f_sb[0][:], ALU.mult).then_inc(f_rdy, 1)
                        if 4 <= u <= 10:
                            if u == 4:
                                if lag:
                                    dve.wait_ge(lv_sel[0], h * 8)
                                select(0, h, 0)
                            select(0, h, u - 3)
                            l = u - 3
                            own.wait()
                            dve.wait_ge(f_rdy, h + 1)
                            if l > 1:
                                dve.wait_ge(lv_up[0], h * LEVELS + (l - 1))
                            grow(dve, own, QF[0][:], KG[0][:], level_T(0, l - 1), level_T(0, l), 1 << (l - 1), True,
                                 SEQ).then_inc(lv_up[0], 1)
                        if u == 8:
                            if lag:
                                dve.wait_ge(o_mm[1], h)
                                dve.wait_ge(lv_sel[1], h * 8)
                            select(1, h, 0)
                            select(1, h, 1)
                        if u >= 9:
                            select(1, h, u - 7)
                    if lag:
                        if u <= 2:
                            select(1, hd, u + 5)
                        if u == 1:
                            states(0, hd)
                        if u == 4:
                            states(1, hd)
                        if u == 8:
                            dve.wait_ge(n_mm, hd + 1)
                            ts(osq[:], bank(UB), 1.0 / P, EPS, ALU.mult, ALU.add).then_inc(nv_rdy, 1)
                        if u == 9:
                            dve.wait_ge(rt_rdy, hd + 1)
                            own.did(dve.reciprocal(osq[:], osq[:]))
                        if u == 10:
                            own.wait()
                            own.did(tt(osq[:], bank(OB), osq[:], ALU.mult))
                            own.wait()
                            dve.wait_ge(gate_rdy, hd + 1)
                            tt(hg[:, ds(hd, 1), :], osq[:].unsqueeze(1), gate_sb[:].unsqueeze(1), ALU.mult
                               ).then_inc(hg_rdy, 1)
                    if main and u == 10:
                        dve.wait_ge(sig_og, h + 1)
                        if lag:
                            dve.wait_ge(hg_rdy, h + 1)
                        tt(gate_sb[:], bank(ZA), sig_a[:], ALU.mult).then_inc(gate_rdy, 1)

            lat_scan(0, True, False)
            with dve.Fori(1, HEADS) as h:
                own.loop(h - 1, PER["lat_v"])
                lat_scan(h, True, True)
                own.end(HEADS - 1)
            lat_scan(HEADS, False, True)
            dve.wait_ge(hg_rdy, HEADS + 1)
            for hd in range(HEADS):
                last = ts(hg[:, hd, :], hg[:, hd, :], vecT[:, V_HG + hd:V_HG + hd + 1], None, ALU.mult)
            last.then_inc(hgw_rdy, 1)

            with dve.Fori(0, KT) as j:
                own.loop(j, PER["merge_v"])
                for u in range(4):
                    nxt = u + 1
                    lo(j * 4 + (U_M + nxt), nxt if nxt < 4 else 0, nxt % 2)
                    dve.wait_ge(ada2_in[u % 2], j * 32 + 16 * (u // 2 + 1))
                    for kk in range(4):
                        k = 4 * u + kk
                        w = ada2[:, u % 2, kk, :]
                        if k == 0:
                            dve.wait_ge(row_mm, j + 1)
                            dve.wait_ge(ada2_free, j * 4 + 2)
                            ins = ts(acc[:], w, cs[:, 0, 0:1], None, ALU.mult)
                        else:
                            own.wait()
                            if kk == 0:
                                dve.wait_ge(ada2_free, j * 4 + (u + 2))
                            ins = stt(out=acc[:], in0=w, scalar=cs[:, 0, k:k + 1], in1=acc[:], op0=ALU.mult,
                                      op1=ALU.add)
                        if kk < 3:
                            own.did(ins)
                        else:
                            ins.then_inc(ada2_free, 1)
                dve.wait_ge(branch_free, j * 2 + 3)
                dve.wait_ge(gp_rdy, j + 2)
                dve.wait_ge(m_rdy, j + 1)
                tt(part_p[:], bank(BF), sig_gp[:], ALU.mult).then_inc(pp_rdy, 1)
                dve.wait_ge(branch_free, j * 2 + 4)
                dve.wait_ge(gh_rdy, j + 2)
                own.did(tt(part_h[:], bank(BB), sig_gh[:], ALU.mult))
                own.wait()
                dve.wait_ge(pp_rdy, j + 2)
                tt(m_sb[:, ds(j, 1), :], part_p[:].unsqueeze(1), part_h[:].unsqueeze(1), ALU.add).then_inc(m_rdy, 1)
                dve.wait_ge(row_mm, j + 2)
                dve.wait_ge(b_in, j * 16 + 16)
                dve.wait_ge(row_out, j * 16 + 32)
                tt(mod_row[0:1, :], ps[0:1, UB, :], b_row[0:1, :], ALU.add).then_inc(row_rdy, 1)
                own.end(KT)

            dve.wait_ge(m_rdy, KT + 1)
            for n in range(8):
                dve.wait_ge(h_hi, H_PIECES + n + 1)
                tt(m_lo[:, 2 * n:2 * n + 2, :], m_sb[:, 2 * n:2 * n + 2, :],
                   m_hi[:, 2 * n:2 * n + 2, :].bitcast(F32), ALU.subtract).then_inc(h_split, 1)

            def project(cb, last):
                for u in range(7 if last else 8):
                    nxt = u + 1
                    lo(cb * 8 + (S_W + nxt), nxt % 4, nxt % 2)
                dve.wait_ge(units_done, cb * 8 + (2 + S_W + 8))
                dve.wait_ge(xp_in, cb * 32 + 32)
                for t in range(NTOK):
                    tt(x2[:, t, ds(cb * 512, 512)], bank(t), m2_part[:], ALU.mult).then_inc(w_ev, 1)
                for t in range(NTOK):
                    dve.wait_ge(w_ev, cb * 4 + (4 + t + 1))
                    o = x2[:, t, ds(cb * 512, 512)]
                    tt(o, o, x_part[:, t, :], ALU.add).then_inc(x2_rdy, 1)

            with dve.Fori(0, 3) as cb:
                project(cb, False)
            project(3, True)

            dve.wait_ge(rows_in, 5 * 16)
            own.did(stt(out=m4_row[:], in0=m4_row[:], scalar=1.0, in1=n2_row[:], op0=ALU.add, op1=ALU.mult))
            dve.wait_ge(ssq_rdy, N_NORMS + 1)
            ts(stat2[:, 1, :], stat2[:, 0, :], 1.0 / D, EPS, ALU.mult, ALU.add).then_inc(var_rdy, 1)
            dve.wait_ge(std_rdy, N_NORMS + 1)
            own.did(dve.reciprocal(stat2[:, 3, :], stat2[:, 2, :]))
            own.wait()
            for t in range(NTOK):
                own.did(stt(out=h2[:, t, :], in0=x2[:, t, :], scalar=stat2[:, 3, t:t + 1], in1=m4_row[:],
                            op0=ALU.mult, op1=ALU.mult))
                own.wait()
                tt(h2[:, t, :], h2[:, t, :], m3_row[:], ALU.add).then_inc(h2_rdy, 1)
            for k in range(1, KT, 2):
                dve.wait_ge(h2_T, k + 1)
                dve.wait_ge(h2T_ev, k)
                dve.tensor_copy(h2T[:, k, :], bank(4 + k % 2)).then_inc(h2T_ev, 1)

            R = lambda i: rt[:, i, :]
            R3 = lambda i: rt[:, i, :].rearrange("p (t e) -> p t e", e=E)
            R4 = lambda i: rt[:, i, :].rearrange("p (g a) -> p g a", a=4)
            SM = lambda i: rt_small[:, i, :]

            def step(ins):
                own.did(ins)
                own.wait()

            def rank(value, out, scratch, width):
                v, o, s = (a.rearrange("p (g a) -> p g a", a=4) for a in (value, out, scratch))
                n = width // 4
                step(dve.memset(out, 0.0))
                for b in range(4):
                    if b < 3:
                        r = s[:, :, b + 1:4]
                        step(tt(r, v[:, :, b:b + 1].to_broadcast([P, n, 3 - b]), v[:, :, b + 1:4], ALU.is_ge))
                        step(tt(o[:, :, b + 1:4], o[:, :, b + 1:4], r, ALU.add))
                    if b > 0:
                        r = s[:, :, 0:b]
                        step(tt(r, v[:, :, b:b + 1].to_broadcast([P, n, b]), v[:, :, 0:b], ALU.is_gt))
                        step(tt(o[:, :, 0:b], o[:, :, 0:b], r, ALU.add))

            dve.wait_ge(score_rdy, 1)
            step(tt(R3(1), R3(0), bias_row[:].unsqueeze(1).to_broadcast([P, NTOK, E]), ALU.add))
            rank(R(1), R(2), R(3), NTOK * E)
            step(stt(out=R(4), in0=R(2), scalar=2.0, in1=R(1), op0=ALU.is_lt, op1=ALU.mult))
            step(dve.tensor_reduce(SM(0), R4(4), AX.X, ALU.add))
            rank(SM(0), SM(1), SM(2), NTOK * GROUPS)
            win_g = SM(3)
            step(ts(win_g, SM(1), 0.0, None, ALU.is_equal))
            of_group = win_g.unsqueeze(2).to_broadcast([P, NTOK * GROUPS, 4])
            step(stt(out=R4(9), in0=R4(2), scalar=0.0, in1=of_group, op0=ALU.is_equal, op1=ALU.mult))
            step(stt(out=R4(10), in0=R4(2), scalar=1.0, in1=of_group, op0=ALU.is_equal, op1=ALU.mult))
            tt(R(8), R(9), R(10), ALU.add).then_inc(sel_rdy, 1)
            for z in range(2):
                step(tt(R(4 + z), R(0), R(9 + z), ALU.mult))
                step(dve.tensor_reduce(gate_w[:, z, :], R3(4 + z), AX.X, ALU.add))
            step(tt(SM(4)[:, 0:NTOK], gate_w[:, 0, :], gate_w[:, 1, :], ALU.add))
            step(dve.reciprocal(SM(4)[:, 4:4 + NTOK], SM(4)[:, 0:NTOK]))
            for z in range(2):
                step(tt(gate_w[:, z, :], gate_w[:, z, :], SM(4)[:, 4:4 + NTOK], ALU.mult))
            dve.wait_ge(pos_mm, 1)
            step(dve.tensor_copy(SM(5), ps[:, 2, 0:E]))
            step(ts(SM(6), SM(5), float(BLK), None, ALU.is_gt))
            step(stt(out=SM(7), in0=SM(5), scalar=2.0 * BLK, in1=SM(6), op0=ALU.is_gt, op1=ALU.add))
            step(stt(out=SM(6), in0=SM(5), scalar=3.0 * BLK, in1=SM(7), op0=ALU.is_gt, op1=ALU.add))
            step(dve.tensor_tensor_scan(SM(8), ones[:, 0:E], SM(6), 0.0, ALU.mult, ALU.add))
            step(tt(SM(9), SM(8), SM(6), ALU.subtract))
            step(ts(SM(9), SM(9), E - 1.0, float(BLK), ALU.add, ALU.mult))
            step(stt(out=SM(10), in0=iota_e[:], scalar=float(BLK), in1=SM(9), op0=ALU.mult, op1=ALU.subtract))
            step(dve.tensor_copy(R(4), ps[:, 1, 0:NTOK * E]))
            over_t = lambda a: a.unsqueeze(1).to_broadcast([P, NTOK, E])
            step(stt(out=R3(5), in0=R3(4), scalar=float(BLK), in1=over_t(SM(10)), op0=ALU.is_lt, op1=ALU.mult))
            step(tt(R(5), R(5), R(4), ALU.add))
            step(tt(R3(5), R3(5), over_t(SM(9)), ALU.add))
            for z in range(2):
                step(tt(R(6 + z), R(5), R(9 + z), ALU.mult))
                step(dve.tensor_reduce(SM(11)[:, 4 * z:4 * z + NTOK], R3(6 + z), AX.X, ALU.add))
            dve.tensor_copy(dest_i[:].rearrange("p z t -> p (z t)"), SM(11)[:, 0:2 * NTOK]).then_inc(dest_rdy, 1)
            later = rt[:, 11:13, :].rearrange("p a b -> p (a b)")[:, 0:NXTRA * E].rearrange("p (b e) -> p b e", e=E)
            step(tt(later, SM(8).unsqueeze(1).to_broadcast([P, NXTRA, E]),
                    iota_e[:, 0:NXTRA].unsqueeze(2).to_broadcast([P, NXTRA, E]), ALU.is_le))
            step(dve.tensor_reduce(SM(12)[:, 0:NXTRA], later, AX.X, ALU.add))
            step(ts(SM(12)[:, 0:NXTRA], SM(12)[:, 0:NXTRA], E - 1.0, None, ALU.min))
            step(dve.tensor_copy(SM(12)[:, NXTRA:NXTRA + 1], SM(8)[:, E - 1:E]))
            step(dve.tensor_copy(route_i[:], SM(12)[:, 0:8]))
            step(dve.memset(table_i[:], 0))
            dve.wait_ge(tab_T, 1)
            dve.tensor_copy(table_i[:, 0:NBLK], ps[:, 3, 0:NBLK]).then_inc(table_rdy, 1)

            def e_lo_unit(g, slot, hslot):
                dve.wait_ge(e_hi_done, g + 1)
                tt(e_lo[:, hslot, :], e_raw[:, slot, :], e_hi[:, hslot, :].bitcast(F32), ALU.subtract
                   ).then_inc(e_split, 1)

            def x_lo(b, part):
                dve.wait_ge(xe_hi_rdy, b * 4 + (part + 1))
                tt(xe_lo[:, 4 * part:4 * part + 4, :].rearrange("p k t -> p (k t)"), bank(6 + part % 2),
                   xe_hi[:, 4 * part:4 * part + 4, :].rearrange("p k t -> p (k t)").bitcast(F32), ALU.subtract
                   ).then_inc(xe_rdy, 1)

            def silu(b, first=False):
                dve.wait_ge(sg_rdy, b + 1)
                if not first:
                    dve.wait_ge(act_rdy, b)
                tt(act_u[:], bank(0), act_sig[:], ALU.mult).then_inc(u_rdy, 1)

            def gate_up(b, units, first=False):
                dve.wait_ge(e_units, units)
                dve.wait_ge(u_rdy, b + 1)
                if not first:
                    dve.wait_ge(act_T, b)
                tt(act[:], bank(1), act_u[:], ALU.mult).then_inc(act_rdy, 1)

            def act_lo(b):
                dve.wait_ge(actT_hi_rdy, b + 1)
                tt(actT_lo[:].rearrange("p k t -> p (k t)"), bank(6),
                   actT_hi[:].rearrange("p k t -> p (k t)").bitcast(F32), ALU.subtract).then_inc(actT_rdy, 1)

            AHEAD = 3
            for q in range(AHEAD):
                e_lo_unit(q, q, q)
            for part in range(4):
                x_lo(0, part)
            for q in range(16):
                n = q + AHEAD
                e_lo_unit(n, n % 8, n % 4)
                if q == 8:
                    silu(0, True)
            gate_up(0, 4 + 16, True)
            for part in range(4):
                x_lo(1, part)
            with dve.Fori(1, E) as e:
                for q in range(24):
                    n = q + AHEAD
                    e_lo_unit(e * 24 + (n - 8), n % 8, n % 4)
                    if q == 3:
                        act_lo(e - 1)
                    if q == 9:
                        silu(e)
                    if q == 17:
                        gate_up(e, e * 24 + 12)
                    if 18 <= q <= 21:
                        x_lo(e + 1, q - 18)
            act_lo(E - 1)
            for q in range(AHEAD, 8):
                n = E * 24 - 8 + q
                e_lo_unit(n, n % 8, n % 4)
            n_extra = dve.value_load(route_i[0:1, 7:8], min_val=0, max_val=NXTRA)
            with dve.Fori(0, NXTRA) as b:
                with dve.If(b < n_extra):
                    for part in range(4):
                        x_lo(b + (E + 1), part)
                    for q in range(24):
                        e_lo_unit(b * 24 + (24 * E + q), q % 8, q % 4)
                        if q == 10:
                            silu(b + E)
                        if q == 16:
                            gate_up(b + E, b * 24 + (24 * E + 20))
                            act_lo(b + E)
                dve.nop()

            dve.wait_ge(rows_in, 7 * 16)
            for i in range(NTOK):
                o = o_sb[:, i % 2, :]
                dve.wait_ge(y_in[i % 2], 32 * (i // 2 + 1))
                if i >= 2:
                    dve.wait_ge(o_out[i % 2], 16)
                step(ts(o, y0[:, i % 2, :], gate_w[:, 0, i:i + 1], None, ALU.mult))
                step(stt(out=o, in0=y1[:, i % 2, :], scalar=gate_w[:, 1, i:i + 1], in1=o, op0=ALU.mult, op1=ALU.add))
                step(tt(o, o, m5_row[:], ALU.mult))
                tt(o, o, x2[:, i, :], ALU.add).then_inc(f_sum, 1)
                dve.wait_ge(ssq_rdy, N_NORMS + 1 + i + 1)
                ts(stat2[:, 1, i:i + 1], stat2[:, 0, i:i + 1], 1.0 / D, EPS, ALU.mult, ALU.add).then_inc(var_rdy, 1)
                dve.wait_ge(std_rdy, N_NORMS + 1 + i + 1)
                step(dve.reciprocal(stat2[:, 3, i:i + 1], stat2[:, 2, i:i + 1]))
                stt(out=o, in0=o, scalar=stat2[:, 3, i:i + 1], in1=fn_row[:], op0=ALU.mult, op1=ALU.mult
                    ).then_inc(o_rdy, 1)

        @block.gpsimd
        def _(pool):
            own = Chain(pool, p_own)
            tt, ts = pool.tensor_tensor, pool.tensor_scalar

            own.did(pool.memset(osq[:], 0.0))
            own.wait()
            pool.dma_start(tok_d.rearrange("(b p) o -> b (p o)", p=P), osq[0:NBLK, 0:P]).then_inc(row_out, 16)
            pool.dma_start(y_d[E * BLK:, :].rearrange("(p r) (s n) -> p (r s) n", p=P, n=512),
                           osq[:].unsqueeze(1).to_broadcast([P, NXTRA * D // 512, 512])).then_inc(row_out, 16)
            pool.wait_ge(row_out, 32)

            def lower_bound(h):
                own.wait()
                own.did(pool.tensor_copy(lb_p[:], lb_all[:, ds(h, 1), :].rearrange("p o w -> p (o w)")))
                own.wait()
                own.pass_waits()

            def ctx_scan(h, lag):
                pool.wait_ge(c_sig_b, h + 1)
                lower_bound(h)
                if lag:
                    pool.wait_ge(c_kg_T, h)
                    pool.wait_ge(c_kg_b, h)
                    own.pass_waits()
                own.did(ts(c_f[:, 1, :], c_sig[:, 1, :], lb_p[:, 3:4], lb_p[:, 2:3], ALU.mult, ALU.add))
                own.wait()
                own.pass_waits()
                own.did(ts(c_kg[:, 1, :], c_f[:, 1, :], -1.0, 1.0, ALU.mult, ALU.add))
                ctx_decays(pool, own, 1).then_inc(c_kg_b, 1)

            ctx_scan(0, False)
            with pool.Fori(1, HEADS) as h:
                own.loop(h - 1, PER["ctx_p"])
                ctx_scan(h, True)
                own.end(HEADS - 1)

            pool.wait_ge(ctx_state, HEADS + 1)
            pool.memset(up[:], 0.0).then_inc(pad_rdy, 1)

            def windows(h):
                pool.wait_ge(p_ev, h + 1)
                pool.wait_ge(coef_in, h * 16 + 16)
                u = up[:, :, HALO:HALO + GRID_W]
                src = up
                for m, (a, b, off) in enumerate(((1, 79, None), (2, 78, 1), (4, 76, 2), (8, 72, 4))):
                    dst = win[m % 2]
                    l, r = (1, 0) if off is None else (off, off)
                    lo_ = src[:, :, a - l:b - l]
                    hi_ = src[:, :, a:b] if off is None else src[:, :, a + r:b + r]
                    own.wait()
                    own.did(tt(dst[:, :, a:b], lo_, hi_, ALU.add))
                    own.wait()
                    c_m = coef[:, m, :].unsqueeze(1).to_broadcast([P, ROWS, GRID_W])
                    t = pool_acc if m == 0 else pool_t
                    own.did(tt(t[:], dst[:, :, HALO:HALO + GRID_W], c_m, ALU.mult))
                    if m:
                        own.wait()
                        own.did(tt(pool_acc[:], pool_acc[:], pool_t[:], ALU.add))
                    src = dst
                own.wait()
                tt(delta[:, ds(h, 1), :].rearrange("p o (r w) -> p (o r) w", w=GRID_W), pool_acc[:], u, ALU.subtract
                   ).then_inc(pool_rdy, 1)

            def lat_scan(h, lag):
                if lag:
                    pool.wait_ge(pool_rdy, h)
                own.wait()
                pool.dma_start(coef[:], pool_coefs[ds(h, 1)].rearrange("o p m w -> (o p) m w")).then_inc(coef_in, 16)
                pool.wait_ge(sig_bw, h + 1)
                lower_bound(h)
                own.did(ts(f_sb[1][:], sig_b[:], lb_p[:, 3:4], lb_p[:, 2:3], ALU.mult, ALU.add))
                own.wait()
                if lag:
                    pool.wait_ge(o_mm[1], h)
                    pool.wait_ge(lv_up[1], h * LEVELS)
                    own.pass_waits()
                own.did(ts(KG[1][:], f_sb[1][:], -1.0, 1.0, ALU.mult, ALU.add))
                pool.wait_ge(q_rdy, h + 1)
                tt(QF[1][:], q_sb[:], f_sb[1][:], ALU.mult).then_inc(fb_rdy, 1)
                for l in range(1, LEVELS + 1):
                    pool.wait_ge(lv_mm[1], h * 8 + (l + 1))
                    own.wait()
                    if l == 1:
                        pool.wait_ge(fb_rdy, h + 1)
                    else:
                        pool.wait_ge(lv_up[1], h * LEVELS + (l - 1))
                    grow(pool, own, QF[1][:], KG[1][:], level_T(1, l - 1), level_T(1, l), 1 << (l - 1), False,
                         SEQ).then_inc(lv_up[1], 1)
                windows(h)

            lat_scan(0, False)
            with pool.Fori(1, HEADS) as h:
                own.loop(h - 1, PER["lat_p"])
                lat_scan(h, True)
                own.end(HEADS - 1)

            pool.wait_ge(hg_rdy, HEADS + 1)
            pool.wait_ge(pool_rdy, HEADS)
            pool.dma_start(w_pg[:], w_pg_d).then_inc(coef_in, 16)
            pool.wait_ge(pg_mm, HEADS)

            def load_ada(j, q):
                pool.wait_ge(ada2_free, j * 4 + (q + 1))
                pool.dma_start(ada2[:, q % 2], w_ada_d[:, 4 * q:4 * q + 4, ds(j * 512 + 2 * D, 512)]
                               ).then_inc(ada2_in[q % 2], 16)

            def merge(j, last):
                pool.wait_ge(row_rdy, j + 1)
                pool.dma_start(b_row[0:1, :], b_ada[0:1, ds(j * 512 + 2 * D, 512)]).then_inc(b_in, 16)
                load_ada(j, 2)
                load_ada(j, 3)
                if not last:
                    load_ada(j + 1, 0)
                    load_ada(j + 1, 1)
                pool.wait_ge(row_rdy, j + 2)
                pool.dma_start(mod_d[0:1, ds(j * 512, 512)], mod_row[0:1, :]).then_inc(row_out, 16)

            load_ada(0, 0)
            load_ada(0, 1)
            with pool.Fori(0, KT - 1) as j:
                merge(j, False)
            merge(KT - 1, True)

            pool.wait_ge(row_out, 16 * (KT + 2))
            pool.wait_ge(m_rdy, KT + 1)
            pool.wait_ge(branch_free, 2 + 2 * KT)
            x_all = x[0].rearrange("(t p) d -> p t d", p=P)
            with pool.Fori(0, 4) as cb:
                pool.wait_ge(x2_rdy, cb * 4 + 4)
                pool.dma_start(x_part[:], x_all[:, :, ds(cb * 512, 512)]).then_inc(xp_in, 16)
                pool.dma_start(m2_part[:], mod_d[0, ds(cb * 512, 512)].partition_broadcast(P)).then_inc(xp_in, 16)

            pool.wait_ge(units_done, 2 + S_W + 32)
            pool.dma_start(m4_row[:], mod_d[0, 2 * D:3 * D].partition_broadcast(P)).then_inc(rows_in, 16)
            pool.dma_start(n2_row[:], norm2_w[0].partition_broadcast(P)).then_inc(rows_in, 16)
            pool.dma_start(m3_row[:], mod_d[0, D:2 * D].partition_broadcast(P)).then_inc(rows_in, 16)
            pool.dma_start(w_r[:], w_r_d).then_inc(rows_in, 16)
            pool.dma_start(bias_row[:], router_bias.partition_broadcast(P)).then_inc(rows_in, 16)
            h2_rows = h2_d.rearrange("(t p) d -> t p d", p=P)
            for t in range(NTOK):
                pool.wait_ge(h2_rdy, t + 1)
                pool.dma_start(h2_rows[t], h2[:, t, :]).then_inc(y_out, 16)
            pool.wait_ge(y_out, 16 * NTOK)
            pool.wait_ge(h2_T, KT)
            pool.dma_start(m5_row[:], mod_d[0, 3 * D:4 * D].partition_broadcast(P)).then_inc(rows_in, 16)
            pool.dma_start(fn_row[:], final_norm_w.partition_broadcast(P)).then_inc(rows_in, 16)
            pool.wait_ge(dest_rdy, 1)
            for z in range(2):
                for t in range(NTOK):
                    pool.indirect_dma_start(out=tok_d, out_offset=bass.IndirectOffsetOnAxis(
                        ap=dest_i[:, z, t:t + 1], axis=0), in_=tok_ids[:, t:t + 1], in_offset=None
                        ).then_inc(tok_out, 16)
            pool.wait_ge(tok_out, 16 * 2 * NTOK)
            pool.dma_start(table_rows[0:NBLK, :], tok_d.rearrange("(b p) o -> b (p o)", p=P)).then_inc(tab_in, 16)
            pool.wait_ge(table_rdy, 1)

            def gather(b, column):
                own.wait()
                own.did(pool.tensor_copy(idx_now[:], table_i[:, ds(column, 1)]))
                own.wait()
                own.pass_waits()
                pool.indirect_dma_start(out=xe[:], out_offset=None, in_=h2_d,
                                        in_offset=bass.IndirectOffsetOnAxis(ap=idx_now[:, 0:1], axis=0)
                                        ).then_inc(xe_in, 16)

            def store(b):
                pool.wait_ge(y_ev, b * 4 + 8)
                pool.dma_start(y_d[ds(b * BLK, BLK), :], y_sb[:]).then_inc(y_out, 16)

            gather(0, 0)
            pool.wait_ge(xe_in, 16)
            pool.wait_ge(xe_T, 4)
            gather(1, 1)
            with pool.Fori(1, E) as e:
                own.loop(e - 1, 2)
                pool.wait_ge(xe_in, e * 16 + 16)
                pool.wait_ge(xe_T, e * 4 + 4)
                gather(e + 1, e + 1)
                store(e - 1)
                own.end(E - 1)
            store(E - 1)
            pool.wait_ge(y_out, 16 * (E + NTOK))
            pool.wait_ge(xe_in, 16 * (E + 1))
            n_extra = pool.value_load(route_i[0:1, 7:8], min_val=0, max_val=NXTRA)
            with pool.Fori(0, NXTRA) as b:
                with pool.If(b < n_extra):
                    own.loop(b, 2)
                    pool.wait_ge(xe_T, b * 4 + 4 * (E + 1))
                    gather(b + (E + 1), b + E)
                    pool.wait_ge(xe_in, b * 16 + 16 * (E + 2))
                    store(b + E)
                    pool.wait_ge(y_out, b * 16 + 16 * (E + NTOK + 1))
                    own.end(0)
                pool.nop()

            for i in range(NTOK):
                if i >= 2:
                    pool.wait_ge(o_rdy, i - 1)
                for z, dst in ((0, y0), (1, y1)):
                    pool.indirect_dma_start(out=dst[:, i % 2, :], out_offset=None, in_=y_d,
                                            in_offset=bass.IndirectOffsetOnAxis(ap=dest_i[:, z, i:i + 1], axis=0)
                                            ).then_inc(y_in[i % 2], 16)


PER = dict(ctx_v=17, ctx_p=20, lat_v=39, lat_p=30, merge_v=13)

_INS = ["x", "c", "ctx", "c_ctx", "w_ada", "b_ada", "norm1_w", "norm2_w", "w_in", "w_pool_group", "pool_scale",
        "hg_norm_w", "lb_logits", "w_branch_pool", "w_branch_hgrn", "w_out", "w_router", "router_bias",
        "w_e1", "w_e3", "w_e2", "final_norm_w"]


def shape_constants():
    i = np.arange(P)
    const = np.zeros((P, 2 * P + E + NTOK), np.float32)
    const[:, 0:P] = np.eye(P)
    const[:, P:2 * P] = i[:, None] < i[None, :]
    const[:, 2 * P:2 * P + E] = np.arange(E)
    const[:, 2 * P + E:] = i[:, None] + P * np.arange(NTOK)
    s, t = i[:, None], i[None, :]
    masks = np.zeros((P, 2, LEVELS, P), np.float32)
    for l in range(LEVELS):
        same = (s >> (l + 1)) == (t >> (l + 1))
        masks[:, 0, l] = same & ((t >> l) & 1 == 1) & ((s >> l) & 1 == 0)
        masks[:, 1, l] = same & ((t >> l) & 1 == 0) & ((s >> l) & 1 == 1)
    w = np.arange(GRID_W)
    coefs = np.zeros((HEADS, P, 4, GRID_W), np.float32)
    for h in range(HEADS):
        m = h // 2
        half = WINDOWS[m] // 2
        count = np.minimum(w + half - 1, GRID_W - 1) - np.maximum(w - half, 0) + 1
        coefs[h, :, m, :] = 1.0 / count
    return const, masks, coefs


def kernel(**inputs):
    import concourse.bacc as _bacc
    from concourse.bass_utils import run_bass_kernel_spmd as _run

    nc = _bacc.Bacc("TRN2", target_bir_lowering=False, num_devices=1)
    arrays, args = {}, []

    def give(name, a):
        a = np.ascontiguousarray(a)
        arrays[f"in_{name}"] = a
        args.append(nc.dram_tensor(f"in_{name}", a.shape, mybir.dt.from_np(a.dtype), kind="ExternalInput").ap())

    for name in _INS:
        give(name, inputs[name])
    for name, a in zip(("consts", "level_masks", "pool_coefs"), shape_constants()):
        give(name, a)
    out = nc.dram_tensor("out_0", (1, SEQ, D), F32, kind="ExternalOutput").ap()
    build(nc, *args, out)
    r = _run(nc, [arrays], core_ids=[0])
    return r.results[0]["out_0"]
```

```python
from contextlib import ExitStack

import numpy as np

import concourse.bass as bass
from concourse import mybir

F32 = mybir.dt.float32
F32R = mybir.dt.float32r
I32 = mybir.dt.int32
U8 = mybir.dt.uint8
ALU = mybir.AluOpType
ACT = mybir.ActivationFunctionType
AX = mybir.AxisListType
ds = bass.ds

P = 128
D = 2048
KT = D // P
SEQ = 512
CTX = 256
NTOK = SEQ // P
NCTX = CTX // P
HEADS = 8
D_POOL = 1024
WINDOWS = (2, 4, 8, 16)
GRID_W = 64
ROWS = SEQ // GRID_W
HALO = 8
PADW = GRID_W + 2 * HALO
LEVELS = 7
NCH = SEQ // P
CTX_LEVELS = 8
E = 16
GROUPS = 4
DX = 512
BLK = 128
NXTRA = 7
NBLK = E + NXTRA
EPS = 1e-6
UNIT = 1024
SLOTS = 6
KB = 1024
BIG = 1 << 20

COL = dict(p=0, q=1024, ff=2048, fb=3072, i=4096, og=5120, gp=6144, gh=8192)
V_C, V_CC, V_N1, V_B, V_PS, V_HG, V_LB, V_ROWS = 0, 16, 32, 48, 80, 88, 96, 112


class Chain:

    def __init__(self, eng, sem):
        self.eng, self.sem, self.start, self.k = eng, sem, 0, 0

    def did(self, ins):
        ins.then_inc(self.sem, 1)
        self.k += 1

    def wait(self):
        self.eng.wait_ge(self.sem, self.start + self.k)

    def pass_waits(self):
        self.eng.sem_inc(self.sem, 1)
        self.k += 1

    def loop(self, turn, per):
        self.entry = (self.start, self.k, per)
        self.start, self.k = self.start + self.k + turn * per, 0

    def end(self, turns):
        start, k, per = self.entry
        assert self.k == per, f"{self.sem}: {self.k} instructions in a turn, {per} stated"
        self.start, self.k = start, k + turns * per


class Room:

    def __init__(self, nc, base, start_kb, end_kb):
        self.nc, self.at, self.end = nc, base + int(start_kb * KB), base + int(end_kb * KB)

    def new(self, name, shape, dtype):
        size = int(np.prod(shape[1:])) * {F32: 4, F32R: 4, I32: 4, U8: 1}[dtype]
        at = self.at
        self.at += (size + 31) // 32 * 32
        assert self.at <= self.end, f"{name} does not fit: {self.at - self.end} bytes over"
        return self.nc.alloc_sbuf_tensor_at(name, shape, dtype, offset=at)


def grow(eng, chain, QF, KG, T, T_next, half, forward, width):
    n = width // (2 * half)
    t = T.rearrange("p (n two) -> p n two", two=2)
    a, b = (1, 0) if forward else (0, 1)
    k = KG.rearrange("p (n two h) -> p n two h", two=2, h=half)
    if QF is not None:
        q = QF.rearrange("p (n two h) -> p n two h", two=2, h=half)
        chain.did(eng.tensor_tensor(q[:, :, a, :], q[:, :, a, :],
                                    t[:, :, b].unsqueeze(2).to_broadcast([P, n, half]), ALU.mult))
    last = eng.tensor_tensor(k[:, :, b, :], k[:, :, b, :],
                             t[:, :, a].unsqueeze(2).to_broadcast([P, n, half]), ALU.mult)
    if T_next is not None:
        chain.did(last)
        last = eng.tensor_tensor(T_next, t[:, :, 0], t[:, :, 1], ALU.mult)
    return last


def build(nc, x, c, ctx_tokens, c_ctx, w_ada, b_ada, norm1_w, norm2_w, w_in, w_pool_group, pool_scale,
          hg_norm_w, lb_logits, w_branch_pool, w_branch_hgrn, w_out, w_router, router_bias, w_e1, w_e3,
          w_e2, final_norm_w, consts, level_masks, pool_coefs, out):
    x_d = x[0].rearrange("(i p) d -> i p d", p=P)
    ctx_d = ctx_tokens[0].rearrange("(i p) d -> i p d", p=P)
    out_d = out[0].rearrange("(i p) d -> i p d", p=P)
    w_in_d = w_in[0].rearrange("(k p) n -> p k n", p=P)
    w_ada_d = w_ada[0].rearrange("(k p) n -> p k n", p=P)
    w_bp_d = w_branch_pool[0].rearrange("(k p) n -> p k n", p=P)
    w_bh_d = w_branch_hgrn[0].rearrange("(k p) n -> p k n", p=P)
    w_out_d = w_out[0].rearrange("(k p) n -> p k n", p=P)
    w_pg_d = w_pool_group[0].rearrange("g (k p) n -> p g k n", p=P)
    w_e1_d = w_e1[0].rearrange("e (k p) n -> e p k n", p=P)
    w_e3_d = w_e3[0].rearrange("e (k p) n -> e p k n", p=P)
    w_e2_d = w_e2[0].rearrange("e (k p) n -> e p k n", p=P)
    w_r_d = w_router.rearrange("(k p) n -> p k n", p=P)

    mod_d = nc.dram_tensor("mod_rows", [1, 4 * D], F32).ap()
    m_d = nc.dram_tensor("merged", [KT, P, SEQ], F32).ap()
    h2_d = nc.dram_tensor("h2_rows", [SEQ, D], F32).ap()
    y_d = nc.dram_tensor("block_outputs", [NBLK * BLK, D], F32).ap()

    stack = ExitStack()
    with stack:
        base = (nc.sbuf_base + 63) // 64 * 64
        top = (nc.sbuf_usable_end - base) / KB

        def sem(name):
            return stack.enter_context(nc.semaphore(name))

        def psum(name, shape):
            return stack.enter_context(nc.psum_tensor(name, shape, F32))

        small = Room(nc, base, 0, 10)
        ident = small.new("ident", [P, P], F32)
        upper = small.new("strict_upper", [P, P], F32)
        iota = small.new("iota", [P, P], F32)
        iota_e = iota[:, 0:E]
        tok_ids = small.new("tok_ids", [P, NTOK], F32)
        ones = small.new("ones", [P, P], F32)
        masks = small.new("level_masks_sb", [P, 2, LEVELS, P // 2], U8)
        vecT = small.new("vecT", [P, V_ROWS], F32)
        cs = small.new("silu_c", [P, 2, KT], F32)
        modT = small.new("modT", [P, 2 * KT, 2], F32)
        scale1 = small.new("scale1", [P, KT, 2], F32)
        lb_all = small.new("lb_all", [P, HEADS, 4], F32)
        lb_tmp = small.new("lb_tmp", [P, 4, 16], F32)
        stat = small.new("stat", [P, 4, 8], F32)
        lb_v = small.new("lb_v", [P, 4], F32)
        lb_p = small.new("lb_p", [P, 4], F32)
        mod_row = small.new("mod_row", [P, 512], F32)

        ada_ring = Room(nc, base, 10, 74).new("ada_ring", [P, 4, 4096], F32)
        ring_start = Room(nc, base, 74, 98)
        x_tok = ring_start.new("x_tok", [P, 3, D], F32)
        prep = Room(nc, base, 98, 114)
        vec_rows = prep.new("vec_rows", [P, P], F32)
        square_junk = prep.new("square_junk", [P, D], F32)
        mod01_row = Room(nc, base, 201, 205).new("mod01_row", [P, 2, 512], F32)
        masks_in = Room(nc, base, 194, 201).new("masks_in", [P, 2, LEVELS, P // 2], F32)
        xT_ctx = Room(nc, base, 114, 130).new("xT_ctx", [P, KT, CTX], F32)
        xT_lat = Room(nc, base, 130, 162).new("xT_lat", [P, KT, SEQ], F32)
        hc_room = Room(nc, base, 162, 194)
        hc_hi = hc_room.new("hc_hi", [P, KT, CTX], F32R)
        hc_lo = hc_room.new("hc_lo", [P, KT, CTX], F32R)
        hl_room = Room(nc, base, 10, 74)
        hl_hi = hl_room.new("hl_hi", [P, KT, SEQ], F32R)
        hl_lo = hl_room.new("hl_lo", [P, KT, SEQ], F32R)
        ring = Room(nc, base, 74, 114)
        raw = ring.new("raw", [P, SLOTS, UNIT], F32)
        w_hi = ring.new("w_hi", [P, 2, UNIT], F32R)
        w_lo = ring.new("w_lo", [P, 2, UNIT], F32R)
        cw = Room(nc, base, 114, 130)
        c_sig = cw.new("c_sig", [P, 2, CTX], F32)
        c_f = cw.new("c_f", [P, 2, CTX], F32)
        c_kg = cw.new("c_kg", [P, 2, CTX], F32)
        c_T = cw.new("c_T", [P, 2, CTX], F32)
        c_vT = cw.new("c_vT", [P, CTX], F32)
        c_v = cw.new("c_v", [P, NCTX, P], F32)
        c_kgT = cw.new("c_kgT", [P, 2, NCTX, P], F32)
        s_ctx = Room(nc, base, 194, 202).new("s_ctx", [P, 2, HEADS, P], F32)
        hg = Room(nc, base, 130, 146).new("hg", [P, HEADS, SEQ], F32)
        delta = Room(nc, base, 162, 178).new("delta", [P, HEADS, SEQ], F32)
        ra = Room(nc, base, 114, 130)
        rb = Room(nc, base, 146, 162)
        rc = Room(nc, base, 178, 194)
        rd = Room(nc, base, 202, top)
        QF = [ra.new("QF_f", [P, SEQ], F32), ra.new("QF_b", [P, SEQ], F32)]
        KG = [ra.new("KG_f", [P, SEQ], F32), ra.new("KG_b", [P, SEQ], F32)]
        TT = [ra.new("T_f", [P, SEQ], F32), ra.new("T_b", [P, SEQ], F32)]
        A = [ra.new("A_f", [P, NCH, P], F32), ra.new("A_b", [P, NCH, P], F32)]
        S = [rb.new("S_f", [P, NCH, P], F32), rb.new("S_b", [P, NCH, P], F32)]
        q_sb = rb.new("q_sb", [P, SEQ], F32)
        f_sb = [rb.new("f_f", [P, SEQ], F32), rb.new("f_b", [P, SEQ], F32)]
        vT_sb = rb.new("vT_sb", [P, SEQ], F32)
        v_sb = rb.new("v_sb", [P, NCH, P], F32)
        gate_sb = rb.new("gate_sb", [P, SEQ], F32)
        up = rc.new("up", [P, ROWS, PADW], F32)
        win = [rc.new("win_a", [P, ROWS, PADW], F32), rc.new("win_b", [P, ROWS, PADW], F32)]
        pool_t = rc.new("pool_t", [P, ROWS, GRID_W], F32)
        pool_acc = rc.new("pool_acc", [P, ROWS, GRID_W], F32)
        sig_a = rc.new("sig_a", [P, SEQ], F32)
        sig_b = rc.new("sig_b", [P, SEQ], F32)
        coef = rd.new("coef", [P, 4, GRID_W], F32)
        kgT = [rd.new("kgT_f", [P, NCH - 1, P], F32), rd.new("kgT_b", [P, NCH - 1, P], F32)]
        osq = small.new("osq", [P, SEQ], F32)
        w_pg = Room(nc, base, 114, 122).new("w_pg", [P, 4, 2, 256], F32)
        ada2 = Room(nc, base, 114, 130).new("ada2", [P, 2, 4, 512], F32)
        poolT = Room(nc, base, 146, 162).new("poolT", [P, HEADS, SEQ], F32)
        hg_lo = Room(nc, base, 130, 146).new("hg_lo", [P, HEADS, SEQ], F32R)
        poolT_lo = Room(nc, base, 146, 162).new("poolT_lo", [P, HEADS, SEQ], F32R)
        hg_hi = Room(nc, base, 162, 178).new("hg_hi", [P, HEADS, SEQ], F32R)
        poolT_hi = Room(nc, base, 178, 194).new("poolT_hi", [P, HEADS, SEQ], F32R)
        mw = Room(nc, base, 194, top)
        acc = mw.new("ada_acc", [P, 512], F32)
        b_row = mw.new("b_row", [P, 512], F32)
        sig_gp = mw.new("sig_gp", [P, SEQ], F32)
        sig_gh = mw.new("sig_gh", [P, SEQ], F32)
        part_p = mw.new("part_p", [P, SEQ], F32)
        m_row = mw.new("m_row", [P, SEQ], F32)
        m_room = Room(nc, base, 10, 74)
        m_hi = m_room.new("m_hi", [P, KT, SEQ], F32R)
        m_lo = m_room.new("m_lo", [P, KT, SEQ], F32R)
        m_sb = Room(nc, base, 42, 74).new("m_sb", [P, KT, SEQ], F32)
        x2 = Room(nc, base, 114, 146).new("x2", [P, NTOK, D], F32)
        ow = Room(nc, base, 146, 154)
        x_part = ow.new("x_part", [P, NTOK, 512], F32)
        
        h2 = Room(nc, base, 162, 194).new("h2", [P, NTOK, D], F32)
        m4_row = Room(nc, base, 90, 98).new("m4_row", [P, D], F32)
        m3_row = Room(nc, base, 154, 162).new("m3_row", [P, D], F32)
        h2T = Room(nc, base, 10, 42).new("h2T", [P, KT, SEQ], F32)
        rt_room = Room(nc, base, 194, 206)
        rt = rt_room.new("rt", [P, 20, NTOK * E], F32)
        rt_small = rt_room.new("rt_small", [P, 16, E], F32)
        w_r = rt_room.new("w_r", [P, KT, E], F32)
        bias_row = rt_room.new("bias_row", [P, E], F32)
        m2_part = rt_room.new("m2_part", [P, 512], F32)
        n2_part = rt_room.new("n2_part", [P, 512], F32)
        keep = Room(nc, base, 206, top)
        dest_i = keep.new("dest_i", [P, 2, NTOK], I32)
        gate_w = keep.new("gate_w", [P, 2, NTOK], F32)
        table_i = keep.new("table_i", [P, NBLK + 1], I32)
        idx_now = keep.new("idx_now", [P, 1], I32)
        route_i = keep.new("route_i", [P, 8], I32)
        stat2 = keep.new("stat2", [P, 4, NTOK], F32)
        part_sq = rt_room.new("part_sq", [P, NTOK, 4], F32)
        tb = Room(nc, base, 42, 54)
        in_block = tb.new("in_block", [P, 2 * NTOK, NBLK + 1], F32)
        block_tok = tb.new("block_tok", [P, 2 * NTOK, NBLK], F32)
        slot_1 = tb.new("slot_1", [P, 2 * NTOK, P], F32)
        e_raw = Room(nc, base, 74, 106).new("e_raw", [P, 8, UNIT], F32)
        act_room = Room(nc, base, 106, 114)
        act_sig = act_room.new("act_sig", [P, DX], F32)
        act_u = act_room.new("act_u", [P, DX], F32)
        act = act_room.new("act", [P, DX], F32)
        eh = Room(nc, base, 42, 74)
        e_hi = eh.new("e_hi", [P, 4, UNIT], F32R)
        e_lo = eh.new("e_lo", [P, 4, UNIT], F32R)
        ex = Room(nc, base, 10, 42)
        xe_hi = ex.new("xe_hi", [P, KT, BLK], F32R)
        xe_lo = ex.new("xe_lo", [P, KT, BLK], F32R)
        actT_hi = ex.new("actT_hi", [P, 4, BLK], F32R)
        actT_lo = ex.new("actT_lo", [P, 4, BLK], F32R)
        xe = Room(nc, base, 148, 156).new("xe", [P, D], F32)
        y_sb = Room(nc, base, 162, 170).new("y_sb", [P, D], F32)
        m5_row = Room(nc, base, 170, 178).new("m5_row", [P, D], F32)
        fn_row = Room(nc, base, 178, 186).new("fn_row", [P, D], F32)
        y0 = Room(nc, base, 10, 42).new("y0", [P, NTOK, D], F32)
        y1 = Room(nc, base, 42, 74).new("y1", [P, NTOK, D], F32)
        f_junk = Room(nc, base, 106, 114).new("f_junk", [P, D], F32)
        o_sb = Room(nc, base, 74, 106).new("o_sb", [P, NTOK, D], F32)

        T_AT = [0] + [sum(SEQ >> k for k in range(1, l)) for l in range(1, LEVELS + 1)]

        def level_T(z, l):
            return f_sb[z][:] if l == 0 else TT[z][:, T_AT[l]:T_AT[l] + (SEQ >> l)]

        def ctx_decays(eng, own, z, first, last_level):
            for l in range(first, last_level + 1):
                at = [sum(CTX >> k for k in range(1, m)) for m in range(CTX_LEVELS + 1)]
                total = c_f[:, z, :] if l == 1 else c_T[:, z, at[l - 1]:at[l - 1] + (CTX >> (l - 1))]
                nxt = c_T[:, z, at[l]:at[l] + (CTX >> l)] if l < CTX_LEVELS else None
                own.wait()
                last = grow(eng, own, None, c_kg[:, z, :], total, nxt, 1 << (l - 1), z == 0, CTX)
                if l < last_level:
                    own.did(last)
            return last

        ps = psum("ps", [P, 8, 512])
        ZA, ZB, BF, BB, BD, TR, OB, UB = range(8)

        def bank(b, n=512):
            return ps[:, b, 0:n]

        consts_in = sem("consts_in")
        vec_in = sem("vec_in")
        x_in = [sem(f"x_in{i}") for i in range(3)]
        ada_in = [sem(f"ada_in{i}") for i in range(4)]
        vec_T, vecT_rdy, cs_rdy = sem("vec_T"), sem("vecT_rdy"), sem("cs_rdy")
        c_sg = sem("c_sg")
        ssq_rdy, var_rdy, std_rdy, xn_rdy = sem("ssq_rdy"), sem("var_rdy"), sem("std_rdy"), sem("xn_rdy")
        x_T, xT_act, xT_dve = sem("x_T"), sem("xT_act"), sem("xT_dve")
        ada_mm, mod_0, mod_rdy, mod_rdy_dve, mod_T = sem("ada_mm"), sem("mod_0"), sem("mod_rdy"), sem("mod_rdy_dve"), sem("mod_T")
        lb_exp, lb_in = sem("lb_exp"), sem("lb_in")
        h_rdy, h_hi, h_split = sem("h_rdy"), sem("h_hi"), sem("h_split")
        raw_in = [sem(f"raw_in{i}") for i in range(SLOTS)]
        hi_done, split_done, units_done = sem("hi_done"), sem("split_done"), sem("units_done")
        v_own, a_own, p_own, sp_own = sem("v_own"), sem("a_own"), sem("p_own"), sem("sp_own")
        c_sig_f, c_sig_b, c_v_ev = sem("c_sig_f"), sem("c_sig_b"), sem("c_v_ev")
        c_kg_f, c_kg_b = sem("c_kg_f"), sem("c_kg_b")
        c_v_T, c_kg_T, c_v_rdy, c_kgT_rdy = sem("c_v_T"), sem("c_kg_T"), sem("c_v_rdy"), sem("c_kgT_rdy")
        c_s_mm, ctx_state = sem("c_s_mm"), sem("ctx_state")
        sig_q, q_rdy, sig_f, f_rdy, v_ev, v_T, v_rdy = (sem(s) for s in (
            "sig_q", "q_rdy", "sig_f", "f_rdy", "v_ev", "v_T", "v_rdy"))
        sig_bw, fb_rdy, sig_og, gate_rdy, p_ev, pool_rdy, coef_in = (sem(s) for s in (
            "sig_bw", "fb_rdy", "sig_og", "gate_rdy", "p_ev", "pool_rdy", "coef_in"))
        lv_mm = [sem("lv_mm_f"), sem("lv_mm_b")]
        lv_up = [sem("lv_up_f"), sem("lv_up_b")]
        lv_sel = [sem("lv_sel_f"), sem("lv_sel_b")]
        kg_T = [sem("kg_T_f"), sem("kg_T_b")]
        kgT_rdy = [sem("kgT_f_rdy"), sem("kgT_b_rdy")]
        u_mm = [sem("u_mm_f"), sem("u_mm_b")]
        s_rdy = [sem("s_f_rdy"), sem("s_b_rdy")]
        o_mm = [sem("o_mm_f"), sem("o_mm_b")]
        osq_rdy, n_mm, nv_rdy, rt_rdy, hg_rdy = (sem(s) for s in (
            "osq_rdy", "n_mm", "nv_rdy", "rt_rdy", "hg_rdy"))
        pad_rdy = sem("pad_rdy")
        pg_mm, pg_ev, hgw_rdy = (sem(s) for s in (
            "pg_mm", "pg_ev", "hgw_rdy"))
        gp_rdy, gh_rdy, pp_rdy, m_rdy, row_mm, row_rdy, row_out, b_in = (sem(s) for s in (
            "gp_rdy", "gh_rdy", "pp_rdy", "m_rdy", "row_mm", "row_rdy", "row_out", "b_in"))
        m_in = x_in + ada_in + [sem("m_in7")]
        M_BASE = [32] * 3 + [64] * 4 + [0]
        ada2_in = [sem("ada2_in0"), sem("ada2_in1")]
        ada2_free = sem("ada2_free")
        xp_in, w_ev, x2_rdy = sem("xp_in"), sem("w_ev"), sem("x2_rdy")
        rows_in, h2_rdy, h2_T, sq_done, lg_mm, m4_rdy, inv_rdy, h2_scaled, h2_last = (sem(s) for s in (
            "rows_in", "h2_rdy", "h2_T", "sq_done", "lg_mm", "m4_rdy", "inv_rdy", "h2_scaled", "h2_last"))
        score_rdy, sel_rdy, pos_mm, onehot_rdy, tab_mm, table_rdy = (sem(s) for s in (
            "score_rdy", "sel_rdy", "pos_mm", "onehot_rdy", "tab_mm", "table_rdy"))
        e_in = raw_in + [sem("e_in6"), sem("e_in7")]
        e_hi_done, e_split, e_units = sem("e_hi_done"), sem("e_split"), sem("e_units")
        xe_in, xe_T, xe_hi_rdy, xe_rdy = (sem(s) for s in (
            "xe_in", "xe_T", "xe_hi_rdy", "xe_rdy"))
        sg_rdy, u_rdy, act_rdy, act_T, actT_hi_rdy, actT_rdy = (sem(s) for s in (
            "sg_rdy", "u_rdy", "act_rdy", "act_T", "actT_hi_rdy", "actT_rdy"))
        y_ev, y_out = sem("y_ev"), sem("y_out")
        y_in, f_sum, o_rdy, o_out = (
            [sem(f"y_in{i}") for i in range(NTOK)], sem("f_sum"), sem("o_rdy"), sem("o_out"))

        block = stack.enter_context(nc.Block())

        CTX_PIECES, H_PIECES, M_PIECES = 8, 16, 24
        XT_H2 = 2 * (NTOK + NCTX)
        C_U, H_U = 6, 12
        U_H = HEADS * C_U
        U_M = U_H + HEADS * H_U
        S_W = U_M + KT * 6
        C_TILES = ("ff", "fb", "i")
        H_TILES = ("q", "ff", "i", "fb", "og", "p")

        def split_value(s):
            return SLOTS + s + 1

        E_BASE = [16 * (U_M // SLOTS + KT + 8)] * 4 + [16 * (U_M // SLOTS + KT)] * 2 + [0] * 2

        @block.sync
        def _(sp):
            sp.dma_start(ident[:], consts[:, 0:P]).then_inc(consts_in, 16)
            sp.dma_start(upper[:], consts[:, P:2 * P]).then_inc(consts_in, 16)
            sp.dma_start(iota[:], consts[:, 2 * P:3 * P]).then_inc(consts_in, 16)
            sp.dma_start(tok_ids[:], consts[:, 3 * P:3 * P + NTOK]).then_inc(consts_in, 16)
            sp.dma_start(masks_in[:], level_masks).then_inc(consts_in, 16)
            for v, r in ((c.rearrange("a (r n) -> (a r) n", n=P), V_C),
                         (c_ctx.rearrange("(r n) -> r n", n=P), V_CC),
                         (norm1_w.rearrange("a (r n) -> (a r) n", n=P), V_N1),
                         (b_ada[:, 0:2 * D].rearrange("a (r n) -> (a r) n", n=P), V_B),
                         (pool_scale.rearrange("a (r n) -> (a r) n", n=P), V_PS),
                         (hg_norm_w.rearrange("a (r n) -> (a r) n", n=P), V_HG),
                         (lb_logits.rearrange("z a (r n) -> (z a r) n", n=P), V_LB)):
                sp.dma_start(vec_rows[r:r + v.shape[0], :], v).then_inc(vec_in, 16)

            def load_x(n):
                if n >= 3:
                    sp.wait_ge(x_T, n - 2)
                src = ctx_d[n] if n < NCTX else x_d[n - NCTX]
                sp.dma_start(x_tok[:, n % 3, :], src).then_inc(x_in[n % 3], 16)

            def load_ada(k):
                if k >= 4:
                    sp.wait_ge(ada_mm, k - 3)
                sp.dma_start(ada_ring[:, k % 4, :], w_ada_d[:, k, 0:2 * D]).then_inc(ada_in[k % 4], 16)

            for n in range(3):
                load_x(n)
            for k in range(2):
                load_ada(k)
            for n in range(3, NTOK + NCTX):
                load_x(n)
            for k in range(2, KT):
                load_ada(k)

            def load_unit(slot, src):
                sp.sem_inc(sp_own, 1)
                sp.dma_start(raw[:, slot, :].rearrange("p (k n) -> p k n", k=src.shape[1]), src
                             ).then_inc(raw_in[slot], 16)

            with sp.Fori(0, HEADS) as h:
                for u in range(C_U):
                    col = COL[C_TILES[u // 2]]
                    sp.wait_ge(split_done, h * C_U + u + 1)
                    load_unit(u, w_in_d[:, 8 * (u % 2):8 * (u % 2) + 8, ds(h * P + col, P)])
            with sp.Fori(0, HEADS) as h:
                for u in range(H_U):
                    col = COL[H_TILES[u // 2]]
                    sp.wait_ge(split_done, h * H_U + (U_H + u + 1))
                    load_unit(u % SLOTS, w_in_d[:, 8 * (u % 2):8 * (u % 2) + 8, ds(h * P + col, P)])
            def load_gates(j, u, u0):
                col = COL["gp" if u < 2 else "gh"]
                sp.wait_ge(split_done, u0 + (U_M + 1))
                load_unit(u, w_in_d[:, 8 * (u % 2):8 * (u % 2) + 8, ds(j * P + col, P)])

            def load_branches(j):
                for u, w in ((4, w_bp_d), (5, w_bh_d)):
                    sp.wait_ge(split_done, j * 6 + (U_M + u + 1))
                    load_unit(u, w[:, 0:8, ds(j * P, P)])

            for u in range(4):
                load_gates(0, u, u)
            with sp.Fori(0, KT - 1) as j:
                load_branches(j)
                for u in range(4):
                    load_gates(j + 1, u, j * 6 + (6 + u))
            load_branches(KT - 1)
            sp.wait_ge(units_done, 2 + S_W - 2)
            def load_merged(n, stores):
                sp.wait_ge(row_out, stores)
                sp.dma_start(m_sb[:, 2 * n:2 * n + 2, :], m_d[2 * n:2 * n + 2].rearrange("k p t -> p k t")
                             ).then_inc(m_in[n], 16)
            def load_out(cb, first, end):
                for u in range(first, end):
                    sp.wait_ge(split_done, cb * 8 + (S_W + u + 3))
                    load_unit(u % 4, w_out_d[:, 2 * u:2 * u + 2, ds(cb * 512, 512)])

            for n in range(KT // 2 - 1):
                load_merged(n, 16 + 32 * (KT - 1))
            load_out(0, 0, 4)
            load_merged(KT // 2 - 1, 32 * KT)
            load_out(0, 4, 8)
            with sp.Fori(1, 4) as cb:
                load_out(cb, 0, 8)

            sp.wait_ge(units_done, 2 + S_W + 32)
            sp.wait_ge(h2_rdy, NTOK - 1)
            sp.wait_ge(h2_last, 1)

            def load_e(g, slot, src):
                sp.wait_ge(e_split, g + 1)
                sp.sem_inc(sp_own, 1)
                sp.dma_start(e_raw[:, slot, :].rearrange("p (k n) -> p k n", k=src.shape[1]), src
                             ).then_inc(e_in[slot], 16)

            def w13(w, e, q):
                return w[ds(e, 1), :, 2 * q:2 * q + 2, :].rearrange("o p k n -> (o p) k n")

            def w2(e, q):
                return w_e2_d[ds(e, 1), :, q // 2:q // 2 + 1, 1024 * (q % 2):1024 * (q % 2) + 1024
                              ].rearrange("o p k n -> (o p) k n")

            for q in range(16):
                load_e(q, q % 8, w13(w_e1_d if q < 8 else w_e3_d, 0, q % 8))
            with sp.Fori(1, E) as e:
                for q in range(24):
                    src = w13(w_e1_d, e, q) if q < 8 else w13(w_e3_d, e, q - 8) if q < 16 else w2(e - 1, q - 16)
                    load_e(e * 24 + (q - 8), q % 8, src)
            for q in range(8):
                load_e(E * 24 - 8 + q, q, w2(E - 1, q))
            sp.wait_ge(table_rdy, 1)
            n_extra = sp.value_load(route_i[0:1, 7:8], min_val=0, max_val=NXTRA)
            with sp.Fori(0, NXTRA) as b:
                with sp.If(b < n_extra):
                    e = sp.value_load(route_i[0:1, ds(b, 1)], min_val=0, max_val=E - 1)
                    for q in range(24):
                        src = w13(w_e1_d, e, q) if q < 8 else w13(w_e3_d, e, q - 8) if q < 16 else w2(e, q - 16)
                        load_e(b * 24 + (E * 24 + q), q % 8, src)
                sp.nop()

            for i in range(NTOK):
                sp.wait_ge(o_rdy, i + 1)
                sp.dma_start(out_d[i], o_sb[:, i, :]).then_inc(o_out, 16)
            sp.wait_ge(o_out, 16 * NTOK)

        @block.tensor
        def _(pe):
            mm = pe.matmul
            pe.sem_inc(units_done, 2)
            pe.sem_inc(e_units, 4)
            for s in (u_mm[0], u_mm[1], o_mm[0], row_mm):
                pe.sem_inc(s, 1)

            pe.wait_ge(consts_in, 80)
            pe.wait_ge(vec_in, 7 * 16)
            pe.transpose(bank(BD, V_ROWS), vec_rows[0:V_ROWS, :], ident[0:V_ROWS, 0:V_ROWS]).then_inc(vec_T, 1)
            def turn_x_tiles(r):
                for n in range(r, r + 3):
                    pe.wait_ge(xn_rdy, n + 1)
                    for g in range(4):
                        if n:
                            pe.wait_ge(xT_act if g % 2 == 0 else xT_dve, 2 * (n - 1) + g // 2 + 1)
                        for j in range(4):
                            last = pe.transpose(ps[:, g, j * P:(j + 1) * P],
                                                x_tok[:, n % 3, (4 * g + j) * P:(4 * g + j + 1) * P], ident[:])
                    last.then_inc(x_T, 1)

            def ada_rows(k):
                pe.wait_ge(ada_in[k % 4], 16 * (k // 4 + 1))
                for b in range(8):
                    c0 = 32 * (b % 4)
                    last = mm(ps[c0:c0 + 2, OB + b // 4, :], cs[:, :, k], ada_ring[:, k % 4, b * 512:(b + 1) * 512],
                              start=(k == 0), stop=(k == KT - 1), tile_position=(0, c0))
                last.then_inc(ada_mm, 1)

            pe.wait_ge(cs_rdy, 1)
            ada_rows(0)
            turn_x_tiles(0)
            for k in range(1, 4):
                ada_rows(k)
            turn_x_tiles(3)
            pe.wait_ge(x_T, NTOK + NCTX)
            pe.sem_inc(split_done, SLOTS)
            for k in range(4, KT):
                ada_rows(k)
            for g in range(2):
                pe.wait_ge((mod_rdy, mod_rdy_dve)[g], 1)
                if g == 0:
                    pe.wait_ge(xT_act, 2 * (NTOK + NCTX))
                    pe.wait_ge(xT_dve, 2 * (NTOK + NCTX))
                for j in range(4):
                    last = pe.transpose(ps[:, g, j * P:(j + 1) * P], mod01_row[:, g, j * P:(j + 1) * P], ident[:])
            last.then_inc(mod_T, 1)

            def unit(s, slot, half, rhs_hi, rhs_lo, dst):
                pe.wait_ge(split_done, split_value(s))
                for kk in range(8):
                    k = 8 * half + kk
                    hi, lo = (w[:, slot, kk * P:(kk + 1) * P] for w in (w_hi, w_lo))
                    mm(dst, hi, rhs_hi[:, k, :], start=(k == 0), stop=False)
                    mm(dst, hi, rhs_lo[:, k, :], start=False, stop=False)
                    last = mm(dst, lo, rhs_hi[:, k, :], start=False, stop=(k == KT - 1))
                last.then_inc(units_done, 1)

            pe.wait_ge(h_split, CTX_PIECES // 2)

            def ctx_scan(h, own, lag):
                hd = h - 1
                for u in range(C_U if own else 4):
                    if own:
                        if lag and u % 2 == 0:
                            pe.wait_ge((c_sig_f, c_sig_b, c_v_ev)[u // 2], h)
                        if not lag and u == 1:
                            pe.wait_ge(h_split, CTX_PIECES)
                        unit(h * C_U + u, u % 2, u % 2, hc_hi, hc_lo, bank((ZA, ZB, BF)[u // 2], CTX))
                    if lag and u == 1:
                        pe.wait_ge(c_v_ev, hd + 1)
                        for t in range(NCTX):
                            last = pe.transpose(ps[:, TR, t * P:(t + 1) * P], c_vT[:, t * P:(t + 1) * P], ident[:])
                        last.then_inc(c_v_T, 1)
                        pe.wait_ge(c_kg_f, hd + 1)
                        pe.wait_ge(c_kg_b, hd + 1)
                        for z in range(2):
                            for t in range(NCTX):
                                o = (z * NCTX + t) * P
                                last = pe.transpose(ps[:, UB, o:o + P], c_kg[:, z, t * P:(t + 1) * P], ident[:])
                        last.then_inc(c_kg_T, 1)
                    if lag and u == 3:
                        pe.wait_ge(c_v_rdy, hd + 1)
                        pe.wait_ge(c_kgT_rdy, hd + 1)
                        pe.wait_ge(ctx_state, hd + 1)
                        for z in range(2):
                            for t in range(NCTX):
                                last = mm(ps[:, OB, z * P:(z + 1) * P], c_kgT[:, z, t, :], c_v[:, t, :],
                                          start=(t == 0), stop=(t == NCTX - 1))
                        last.then_inc(c_s_mm, 1)

            ctx_scan(0, True, False)
            with pe.Fori(1, HEADS) as h:
                ctx_scan(h, True, True)
            ctx_scan(HEADS, False, True)

            def readers(a, z, l):
                return a.rearrange("p (n two h) -> p n two h", two=2, h=1 << l)[:, :, 1 - z, :]

            def level(z, hd, idx):
                Bk = BD if idx == 0 else (BF, BB)[z]
                lhs, rhs = KG[z], (q_sb if idx == 0 else QF[z])
                if idx >= 2:
                    pe.wait_ge(lv_up[z], hd * LEVELS + (idx - 1))
                    pe.wait_ge(lv_sel[z], hd * 8 + idx)
                for ch in range(NCH):
                    lhs_ch, rhs_ch = lhs[:, ch * P:(ch + 1) * P], rhs[:, ch * P:(ch + 1) * P]
                    if idx == 0:
                        last = mm(ps[:, Bk, ch * P:(ch + 1) * P], lhs_ch, rhs_ch, start=True, stop=True)
                    else:
                        last = mm(ps[:, Bk, ch * P // 2:(ch + 1) * P // 2], lhs_ch, readers(rhs_ch, z, idx - 1),
                                  start=True, stop=True)
                last.then_inc(lv_mm[z], 1)

            def turn_kg(z, hd):
                pe.wait_ge(lv_up[z], hd * LEVELS + LEVELS)
                for t in range(NCH - 1):
                    ch = t if z == 0 else t + 1
                    last = pe.transpose(ps[:, TR, t * P:(t + 1) * P], KG[z][:, ch * P:(ch + 1) * P], ident[:])
                last.then_inc(kg_T[z], 1)

            def chunk_sums(z, hd):
                pe.wait_ge(kgT_rdy[z], hd + 1)
                for t in range(NCH - 1):
                    ch = t if z == 0 else t + 1
                    last = mm(ps[:, UB, t * P:(t + 1) * P], kgT[z][:, t, :], v_sb[:, ch, :], start=True, stop=True)
                last.then_inc(u_mm[z], 1)

            def outputs(z, hd):
                pe.wait_ge(s_rdy[z], hd + 1)
                pe.wait_ge(lv_sel[z], hd * 8 + 8)
                for ch in range(NCH):
                    o = ps[:, OB, ch * P:(ch + 1) * P]
                    mm(o, v_sb[:, ch, :], A[z][:, ch, :], start=(z == 0 and ch == 0), stop=False,
                       skip_group_check=True)
                    last = mm(o, S[z][:, ch, :], QF[z][:, ch * P:(ch + 1) * P], start=False,
                              stop=(z == 1 and ch == NCH - 1), skip_group_check=True)
                last.then_inc(o_mm[z], 1)

            pe.wait_ge(ctx_state, HEADS + 1)
            pe.wait_ge(h_split, H_PIECES)

            def lat_scan(h, own, lag):
                hd = h - 1
                for u in range(H_U if own else 8):
                    if not own and u < 4:
                        if u % 2 == 0:
                            pe.wait_ge(*((gate_rdy, HEADS), (p_ev, HEADS))[u // 2])
                        unit(U_M + u, u % 2, u % 2, hl_hi, hl_lo, bank((ZA, ZB)[u // 2]))
                    if own:
                        if lag and u % 2 == 0:
                            pe.wait_ge(*((gate_rdy, h), (p_ev, h), (q_rdy, h + 1), (f_rdy, h + 1), (v_ev, h + 1),
                                         (sig_bw, h + 1))[u // 2])
                        elif u % 2 == 0 and u >= 4:
                            pe.wait_ge(*((q_rdy, h + 1), (f_rdy, h + 1), (v_ev, h + 1), (sig_bw, h + 1))[u // 2 - 2])
                        unit(h * H_U + (U_H + u), u % 2, u % 2, hl_hi, hl_lo, bank((ZA, ZB)[u // 2 % 2]))
                        if u == 4:
                            pe.wait_ge(f_rdy, h + 1)
                            if lag:
                                pe.wait_ge(lv_sel[1], hd * 8 + 1)
                            level(0, h, 0)
                            if lag:
                                pe.wait_ge(lv_sel[0], h * 8)
                            level(0, h, 1)
                        if 5 <= u <= 10:
                            level(0, h, u - 3)
                        if u == 7:
                            pe.wait_ge(v_ev, h + 1)
                            if lag:
                                pe.wait_ge(kgT_rdy[1], h)
                            for t in range(NCH):
                                last = pe.transpose(ps[:, TR, t * P:(t + 1) * P], vT_sb[:, t * P:(t + 1) * P],
                                                    ident[:])
                            last.then_inc(v_T, 1)
                        if u == 8:
                            pe.wait_ge(fb_rdy, h + 1)
                            pe.wait_ge(lv_sel[0], h * 8 + 1)
                            level(1, h, 0)
                            if lag:
                                pe.wait_ge(lv_sel[1], h * 8)
                            level(1, h, 1)
                        if 9 <= u <= 11:
                            level(1, h, u - 7)
                        if u == 11:
                            pe.wait_ge(v_rdy, h + 1)
                            turn_kg(0, h)
                    if lag:
                        if u <= 2:
                            level(1, hd, u + 5)
                        if u == 1:
                            pe.wait_ge(hg_rdy, hd + 1)
                            chunk_sums(0, hd)
                        if u == 2:
                            outputs(0, hd)
                        if u == 3:
                            pe.wait_ge(kgT_rdy[0], hd + 1)
                            turn_kg(1, hd)
                        if u == 4:
                            pe.wait_ge(s_rdy[0], hd + 1)
                            chunk_sums(1, hd)
                        if u == 5:
                            outputs(1, hd)
                        if u == 7:
                            pe.wait_ge(osq_rdy, hd + 1)
                            pe.wait_ge(s_rdy[1], hd + 1)
                            mm(bank(UB), ones[:], osq[:], start=True, stop=True).then_inc(n_mm, 1)

            lat_scan(0, True, False)
            with pe.Fori(1, HEADS) as h:
                lat_scan(h, True, True)
            lat_scan(HEADS, False, True)

            pe.wait_ge(pool_rdy, HEADS)
            pe.wait_ge(coef_in, 16 * (HEADS + 1))
            pe.wait_ge(lv_sel[1], HEADS * 8)
            pe.wait_ge(gate_rdy, HEADS)
            pe.wait_ge(p_ev, HEADS)
            for t in range(HEADS):
                g, half = t // 2, t % 2
                if t >= 2:
                    pe.wait_ge(pg_ev, t - 1)
                for k in range(2):
                    last = mm(bank((BF, BB)[t % 2]), w_pg[:, g, k, half * P:(half + 1) * P], delta[:, 2 * g + k, :],
                              start=(k == 0), stop=(k == 1))
                last.then_inc(pg_mm, 1)
            def branches(j):
                pe.wait_ge(m_rdy, j + 1)
                for u, a_hi, a_lo, b, pieces in ((4, poolT_hi, poolT_lo, BF, 4), (5, hg_hi, hg_lo, BB, 8)):
                    pe.wait_ge(h_split, H_PIECES + pieces)
                    pe.wait_ge(split_done, j * 6 + (SLOTS + U_M + u + 1))
                    for k in range(8):
                        hi, lo = (w[:, u % 2, k * P:(k + 1) * P] for w in (w_hi, w_lo))
                        mm(bank(b), hi, a_hi[:, k, :], start=(k == 0), stop=False)
                        mm(bank(b), hi, a_lo[:, k, :], start=False, stop=False)
                        last = mm(bank(b), lo, a_hi[:, k, :], start=False, stop=(k == 7))
                    last.then_inc(units_done, 1)

            def ada_sum(j):
                pe.wait_ge(ada2_free, j * 4 + 6)
                pe.wait_ge(row_rdy, j + 1)
                mm(ps[0:1, UB, :], ones[:, 0:1], acc[:], start=True, stop=True).then_inc(row_mm, 1)

            pe.wait_ge(pg_ev, HEADS)
            with pe.Fori(0, KT - 1) as j:
                branches(j)
                for u in range(4):
                    if u % 2 == 0:
                        pe.wait_ge((gp_rdy, gh_rdy)[u // 2], j + 2)
                    unit(j * 6 + (U_M + 6 + u), u % 2, u % 2, hl_hi, hl_lo, bank((ZA, ZB)[u // 2]))
                ada_sum(j)
            branches(KT - 1)

            def logits(t):
                pe.wait_ge(xT_act, XT_H2 + 2 * t + 2)
                pe.wait_ge(xT_dve, XT_H2 + 2 * t + 2)
                for k in range(KT):
                    last = mm(ps[:, 0, t * E:(t + 1) * E], h2T[:, k, t * P:(t + 1) * P], w_r[:, k, :],
                              start=(k == 0), stop=(k == KT - 1))
                last.then_inc(lg_mm, 1)

            pe.wait_ge(m_rdy, KT + 1)
            def project(cb):
                for u in range(8):
                    s = cb * 8 + (S_W + u)
                    pe.wait_ge(split_done, split_value(s))
                    pe.wait_ge(h_split, M_PIECES + u + 1)
                    for t in range(NTOK):
                        if u == 0:
                            pe.wait_ge(w_ev, cb * 4 + (t + 1))
                        for kk in range(2):
                            k = 2 * u + kk
                            hi, lo = (w[:, u % 2, kk * 512:(kk + 1) * 512] for w in (w_hi, w_lo))
                            a_hi, a_lo = (m[:, k, t * P:(t + 1) * P] for m in (m_hi, m_lo))
                            mm(bank(t), a_hi, hi, start=(k == 0), stop=False)
                            mm(bank(t), a_hi, lo, start=False, stop=False)
                            last = mm(bank(t), a_lo, hi, start=False, stop=(k == KT - 1))
                    last.then_inc(units_done, 1)

            project(0)
            ada_sum(KT - 1)
            with pe.Fori(1, 4) as cb:
                project(cb)

            pe.wait_ge(rows_in, 4 * 16)
            for t in range(NTOK):
                if t == 0:
                    pe.wait_ge(w_ev, 20)
                pe.wait_ge(*((h2_rdy, t + 1) if t < NTOK - 1 else (h2_last, 1)))
                for g in range(4):
                    if t:
                        pe.wait_ge(xT_act if g % 2 == 0 else xT_dve, XT_H2 + 2 * (t - 1) + g // 2 + 1)
                    else:
                        pe.wait_ge(sq_done, 16)
                    for j in range(4):
                        last = pe.transpose(ps[:, 4 + g, j * P:(j + 1) * P],
                                            h2[:, t, (4 * g + j) * P:(4 * g + j + 1) * P], ident[:])
                last.then_inc(h2_T, 1)
                if t:
                    logits(t - 1)
            logits(NTOK - 1)
            pe.wait_ge(sel_rdy, 1)
            chosen = rt[:, 8, :].rearrange("p (t e) -> p t e", e=E)
            for t in range(NTOK):
                for s in range(t + 1):
                    mm(ps[:, 1, t * E:(t + 1) * E], upper[:] if s == t else ones[:], chosen[:, s, :],
                       start=(s == 0), stop=(s == t))
            for s in range(NTOK):
                last = mm(ps[:, 2, 0:E], ones[:], chosen[:, s, :], start=(s == 0), stop=(s == NTOK - 1))
            last.then_inc(pos_mm, 1)
            pe.wait_ge(onehot_rdy, 1)
            for n in range(2 * NTOK):
                last = mm(ps[:, 3, 0:NBLK], slot_1[:, n, :], block_tok[:, n, :], start=(n == 0),
                          stop=(n == 2 * NTOK - 1))
            last.then_inc(tab_mm, 1)
            pe.wait_ge(table_rdy, 1)

            def e_unit(g, slot, parts):
                pe.wait_ge(e_split, g + 9)
                for b, n, a_hi, a_lo, start, stop in parts:
                    hi, lo = (w[:, slot, n * 512:(n + 1) * 512] for w in (e_hi, e_lo))
                    mm(bank(b), a_hi, hi, start=start, stop=False)
                    mm(bank(b), a_hi, lo, start=False, stop=False)
                    last = mm(bank(b), a_lo, hi, start=False, stop=stop)
                last.then_inc(e_units, 1)

            def up_unit(g, q, b):
                e_unit(g, q % 4, [(b, kk, xe_hi[:, 2 * q + kk, :], xe_lo[:, 2 * q + kk, :],
                                   2 * q + kk == 0, 2 * q + kk == KT - 1) for kk in range(2)])

            def down_unit(g, q):
                k = q // 2
                e_unit(g, q % 4, [(2 + 2 * (q % 2) + n, n, actT_hi[:, k, :], actT_lo[:, k, :], k == 0, k == 3)
                                  for n in range(2)])

            def turn_x(b, part):
                if part == 0:
                    pe.wait_ge(xe_in, b * 16 + 16)
                pe.wait_ge(xe_rdy, b * 4 + (part + 1))
                pe.wait_ge(actT_rdy, b + 1)
                for j in range(4):
                    last = pe.transpose(ps[:, 6 + part % 2, j * P:(j + 1) * P],
                                        xe[:, (4 * part + j) * P:(4 * part + j + 1) * P], ident[:])
                last.then_inc(xe_T, 1)

            def turn_act(b):
                pe.wait_ge(act_rdy, b + 1)
                for j in range(4):
                    last = pe.transpose(ps[:, 6, j * P:(j + 1) * P], act[:, j * P:(j + 1) * P], ident[:])
                last.then_inc(act_T, 1)

            def x_ready(b):
                pe.wait_ge(xe_rdy, b * 4 + 6)

            for part in range(4):
                turn_x(0, part)
            x_ready(0)
            for q in range(16):
                up_unit(q, q % 8, q // 8)
            for part in range(4):
                if part == 0:
                    pe.wait_ge(e_units, 4 + 16)
                turn_x(1, part)
            with pe.Fori(1, E) as e:
                x_ready(e)
                for q in range(24):
                    g = e * 24 + (q - 8)
                    if q == 0:
                        pe.wait_ge(u_rdy, e)
                    if q == 8:
                        pe.wait_ge(act_rdy, e)
                    if q == 16:
                        pe.wait_ge(actT_rdy, e + 2)
                        pe.wait_ge(y_ev, e * 4)
                    if q < 16:
                        up_unit(g, q % 8, q // 8)
                    else:
                        down_unit(g, q - 16)
                    if q == 2:
                        turn_act(e - 1)
                    if 17 <= q <= 20:
                        turn_x(e + 1, q - 17)
            x_ready(E)
            turn_act(E - 1)
            pe.wait_ge(actT_rdy, E + 2)
            pe.wait_ge(y_ev, 4 * E)
            for q in range(8):
                down_unit(E * 24 - 8 + q, q)
            n_extra = pe.value_load(route_i[0:1, 7:8], min_val=0, max_val=NXTRA)
            with pe.Fori(0, NXTRA) as b:
                with pe.If(b < n_extra):
                    for part in range(4):
                        turn_x(b + (E + 1), part)
                    x_ready(b + (E + 1))
                    pe.wait_ge(u_rdy, b + E)
                    pe.wait_ge(act_rdy, b + E)
                    for q in range(16):
                        up_unit(b * 24 + (E * 24 + q), q % 8, q // 8)
                    turn_act(b + E)
                    pe.wait_ge(actT_rdy, b + (E + 3))
                    pe.wait_ge(y_ev, b * 4 + 4 * (E + 1))
                    for q in range(8):
                        down_unit(b * 24 + (E * 24 + 16 + q), q)
                pe.nop()

        @block.scalar
        def _(act_e):
            own = Chain(act_e, a_own)
            activate = act_e.activation
            act_e.sem_inc(gp_rdy, 1)
            act_e.sem_inc(gh_rdy, 1)
            act_e.sem_inc(y_ev, 4)

            act_e.wait_ge(vecT_rdy, 1)
            activate(cs[:], vecT[:, 0:2 * KT].rearrange("p (z k) -> p z k", z=2), ACT.Sigmoid).then_inc(c_sg, 1)
            act_e.wait_ge(lb_in, 1)
            activate(lb_tmp[:, 1, :], lb_tmp[:, 0, :], ACT.Exp).then_inc(lb_exp, 1)
            for r in range(0, NTOK + NCTX, 3):
                for n in range(r, r + 3):
                    act_e.wait_ge(x_in[n % 3], 16 * (n // 3 + 1))
                    own.wait()
                    own.did(activate(square_junk[:], x_tok[:, n % 3, :], ACT.Square, accum_out=stat[:, 0, n:n + 1]))
                own.wait()
                act_e.nop().then_inc(ssq_rdy, 1)
                act_e.wait_ge(var_rdy, r // 3 + 1)
                activate(stat[:, 2, r:r + 3], stat[:, 1, r:r + 3], ACT.Sqrt).then_inc(std_rdy, 1)
                for n in range(r, r + 3):
                    act_e.wait_ge(x_T, n + 1)
                    for g in (0, 2):
                        dst = xT_ctx[:, 4 * g:4 * g + 4, n * P:(n + 1) * P] if n < NCTX else \
                            xT_lat[:, 4 * g:4 * g + 4, (n - NCTX) * P:(n - NCTX + 1) * P]
                        act_e.copy(dst, bank(g).rearrange("p (j t) -> p j t", j=4)).then_inc(xT_act, 1)
            def hi(s, slot, hslot, uses):
                act_e.wait_ge(raw_in[slot], uses)
                act_e.wait_ge(units_done, s + 1)
                act_e.copy(w_hi[:, hslot, :], raw[:, slot, :]).then_inc(hi_done, 1)

            act_e.wait_ge(split_done, SLOTS)
            hi(0, 0, 0, 16)
            act_e.wait_ge(ada_mm, KT)
            act_e.wait_ge(mod_0, 1)
            for q in range(4):
                last = act_e.copy(mod01_row[32 * q:32 * q + 2, 0, :], ps[32 * q:32 * q + 2, OB, :])
            last.then_inc(mod_rdy, 1)
            for n in range(CTX_PIECES):
                act_e.wait_ge(h_rdy, n + 1)
                act_e.copy(hc_hi[:, 2 * n:2 * n + 2, :], xT_ctx[:, 2 * n:2 * n + 2, :]).then_inc(h_hi, 1)

            def ctx_scan(h, main, lag):
                hd = h - 1
                for u in range(C_U if main else 4):
                    if main:
                        hi(h * C_U + (u + 1), (u + 1) % SLOTS, (u + 1) % 2, h * 16 + 16 * ((u + 1) // SLOTS + 1))
                        done = h * C_U + (2 + u + 1)
                        if u == 1:
                            act_e.wait_ge(units_done, done)
                            if lag:
                                act_e.wait_ge(c_kg_f, h)
                            activate(c_sig[:, 0, :], bank(ZA, CTX), ACT.Sigmoid).then_inc(c_sig_f, 1)
                        if u == 3:
                            act_e.wait_ge(units_done, done)
                            if lag:
                                act_e.wait_ge(c_kg_b, h)
                            activate(c_sig[:, 1, :], bank(ZB, CTX), ACT.Sigmoid).then_inc(c_sig_b, 1)
                        if u == 5:
                            act_e.wait_ge(units_done, done)
                            if lag:
                                act_e.wait_ge(c_v_T, h)
                            act_e.copy(c_vT[:], bank(BF, CTX)).then_inc(c_v_ev, 1)
                    if main and u == 4:
                        act_e.wait_ge(h_rdy, h + (CTX_PIECES + 1))
                        act_e.copy(hl_hi[:, ds(2 * h, 2), :], xT_lat[:, ds(2 * h, 2), :]).then_inc(h_hi, 1)
                    if lag and u == 2:
                        act_e.wait_ge(ctx_state, hd + 1)
                        act_e.wait_ge(c_v_T, hd + 1)
                        act_e.copy(c_v[:].rearrange("p t v -> p (t v)"), bank(TR, CTX)).then_inc(c_v_rdy, 1)
                        act_e.wait_ge(c_kg_T, hd + 1)
                        act_e.copy(c_kgT[:].rearrange("p z t k -> p (z t k)"), bank(UB)).then_inc(c_kgT_rdy, 1)

            ctx_scan(0, True, False)
            with act_e.Fori(1, HEADS) as h:
                ctx_scan(h, True, True)
            ctx_scan(HEADS, False, True)

            act_e.wait_ge(ctx_state, HEADS + 1)
            act_e.wait_ge(pad_rdy, 1)

            def kgT_copy(z, hd):
                act_e.wait_ge(kg_T[z], hd + 1)
                act_e.wait_ge(u_mm[z], hd + 1)
                act_e.copy(kgT[z][:].rearrange("p t k -> p (t k)"), bank(TR, (NCH - 1) * P)).then_inc(kgT_rdy[z], 1)

            def lat_scan(h, main, lag):
                hd = h - 1
                for u in range(H_U if main else 9):
                    if main:
                        hi(h * H_U + (U_H + u + 1), (u + 1) % SLOTS, (u + 1) % 2,
                           h * 32 + 16 * (U_H // SLOTS + (u + 1) // SLOTS + 1))
                        done = h * H_U + (2 + U_H + u + 1)
                        if u == 1:
                            act_e.wait_ge(units_done, done)
                            if lag:
                                act_e.wait_ge(gate_rdy, h)
                            activate(sig_a[:], bank(ZA), ACT.Sigmoid).then_inc(sig_q, 1)
                        if u == 3:
                            act_e.wait_ge(units_done, done)
                            act_e.wait_ge(q_rdy, h + 1)
                            activate(sig_a[:], bank(ZB), ACT.Sigmoid).then_inc(sig_f, 1)
                        if u == 5:
                            act_e.wait_ge(units_done, done)
                            if lag:
                                act_e.wait_ge(v_T, h)
                            act_e.copy(vT_sb[:], bank(ZA)).then_inc(v_ev, 1)
                        if u == 7:
                            act_e.wait_ge(units_done, done)
                            if lag:
                                act_e.wait_ge(fb_rdy, h)
                            activate(sig_b[:], bank(ZB), ACT.Sigmoid).then_inc(sig_bw, 1)
                            act_e.wait_ge(v_T, h + 1)
                            if lag:
                                act_e.wait_ge(o_mm[1], h)
                            act_e.copy(v_sb[:].rearrange("p t v -> p (t v)"), bank(TR)).then_inc(v_rdy, 1)
                        if u == 9:
                            act_e.wait_ge(units_done, done)
                            act_e.wait_ge(f_rdy, h + 1)
                            activate(sig_a[:], bank(ZA), ACT.Sigmoid).then_inc(sig_og, 1)
                        if u == 11:
                            act_e.wait_ge(units_done, done)
                            if lag:
                                act_e.wait_ge(pool_rdy, h)
                            act_e.copy(up[:, :, HALO:HALO + GRID_W], bank(ZB).rearrange("p (r w) -> p r w", w=GRID_W)
                                       ).then_inc(p_ev, 1)
                    elif u < 4:
                        hi(U_M + u + 1, u + 1, (u + 1) % 2, 16 * (U_M // SLOTS + 1))
                    if lag:
                        if u == 0:
                            kgT_copy(0, hd)
                        if u == 3:
                            kgT_copy(1, hd)
                        if u == 5:
                            act_e.wait_ge(o_mm[1], hd + 1)
                            act_e.wait_ge(hg_rdy, hd + 1)
                            activate(osq[:], bank(OB), ACT.Square).then_inc(osq_rdy, 1)
                        if u == 8:
                            act_e.wait_ge(nv_rdy, hd + 1)
                            activate(osq[:], osq[:], ACT.Sqrt).then_inc(rt_rdy, 1)

            lat_scan(0, True, False)
            with act_e.Fori(1, HEADS) as h:
                lat_scan(h, True, True)
            lat_scan(HEADS, False, True)

            def gates(j, units, which):
                act_e.wait_ge(units_done, units)
                if which == 0:
                    act_e.wait_ge(pp_rdy, j + 1)
                    activate(sig_gp[:], bank(ZA), ACT.Sigmoid).then_inc(gp_rdy, 1)
                else:
                    act_e.wait_ge(m_rdy, j + 1)
                    activate(sig_gh[:], bank(ZB), ACT.Sigmoid).then_inc(gh_rdy, 1)

            act_e.wait_ge(s_rdy[1], HEADS)
            gates(0, 2 + U_M + 2, 0)
            gates(0, 2 + U_M + 4, 1)
            for t in range(HEADS):
                act_e.wait_ge(pg_mm, t + 1)
                if t == HEADS - 1:
                    act_e.wait_ge(hg_rdy, HEADS + 1)
                activate(poolT[:, t, :], bank((BF, BB)[t % 2]), ACT.Copy, scale=vecT[:, V_PS + t:V_PS + t + 1]
                         ).then_inc(pg_ev, 1)
            act_e.wait_ge(pg_ev, HEADS)
            for n in range(8):
                if n == 4:
                    act_e.wait_ge(hgw_rdy, 1)
                dst, src = ((poolT_hi, poolT), (hg_hi, hg))[n // 4]
                k = 2 * (n % 4)
                act_e.copy(dst[:, k:k + 2, :], src[:, k:k + 2, :]).then_inc(h_hi, 1)

            with act_e.Fori(0, KT - 1) as j:
                for i in range(6):
                    u = 5 + i
                    hi(j * 6 + (U_M + u), u % 6, u % 2, j * 16 + 16 * (U_M // SLOTS + u // 6 + 1))
                    if i == 3:
                        gates(j + 1, j * 6 + (2 + U_M + 8), 0)
                    if i == 5:
                        gates(j + 1, j * 6 + (2 + U_M + 10), 1)
            hi(S_W - 1, 5, 1, 16 * (S_W // SLOTS))
            hi(S_W, 0, 0, 16 * (S_W // SLOTS + 1))

            def merged_hi(n):
                act_e.wait_ge(m_in[n], M_BASE[n] + 16)
                act_e.copy(m_hi[:, 2 * n:2 * n + 2, :], m_sb[:, 2 * n:2 * n + 2, :]).then_inc(h_hi, 1)

            def out_hi(cb, first, last):
                for u in range(7 if last else 8):
                    nxt = u + 1
                    hi(cb * 8 + (S_W + nxt), nxt % 4, nxt % 2,
                       cb * 32 + 16 * ((U_M + 6 * KT) // SLOTS + nxt // 4 + 1))
                    if first and nxt < 8:
                        merged_hi(nxt)

            def squares(cb):
                for t in range(NTOK):
                    act_e.wait_ge(x2_rdy, cb * 4 + (4 + t + 1))
                    own.wait()
                    cols, one = (slice(cb * 512, cb * 512 + 512), slice(cb, cb + 1)) if isinstance(cb, int) else (
                        ds(cb * 512, 512), ds(cb, 1))
                    own.did(activate(bank(4 + t % 3), x2[:, t, cols], ACT.Square, accum_out=part_sq[:, t, one]))

            merged_hi(0)
            out_hi(0, True, False)
            squares(0)
            with act_e.Fori(1, 3) as cb:
                own.loop(cb - 1, NTOK)
                out_hi(cb, False, False)
                squares(cb)
                own.end(2)
            out_hi(3, False, True)
            squares(3)

            own.wait()
            act_e.sem_inc(sq_done, 16)
            act_e.wait_ge(var_rdy, 2 + 1)
            activate(stat2[:, 2, :], stat2[:, 1, :], ACT.Sqrt).then_inc(std_rdy, 1)
            act_e.wait_ge(inv_rdy, 1)
            activate(h2[:, NTOK - 1, :], x2[:, NTOK - 1, :], ACT.Copy, scale=stat2[:, 3, NTOK - 1:NTOK]
                     ).then_inc(h2_scaled, 1)
            for t in range(NTOK):
                act_e.wait_ge(h2_T, t + 1)
                for g in (0, 2):
                    act_e.copy(h2T[:, 4 * g:4 * g + 4, t * P:(t + 1) * P],
                               bank(4 + g).rearrange("p (j t) -> p j t", j=4)).then_inc(xT_act, 1)
            act_e.wait_ge(lg_mm, NTOK)
            activate(rt[:, 0, :], bank(0, NTOK * E), ACT.Sigmoid).then_inc(score_rdy, 1)

            def e_hi_unit(g, slot, hslot, uses):
                act_e.wait_ge(e_in[slot], uses + E_BASE[slot])
                act_e.wait_ge(e_units, g + 1)
                act_e.copy(e_hi[:, hslot, :], e_raw[:, slot, :]).then_inc(e_hi_done, 1)

            def x_hi(b, part):
                act_e.wait_ge(xe_T, b * 4 + (part + 1))
                act_e.copy(xe_hi[:, 4 * part:4 * part + 4, :].rearrange("p k t -> p (k t)"), bank(6 + part % 2)
                           ).then_inc(xe_hi_rdy, 1)

            def sig1(b):
                act_e.wait_ge(u_rdy, b)
                activate(act_sig[:], bank(0), ACT.Sigmoid).then_inc(sg_rdy, 1)

            def act_hi(b):
                act_e.wait_ge(act_T, b + 1)
                act_e.copy(actT_hi[:].rearrange("p k t -> p (k t)"), bank(6)).then_inc(actT_hi_rdy, 1)

            def y_copy(b, units):
                act_e.wait_ge(e_units, units)
                act_e.wait_ge(y_out, b * 32 + 16 * NTOK)
                for part in range(4):
                    act_e.copy(y_sb[:, part * 512:(part + 1) * 512], bank(2 + part)).then_inc(y_ev, 1)

            AHEAD = 3
            act_e.wait_ge(table_rdy, 1)
            for q in range(AHEAD):
                e_hi_unit(q, q, q, 16)
            for part in range(4):
                x_hi(0, part)
            for q in range(16):
                n = q + AHEAD
                e_hi_unit(n, n % 8, n % 4, 16 * (n // 8 + 1))
                if q == 8:
                    act_e.wait_ge(e_units, 4 + 8)
                    activate(act_sig[:], bank(0), ACT.Sigmoid).then_inc(sg_rdy, 1)
            act_e.wait_ge(e_units, 4 + 16)
            for part in range(4):
                x_hi(1, part)
            with act_e.Fori(1, E) as e:
                for q in range(24):
                    n = q + AHEAD
                    e_hi_unit(e * 24 + (n - 8), n % 8, n % 4, e * 48 + 16 * (n // 8))
                    if q == 3:
                        act_hi(e - 1)
                    if q == 9:
                        act_e.wait_ge(e_units, e * 24 + 4)
                        sig1(e)
                    if q == 17:
                        act_e.wait_ge(e_units, e * 24 + 12)
                    if 18 <= q <= 21:
                        x_hi(e + 1, q - 18)
                y_copy(e - 1, e * 24 + 20)
            act_hi(E - 1)
            for q in range(AHEAD, 8):
                n = E * 24 - 8 + q
                e_hi_unit(n, n % 8, n % 4, 16 * (n // 8 + 1))
            y_copy(E - 1, E * 24 + 4)
            n_extra = act_e.value_load(route_i[0:1, 7:8], min_val=0, max_val=NXTRA)
            with act_e.Fori(0, NXTRA) as b:
                with act_e.If(b < n_extra):
                    for part in range(4):
                        x_hi(b + (E + 1), part)
                    for q in range(24):
                        e_hi_unit(b * 24 + (24 * E + q), q % 8, q % 4, b * 48 + 16 * (3 * E + q // 8 + 1))
                        if q == 10:
                            act_e.wait_ge(e_units, b * 24 + (24 * E + 12))
                            sig1(b + E)
                        if q == 16:
                            act_hi(b + E)
                    y_copy(b + E, b * 24 + (E * 24 + 28))
                act_e.nop()

            for i in range(NTOK):
                act_e.wait_ge(f_sum, i + 1)
                own.wait()
                own.did(activate(f_junk[:], o_sb[:, i, :], ACT.Square, accum_out=stat2[:, 0, i:i + 1]))
                own.wait()
                act_e.nop().then_inc(ssq_rdy, 1)
                act_e.wait_ge(var_rdy, 3 + i + 1)
                activate(stat2[:, 2, i:i + 1], stat2[:, 1, i:i + 1], ACT.Sqrt).then_inc(std_rdy, 1)

        @block.vector
        def _(dve):
            own = Chain(dve, v_own)
            tt, ts, stt = dve.tensor_tensor, dve.tensor_scalar, dve.scalar_tensor_tensor
            for s, n in ((ctx_state, 1), (hg_rdy, 1), (pp_rdy, 1), (m_rdy, 1), (row_rdy, 1), (ada2_free, 2),
                         (w_ev, 4), (x2_rdy, 4), (m4_rdy, 1), (e_split, 8), (xe_rdy, 2), (actT_rdy, 2)):
                dve.sem_inc(s, n)

            own.did(dve.memset(ones[:], 1.0))
            dve.memset(mod01_row[:], 0.0).then_inc(mod_0, 1)
            dve.wait_ge(consts_in, 80)
            own.did(dve.tensor_copy(masks[:], masks_in[:]))
            dve.wait_ge(vec_T, 1)
            dve.tensor_copy(vecT[:], bank(BD, V_ROWS)).then_inc(vecT_rdy, 1)
            dve.wait_ge(vecT_rdy, 1)
            dve.wait_ge(c_sg, 1)
            tt(cs[:], vecT[:, 0:2 * KT].rearrange("p (z k) -> p z k", z=2), cs[:], ALU.mult).then_inc(cs_rdy, 1)
            lb = vecT[:, V_LB:V_LB + 16]
            tt(lb_tmp[:, 0, :], lb, lb, ALU.subtract).then_inc(lb_in, 1)
            dve.wait_ge(lb_exp, 1)
            own.did(dve.reciprocal(lb_tmp[:, 2, :], lb_tmp[:, 1, :]))
            own.wait()
            own.did(tt(lb_tmp[:, 3, :], lb_tmp[:, 1, :], lb_tmp[:, 2, :], ALU.mult))
            own.wait()
            prob = lb_tmp[:, 3, :].rearrange("p (z h) -> p z h", z=2)
            lbv = lb_all[:].rearrange("p h (z w) -> p w z h", z=2)
            own.did(tt(lbv[:, 0], prob, prob, ALU.subtract))
            own.wait()
            own.did(ts(lbv[:, 1], lbv[:, 0], -1.0, 1.0, ALU.mult, ALU.add))
            for r in range(0, NTOK + NCTX, 3):
                dve.wait_ge(ssq_rdy, r // 3 + 1)
                ts(stat[:, 1, r:r + 3], stat[:, 0, r:r + 3], 1.0 / D, EPS, ALU.mult, ALU.add).then_inc(var_rdy, 1)
                dve.wait_ge(std_rdy, r // 3 + 1)
                own.did(dve.reciprocal(stat[:, 3, r:r + 3], stat[:, 2, r:r + 3]))
                own.wait()
                for n in range(r, r + 3):
                    ts(x_tok[:, n % 3, :], x_tok[:, n % 3, :], stat[:, 3, n:n + 1], None, ALU.mult).then_inc(xn_rdy, 1)
                for n in range(r, r + 3):
                    dve.wait_ge(x_T, n + 1)
                    for g in (1, 3):
                        dst = xT_ctx[:, 4 * g:4 * g + 4, n * P:(n + 1) * P] if n < NCTX else \
                            xT_lat[:, 4 * g:4 * g + 4, (n - NCTX) * P:(n - NCTX + 1) * P]
                        dve.tensor_copy(dst, bank(g).rearrange("p (j t) -> p j t", j=4)).then_inc(xT_dve, 1)
            def lo(s, slot, hslot):
                dve.wait_ge(hi_done, s + 1)
                tt(w_lo[:, hslot, :], raw[:, slot, :], w_hi[:, hslot, :].bitcast(F32), ALU.subtract
                   ).then_inc(split_done, 1)

            lo(0, 0, 0)
            dve.wait_ge(ada_mm, KT)
            dve.wait_ge(mod_0, 1)
            for q in range(4):
                last = dve.tensor_copy(mod01_row[32 * q:32 * q + 2, 1, :], ps[32 * q:32 * q + 2, UB, :])
            last.then_inc(mod_rdy_dve, 1)
            dve.wait_ge(mod_T, 1)
            for g in range(2):
                own.did(tt(modT[:, KT * g:KT * g + KT, :].rearrange("p (c j) z -> p c j z", c=4),
                           ps[:, g, :].rearrange("p (j c r) -> p c j r", j=4, c=4)[:, :, :, 0:2],
                           vecT[:, V_B + KT * g:V_B + KT * g + KT].rearrange("p (c j) -> p c j", c=4)
                           .unsqueeze(3).to_broadcast([P, 4, 4, 2]), ALU.add))
            own.wait()
            own.did(stt(out=scale1[:], in0=modT[:, KT:2 * KT, :], scalar=1.0,
                        in1=vecT[:, V_N1:V_N1 + KT].unsqueeze(2).to_broadcast([P, KT, 2]),
                        op0=ALU.add, op1=ALU.mult))
            own.wait()
            dve.wait_ge(xT_act, 2 * (NTOK + NCTX))
            dve.wait_ge(xT_dve, 2 * (NTOK + NCTX))

            def modulate(xT, n, z):
                for j in (2 * n, 2 * n + 1):
                    last = ts(xT[:, j, :], xT[:, j, :], scale1[:, j, z:z + 1], modT[:, j, z:z + 1],
                              ALU.mult, ALU.add)
                last.then_inc(h_rdy, 1)

            def ctx_lo(n):
                dve.wait_ge(h_hi, n + 1)
                dst, hi_, src = (a[:, 2 * n:2 * n + 2, :] for a in (hc_lo, hc_hi, xT_ctx))
                tt(dst, src, hi_.bitcast(F32), ALU.subtract).then_inc(h_split, 1)

            for n in range(CTX_PIECES):
                modulate(xT_ctx, n, 1)
                if n:
                    ctx_lo(n - 1)
            ctx_lo(CTX_PIECES - 1)

            for n in range(KT // 2):
                modulate(xT_lat, n, 0)

            def ctx_scan(h, main, lag):
                hd = h - 1
                for u in range(C_U if main else 4):
                    if main:
                        lo(h * C_U + (u + 1), (u + 1) % SLOTS, (u + 1) % 2)
                        if u == 1:
                            own.wait()
                            own.did(dve.tensor_copy(lb_v[:], lb_all[:, ds(h, 1), :].rearrange("p o w -> p (o w)")))
                            own.wait()
                            dve.wait_ge(c_sig_f, h + 1)
                            if lag:
                                dve.wait_ge(c_kg_T, h)
                                dve.wait_ge(c_kg_f, h)
                            own.did(ts(c_f[:, 0, :], c_sig[:, 0, :], lb_v[:, 1:2], lb_v[:, 0:1], ALU.mult, ALU.add))
                            own.wait()
                            own.did(ts(c_kg[:, 0, :], c_f[:, 0, :], -1.0, 1.0, ALU.mult, ALU.add))
                        if 2 <= u <= 4:
                            ins = ctx_decays(dve, own, 0, *((1, 2), (3, 5), (6, 8))[u - 2])
                            if u == 4:
                                ins.then_inc(c_kg_f, 1)
                            else:
                                own.did(ins)
                        if u == 5:
                            dve.wait_ge(h_hi, h + (CTX_PIECES + 1))
                            tt(hl_lo[:, ds(2 * h, 2), :], xT_lat[:, ds(2 * h, 2), :],
                               hl_hi[:, ds(2 * h, 2), :].bitcast(F32), ALU.subtract).then_inc(h_split, 1)
                    if lag and u == 3:
                        dve.wait_ge(c_s_mm, hd + 1)
                        dve.tensor_copy(s_ctx[:, :, ds(hd, 1), :],
                                        bank(OB, 2 * P).rearrange("p (z o v) -> p z o v", z=2, o=1)
                                        ).then_inc(ctx_state, 1)

            ctx_scan(0, True, False)
            with dve.Fori(1, HEADS) as h:
                own.loop(h - 1, PER["ctx_v"])
                ctx_scan(h, True, True)
                own.end(HEADS - 1)
            ctx_scan(HEADS, False, True)

            def select(z, hd, idx):
                dve.wait_ge(lv_mm[z], hd * 8 + (idx + 1))
                if idx == 0:
                    tt(A[z][:], bank(BD).rearrange("p (c t) -> p c t", c=NCH),
                       ident[:].unsqueeze(1).to_broadcast([P, NCH, P]), ALU.mult).then_inc(lv_sel[z], 1)
                else:
                    dve.wait_ge(lv_sel[z], hd * 8 + idx)
                    own.pass_waits()
                    half = 1 << (idx - 1)
                    n = P // (2 * half)
                    dve.copy_predicated(
                        A[z][:].rearrange("p c (n two h) -> p c n two h", two=2, h=half)[:, :, :, 1 - z, :],
                        masks[:, z, idx - 1, :].rearrange("p (n h) -> p n h", h=half).unsqueeze(1)
                        .to_broadcast([P, NCH, n, half]),
                        bank((BF, BB)[z], SEQ // 2).rearrange("p (c n h) -> p c n h", c=NCH, h=half)
                        ).then_inc(lv_sel[z], 1)

            def states(z, hd):
                order = range(NCH) if z == 0 else range(NCH - 1, -1, -1)
                dve.wait_ge(u_mm[z], hd + 2)
                if z == 0:
                    dve.wait_ge(o_mm[0], hd + 1)
                T_chunk = TT[z][:, T_AT[LEVELS]:T_AT[LEVELS] + NCH]
                prev = order[0]
                dve.wait_ge(ctx_state, HEADS + 1)
                own.did(dve.tensor_copy(S[z][:, prev, :], s_ctx[:, z, ds(hd, 1), :].rearrange("p o v -> p (o v)")))
                for n, ch in enumerate(order[1:]):
                    own.wait()
                    t = prev if z == 0 else prev - 1
                    ins = stt(out=S[z][:, ch, :], in0=S[z][:, prev, :], scalar=T_chunk[:, prev:prev + 1],
                              in1=ps[:, UB, t * P:(t + 1) * P], op0=ALU.mult, op1=ALU.add)
                    if n < NCH - 2:
                        own.did(ins)
                    else:
                        ins.then_inc(s_rdy[z], 1)
                    prev = ch

            def lat_scan(h, main, lag):
                hd = h - 1
                for u in range(H_U if main else 11):
                    if main:
                        lo(h * H_U + (U_H + u + 1), (u + 1) % SLOTS, (u + 1) % 2)
                        if u == 1:
                            dve.wait_ge(sig_q, h + 1)
                            if lag:
                                dve.wait_ge(fb_rdy, h)
                            tt(q_sb[:], bank(ZA), sig_a[:], ALU.mult).then_inc(q_rdy, 1)
                        if u == 3:
                            own.wait()
                            own.did(dve.tensor_copy(lb_v[:], lb_all[:, ds(h, 1), :].rearrange("p o w -> p (o w)")))
                            own.wait()
                            dve.wait_ge(sig_f, h + 1)
                            own.did(ts(f_sb[0][:], sig_a[:], lb_v[:, 1:2], lb_v[:, 0:1], ALU.mult, ALU.add))
                            if lag:
                                dve.wait_ge(o_mm[0], h + 1)
                                dve.wait_ge(lv_up[0], h * LEVELS)
                            own.wait()
                            own.did(ts(KG[0][:], f_sb[0][:], -1.0, 1.0, ALU.mult, ALU.add))
                            dve.wait_ge(q_rdy, h + 1)
                            tt(QF[0][:], q_sb[:], f_sb[0][:], ALU.mult).then_inc(f_rdy, 1)
                        if 4 <= u <= 10:
                            if u == 4:
                                if lag:
                                    dve.wait_ge(lv_sel[0], h * 8)
                                select(0, h, 0)
                            select(0, h, u - 3)
                            l = u - 3
                            own.wait()
                            dve.wait_ge(f_rdy, h + 1)
                            if l > 1:
                                dve.wait_ge(lv_up[0], h * LEVELS + (l - 1))
                            grow(dve, own, QF[0][:], KG[0][:], level_T(0, l - 1), level_T(0, l), 1 << (l - 1), True,
                                 SEQ).then_inc(lv_up[0], 1)
                        if u == 8:
                            if lag:
                                dve.wait_ge(o_mm[1], h)
                                dve.wait_ge(lv_sel[1], h * 8)
                            select(1, h, 0)
                            select(1, h, 1)
                        if u >= 9:
                            select(1, h, u - 7)
                    elif u < 4:
                        lo(U_M + u + 1, u + 1, (u + 1) % 2)
                    if lag:
                        if u <= 2:
                            select(1, hd, u + 5)
                        if u == 1:
                            states(0, hd)
                        if u == 4:
                            states(1, hd)
                        if u == 8:
                            dve.wait_ge(n_mm, hd + 1)
                            ts(osq[:], bank(UB), 1.0 / P, EPS, ALU.mult, ALU.add).then_inc(nv_rdy, 1)
                        if u == 9:
                            dve.wait_ge(rt_rdy, hd + 1)
                            own.did(dve.reciprocal(osq[:], osq[:]))
                        if u == 10:
                            own.wait()
                            own.did(tt(osq[:], bank(OB), osq[:], ALU.mult))
                            own.wait()
                            dve.wait_ge(gate_rdy, hd + 1)
                            tt(hg[:, ds(hd, 1), :], osq[:].unsqueeze(1), gate_sb[:].unsqueeze(1), ALU.mult
                               ).then_inc(hg_rdy, 1)
                    if main and u == 10:
                        dve.wait_ge(sig_og, h + 1)
                        if lag:
                            dve.wait_ge(hg_rdy, h + 1)
                        tt(gate_sb[:], bank(ZA), sig_a[:], ALU.mult).then_inc(gate_rdy, 1)

            lat_scan(0, True, False)
            with dve.Fori(1, HEADS) as h:
                own.loop(h - 1, PER["lat_v"])
                lat_scan(h, True, True)
                own.end(HEADS - 1)
            lat_scan(HEADS, False, True)
            dve.wait_ge(hg_rdy, HEADS + 1)
            for hd in range(HEADS):
                last = ts(hg[:, hd, :], hg[:, hd, :], vecT[:, V_HG + hd:V_HG + hd + 1], None, ALU.mult)
            last.then_inc(hgw_rdy, 1)

            for n in range(8):
                dve.wait_ge(h_hi, H_PIECES + n + 1)
                dst, src, hi_ = ((poolT_lo, poolT, poolT_hi), (hg_lo, hg, hg_hi))[n // 4]
                k = 2 * (n % 4)
                tt(dst[:, k:k + 2, :], src[:, k:k + 2, :], hi_[:, k:k + 2, :].bitcast(F32), ALU.subtract
                   ).then_inc(h_split, 1)

            def ada_step(j, i):
                dve.wait_ge(ada2_in[i % 2], j * 32 + 16 * (i // 2 + 1))
                for kk in range(4):
                    k = 4 * i + kk
                    w = ada2[:, i % 2, kk, :]
                    if k == 0:
                        dve.wait_ge(row_mm, j + 1)
                        dve.wait_ge(ada2_free, j * 4 + 2)
                        ins = ts(acc[:], w, cs[:, 0, 0:1], None, ALU.mult)
                    else:
                        own.wait()
                        if kk == 0:
                            dve.wait_ge(ada2_free, j * 4 + (i + 2))
                        ins = stt(out=acc[:], in0=w, scalar=cs[:, 0, k:k + 1], in1=acc[:], op0=ALU.mult,
                                  op1=ALU.add)
                    if kk < 3:
                        own.did(ins)
                    else:
                        ins.then_inc(ada2_free, 1)

            def ada_row(j):
                dve.wait_ge(row_mm, j + 2)
                dve.wait_ge(b_in, j * 16 + 16)
                tt(mod_row[0:1, :], ps[0:1, UB, :], b_row[0:1, :], ALU.add).then_inc(row_rdy, 1)

            def merge(j, last):
                for i in range(3 if last else 6):
                    u = 5 + i
                    if last and i < 2:
                        lo(S_W - 1 + i, 5 * (1 - i), (1 + i) % 2)
                    elif not last:
                        lo(j * 6 + (U_M + u), u % 6, u % 2)
                    if i < 4 and not last:
                        ada_step(j, i)
                    if i == 1:
                        dve.wait_ge(units_done, j * 6 + (2 + U_M + 5))
                        dve.wait_ge(gp_rdy, j + 2)
                        dve.wait_ge(m_rdy, j + 1)
                        tt(part_p[:], bank(BF), sig_gp[:], ALU.mult).then_inc(pp_rdy, 1)
                    if i == 2:
                        dve.wait_ge(units_done, j * 6 + (2 + U_M + 6))
                        dve.wait_ge(gh_rdy, j + 2)
                        dve.wait_ge(row_out, j * 32 + 16)
                        own.did(tt(m_row[:], bank(BB), sig_gh[:], ALU.mult))
                        own.wait()
                        dve.wait_ge(pp_rdy, j + 2)
                        tt(m_row[:], m_row[:], part_p[:], ALU.add).then_inc(m_rdy, 1)
                if not last:
                    ada_row(j)

            with dve.Fori(0, KT - 1) as j:
                own.loop(j, PER["merge_v"])
                merge(j, False)
                own.end(KT - 1)
            merge(KT - 1, True)

            def merged_lo(n):
                dve.wait_ge(h_hi, M_PIECES + n + 1)
                tt(m_lo[:, 2 * n:2 * n + 2, :], m_sb[:, 2 * n:2 * n + 2, :],
                   m_hi[:, 2 * n:2 * n + 2, :].bitcast(F32), ALU.subtract).then_inc(h_split, 1)

            def project(cb, first, last):
                for u in range(7 if last else 8):
                    nxt = u + 1
                    lo(cb * 8 + (S_W + nxt), nxt % 4, nxt % 2)
                    if first and nxt < 8:
                        merged_lo(nxt)
                    if first and u < 4:
                        ada_step(KT - 1, u)
                dve.wait_ge(units_done, cb * 8 + (2 + S_W + 8))
                dve.wait_ge(xp_in, cb * 48 + 48)
                at = (lambda n: slice(cb * n, cb * n + n)) if isinstance(cb, int) else (lambda n: ds(cb * n, n))
                for t in range(NTOK):
                    tt(x2[:, t, at(512)], bank(t), m2_part[:], ALU.mult).then_inc(w_ev, 1)
                for t in range(NTOK):
                    dve.wait_ge(w_ev, cb * 4 + (4 + t + 1))
                    o = x2[:, t, at(512)]
                    tt(o, o, x_part[:, t, :], ALU.add).then_inc(x2_rdy, 1)
                dve.wait_ge(rows_in, 4 * 16)
                m4 = m4_row[:, at(512)]
                stt(out=m4, in0=m4, scalar=1.0, in1=n2_part[:], op0=ALU.add, op1=ALU.mult).then_inc(m4_rdy, 1)

            merged_lo(0)
            project(0, True, False)
            ada_row(KT - 1)
            with dve.Fori(1, 3) as cb:
                project(cb, False, False)
            project(3, False, True)

            dve.wait_ge(sq_done, 16)
            own.did(dve.tensor_reduce(stat2[:, 0, :], part_sq[:], AX.X, ALU.add))
            own.wait()
            ts(stat2[:, 1, :], stat2[:, 0, :], 1.0 / D, EPS, ALU.mult, ALU.add).then_inc(var_rdy, 1)
            dve.wait_ge(std_rdy, 2 + 1)
            dve.reciprocal(stat2[:, 3, :], stat2[:, 2, :]).then_inc(inv_rdy, 1)
            dve.wait_ge(inv_rdy, 1)
            dve.wait_ge(m4_rdy, 5)

            def evacuate(t):
                dve.wait_ge(h2_T, t + 1)
                for g in (1, 3):
                    dve.tensor_copy(h2T[:, 4 * g:4 * g + 4, t * P:(t + 1) * P],
                                    bank(4 + g).rearrange("p (j t) -> p j t", j=4)).then_inc(xT_dve, 1)

            for t in range(NTOK - 1):
                own.wait()
                own.did(stt(out=h2[:, t, :], in0=x2[:, t, :], scalar=stat2[:, 3, t:t + 1], in1=m4_row[:],
                            op0=ALU.mult, op1=ALU.mult))
                own.wait()
                tt(h2[:, t, :], h2[:, t, :], m3_row[:], ALU.add).then_inc(h2_rdy, 1)
                if t:
                    evacuate(t - 1)
            for t in (NTOK - 2, NTOK - 1):
                evacuate(t)

            R = lambda i: rt[:, i, :]
            R3 = lambda i: rt[:, i, :].rearrange("p (t e) -> p t e", e=E)
            R4 = lambda i: rt[:, i, :].rearrange("p (g a) -> p g a", a=4)
            SM = lambda i: rt_small[:, i, :]

            def step(ins):
                own.did(ins)
                own.wait()

            def rank(value, out, scratch, width):
                v, o, s = (a.rearrange("p (g a) -> p g a", a=4) for a in (value, out, scratch))
                n = width // 4
                step(dve.memset(out, 0.0))
                for b in range(4):
                    if b < 3:
                        r = s[:, :, b + 1:4]
                        step(tt(r, v[:, :, b:b + 1].to_broadcast([P, n, 3 - b]), v[:, :, b + 1:4], ALU.is_ge))
                        step(tt(o[:, :, b + 1:4], o[:, :, b + 1:4], r, ALU.add))
                    if b > 0:
                        r = s[:, :, 0:b]
                        step(tt(r, v[:, :, b:b + 1].to_broadcast([P, n, b]), v[:, :, 0:b], ALU.is_gt))
                        step(tt(o[:, :, 0:b], o[:, :, 0:b], r, ALU.add))

            dve.wait_ge(score_rdy, 1)
            step(tt(R3(1), R3(0), bias_row[:].unsqueeze(1).to_broadcast([P, NTOK, E]), ALU.add))
            rank(R(1), R(2), R(3), NTOK * E)
            step(stt(out=R(4), in0=R(2), scalar=2.0, in1=R(1), op0=ALU.is_lt, op1=ALU.mult))
            step(dve.tensor_reduce(SM(0), R4(4), AX.X, ALU.add))
            rank(SM(0), SM(1), SM(2), NTOK * GROUPS)
            win_g = SM(3)
            step(ts(win_g, SM(1), 0.0, None, ALU.is_equal))
            of_group = win_g.unsqueeze(2).to_broadcast([P, NTOK * GROUPS, 4])
            step(stt(out=R4(9), in0=R4(2), scalar=0.0, in1=of_group, op0=ALU.is_equal, op1=ALU.mult))
            step(stt(out=R4(10), in0=R4(2), scalar=1.0, in1=of_group, op0=ALU.is_equal, op1=ALU.mult))
            tt(R(8), R(9), R(10), ALU.add).then_inc(sel_rdy, 1)
            for z in range(2):
                step(tt(R(4 + z), R(0), R(9 + z), ALU.mult))
                step(dve.tensor_reduce(gate_w[:, z, :], R3(4 + z), AX.X, ALU.add))
            step(tt(SM(4)[:, 0:NTOK], gate_w[:, 0, :], gate_w[:, 1, :], ALU.add))
            step(dve.reciprocal(SM(4)[:, 4:4 + NTOK], SM(4)[:, 0:NTOK]))
            for z in range(2):
                step(tt(gate_w[:, z, :], gate_w[:, z, :], SM(4)[:, 4:4 + NTOK], ALU.mult))
            dve.wait_ge(pos_mm, 1)
            step(dve.tensor_copy(SM(5), ps[:, 2, 0:E]))
            step(ts(SM(6), SM(5), float(BLK), None, ALU.is_gt))
            step(stt(out=SM(7), in0=SM(5), scalar=2.0 * BLK, in1=SM(6), op0=ALU.is_gt, op1=ALU.add))
            step(stt(out=SM(6), in0=SM(5), scalar=3.0 * BLK, in1=SM(7), op0=ALU.is_gt, op1=ALU.add))
            step(dve.tensor_tensor_scan(SM(8), ones[:, 0:E], SM(6), 0.0, ALU.mult, ALU.add))
            step(tt(SM(9), SM(8), SM(6), ALU.subtract))
            step(ts(SM(9), SM(9), E - 1.0, float(BLK), ALU.add, ALU.mult))
            step(stt(out=SM(10), in0=iota_e, scalar=float(BLK), in1=SM(9), op0=ALU.mult, op1=ALU.subtract))
            step(dve.tensor_copy(R(4), ps[:, 1, 0:NTOK * E]))
            over_t = lambda a: a.unsqueeze(1).to_broadcast([P, NTOK, E])
            step(stt(out=R3(5), in0=R3(4), scalar=float(BLK), in1=over_t(SM(10)), op0=ALU.is_lt, op1=ALU.mult))
            step(tt(R(5), R(5), R(4), ALU.add))
            step(tt(R3(5), R3(5), over_t(SM(9)), ALU.add))
            for z in range(2):
                step(tt(R(6 + z), R(5), R(9 + z), ALU.mult))
                step(dve.tensor_reduce(SM(11)[:, 4 * z:4 * z + NTOK], R3(6 + z), AX.X, ALU.add))
            own.did(dve.tensor_copy(dest_i[:].rearrange("p z t -> p (z t)"), SM(11)[:, 0:2 * NTOK]))
            starts24 = rt[:, 17, 0:NBLK + 1]
            step(ts(starts24, iota[:, 0:NBLK + 1], float(BLK), None, ALU.mult))
            n2 = 2 * NTOK
            step(tt(in_block[:], SM(11)[:, 0:n2].unsqueeze(2).to_broadcast([P, n2, NBLK + 1]),
                    starts24.unsqueeze(1).to_broadcast([P, n2, NBLK + 1]), ALU.is_ge))
            step(dve.tensor_reduce(SM(14)[:, 0:n2], in_block[:], AX.X, ALU.add))
            step(ts(SM(14)[:, 0:n2], SM(14)[:, 0:n2], -float(BLK), float(BLK), ALU.mult, ALU.add))
            step(tt(SM(14)[:, 0:n2], SM(14)[:, 0:n2], SM(11)[:, 0:n2], ALU.add))
            step(tt(block_tok[:], in_block[:, :, 0:NBLK], in_block[:, :, 1:NBLK + 1], ALU.subtract))
            for z in range(2):
                b_z = block_tok[:, NTOK * z:NTOK * z + NTOK, :]
                step(tt(b_z, b_z, tok_ids[:].unsqueeze(2).to_broadcast([P, NTOK, NBLK]), ALU.mult))
            tt(slot_1[:], SM(14)[:, 0:n2].unsqueeze(2).to_broadcast([P, n2, P]),
               iota[:].unsqueeze(1).to_broadcast([P, n2, P]), ALU.is_equal).then_inc(onehot_rdy, 1)
            later = rt[:, 11:13, :].rearrange("p a b -> p (a b)")[:, 0:NXTRA * E].rearrange("p (b e) -> p b e", e=E)
            step(tt(later, SM(8).unsqueeze(1).to_broadcast([P, NXTRA, E]),
                    iota_e[:, 0:NXTRA].unsqueeze(2).to_broadcast([P, NXTRA, E]), ALU.is_le))
            step(dve.tensor_reduce(SM(12)[:, 0:NXTRA], later, AX.X, ALU.add))
            step(ts(SM(12)[:, 0:NXTRA], SM(12)[:, 0:NXTRA], E - 1.0, None, ALU.min))
            step(dve.tensor_copy(SM(12)[:, NXTRA:NXTRA + 1], SM(8)[:, E - 1:E]))
            step(dve.tensor_copy(route_i[:], SM(12)[:, 0:8]))
            step(dve.memset(table_i[:], 0))
            dve.wait_ge(tab_mm, 1)
            dve.tensor_copy(table_i[:, 0:NBLK], ps[:, 3, 0:NBLK]).then_inc(table_rdy, 1)

            def e_lo_unit(g, slot, hslot):
                dve.wait_ge(e_hi_done, g + 1)
                tt(e_lo[:, hslot, :], e_raw[:, slot, :], e_hi[:, hslot, :].bitcast(F32), ALU.subtract
                   ).then_inc(e_split, 1)

            def x_lo(b, part):
                dve.wait_ge(xe_hi_rdy, b * 4 + (part + 1))
                tt(xe_lo[:, 4 * part:4 * part + 4, :].rearrange("p k t -> p (k t)"), bank(6 + part % 2),
                   xe_hi[:, 4 * part:4 * part + 4, :].rearrange("p k t -> p (k t)").bitcast(F32), ALU.subtract
                   ).then_inc(xe_rdy, 1)

            def silu(b, first=False):
                dve.wait_ge(sg_rdy, b + 1)
                if not first:
                    dve.wait_ge(act_rdy, b)
                tt(act_u[:], bank(0), act_sig[:], ALU.mult).then_inc(u_rdy, 1)

            def gate_up(b, units, first=False):
                dve.wait_ge(e_units, units)
                dve.wait_ge(u_rdy, b + 1)
                if not first:
                    dve.wait_ge(act_T, b)
                tt(act[:], bank(1), act_u[:], ALU.mult).then_inc(act_rdy, 1)

            def act_lo(b):
                dve.wait_ge(actT_hi_rdy, b + 1)
                tt(actT_lo[:].rearrange("p k t -> p (k t)"), bank(6),
                   actT_hi[:].rearrange("p k t -> p (k t)").bitcast(F32), ALU.subtract).then_inc(actT_rdy, 1)

            AHEAD = 3
            for q in range(AHEAD):
                e_lo_unit(q, q, q)
            for part in range(4):
                x_lo(0, part)
            for q in range(16):
                n = q + AHEAD
                e_lo_unit(n, n % 8, n % 4)
                if q == 8:
                    silu(0, True)
            gate_up(0, 4 + 16, True)
            for part in range(4):
                x_lo(1, part)
            with dve.Fori(1, E) as e:
                for q in range(24):
                    n = q + AHEAD
                    e_lo_unit(e * 24 + (n - 8), n % 8, n % 4)
                    if q == 3:
                        act_lo(e - 1)
                    if q == 9:
                        silu(e)
                    if q == 17:
                        gate_up(e, e * 24 + 12)
                    if 18 <= q <= 21:
                        x_lo(e + 1, q - 18)
            act_lo(E - 1)
            for q in range(AHEAD, 8):
                n = E * 24 - 8 + q
                e_lo_unit(n, n % 8, n % 4)
            n_extra = dve.value_load(route_i[0:1, 7:8], min_val=0, max_val=NXTRA)
            with dve.Fori(0, NXTRA) as b:
                with dve.If(b < n_extra):
                    for part in range(4):
                        x_lo(b + (E + 1), part)
                    for q in range(24):
                        e_lo_unit(b * 24 + (24 * E + q), q % 8, q % 4)
                        if q == 10:
                            silu(b + E)
                        if q == 16:
                            gate_up(b + E, b * 24 + (24 * E + 20))
                            act_lo(b + E)
                dve.nop()

            def finish(i):
                o = o_sb[:, i, :]
                dve.wait_ge(ssq_rdy, 2 + i + 1)
                ts(stat2[:, 1, i:i + 1], stat2[:, 0, i:i + 1], 1.0 / D, EPS, ALU.mult, ALU.add).then_inc(var_rdy, 1)
                dve.wait_ge(std_rdy, 3 + i + 1)
                step(dve.reciprocal(stat2[:, 3, i:i + 1], stat2[:, 2, i:i + 1]))
                stt(out=o, in0=o, scalar=stat2[:, 3, i:i + 1], in1=fn_row[:], op0=ALU.mult, op1=ALU.mult
                    ).then_inc(o_rdy, 1)

            dve.wait_ge(rows_in, 6 * 16)
            for i in range(NTOK):
                o = o_sb[:, i, :]
                dve.wait_ge(y_in[i], 32)
                step(stt(out=o, in0=y0[:, i, :], scalar=gate_w[:, 0, i:i + 1], in1=x2[:, i, :], op0=ALU.mult,
                         op1=ALU.add))
                stt(out=o, in0=y1[:, i, :], scalar=gate_w[:, 1, i:i + 1], in1=o, op0=ALU.mult, op1=ALU.add
                    ).then_inc(f_sum, 1)
                if i:
                    finish(i - 1)
            finish(NTOK - 1)

        @block.gpsimd
        def _(pool):
            own = Chain(pool, p_own)
            tt, ts = pool.tensor_tensor, pool.tensor_scalar

            own.did(pool.memset(osq[:], 0.0))
            own.wait()
            pool.dma_start(y_d[E * BLK:, :].rearrange("(p r) (s n) -> p (r s) n", p=P, n=512),
                           osq[:].unsqueeze(1).to_broadcast([P, NXTRA * D // 512, 512])).then_inc(row_out, 16)
            pool.wait_ge(row_out, 16)

            def lower_bound(h):
                own.wait()
                own.did(pool.tensor_copy(lb_p[:], lb_all[:, ds(h, 1), :].rearrange("p o w -> p (o w)")))
                own.wait()
                own.pass_waits()

            def ctx_scan(h, lag):
                pool.wait_ge(c_sig_b, h + 1)
                lower_bound(h)
                if lag:
                    pool.wait_ge(c_kg_T, h)
                    pool.wait_ge(c_kg_b, h)
                    own.pass_waits()
                own.did(ts(c_f[:, 1, :], c_sig[:, 1, :], lb_p[:, 3:4], lb_p[:, 2:3], ALU.mult, ALU.add))
                own.wait()
                own.pass_waits()
                own.did(ts(c_kg[:, 1, :], c_f[:, 1, :], -1.0, 1.0, ALU.mult, ALU.add))
                ctx_decays(pool, own, 1, 1, CTX_LEVELS).then_inc(c_kg_b, 1)

            ctx_scan(0, False)
            with pool.Fori(1, HEADS) as h:
                own.loop(h - 1, PER["ctx_p"])
                ctx_scan(h, True)
                own.end(HEADS - 1)

            pool.wait_ge(ctx_state, HEADS + 1)
            pool.memset(up[:], 0.0).then_inc(pad_rdy, 1)

            def windows(h):
                pool.wait_ge(p_ev, h + 1)
                pool.wait_ge(coef_in, h * 16 + 16)
                u = up[:, :, HALO:HALO + GRID_W]
                src = up
                for m, (a, b, off) in enumerate(((1, 79, None), (2, 78, 1), (4, 76, 2), (8, 72, 4))):
                    dst = win[m % 2]
                    l, r = (1, 0) if off is None else (off, off)
                    lo_ = src[:, :, a - l:b - l]
                    hi_ = src[:, :, a:b] if off is None else src[:, :, a + r:b + r]
                    own.wait()
                    own.did(tt(dst[:, :, a:b], lo_, hi_, ALU.add))
                    own.wait()
                    c_m = coef[:, m, :].unsqueeze(1).to_broadcast([P, ROWS, GRID_W])
                    t = pool_acc if m == 0 else pool_t
                    own.did(tt(t[:], dst[:, :, HALO:HALO + GRID_W], c_m, ALU.mult))
                    if m:
                        own.wait()
                        own.did(tt(pool_acc[:], pool_acc[:], pool_t[:], ALU.add))
                    src = dst
                own.wait()
                tt(delta[:, ds(h, 1), :].rearrange("p o (r w) -> p (o r) w", w=GRID_W), pool_acc[:], u, ALU.subtract
                   ).then_inc(pool_rdy, 1)

            def lat_scan(h, lag):
                if lag:
                    pool.wait_ge(pool_rdy, h)
                own.wait()
                pool.dma_start(coef[:], pool_coefs[ds(h, 1)].rearrange("o p m w -> (o p) m w")).then_inc(coef_in, 16)
                pool.wait_ge(sig_bw, h + 1)
                lower_bound(h)
                own.did(ts(f_sb[1][:], sig_b[:], lb_p[:, 3:4], lb_p[:, 2:3], ALU.mult, ALU.add))
                own.wait()
                if lag:
                    pool.wait_ge(o_mm[1], h)
                    pool.wait_ge(lv_up[1], h * LEVELS)
                    own.pass_waits()
                own.did(ts(KG[1][:], f_sb[1][:], -1.0, 1.0, ALU.mult, ALU.add))
                pool.wait_ge(q_rdy, h + 1)
                tt(QF[1][:], q_sb[:], f_sb[1][:], ALU.mult).then_inc(fb_rdy, 1)
                for l in range(1, LEVELS + 1):
                    pool.wait_ge(lv_mm[1], h * 8 + (l + 1))
                    own.wait()
                    if l == 1:
                        pool.wait_ge(fb_rdy, h + 1)
                    else:
                        pool.wait_ge(lv_up[1], h * LEVELS + (l - 1))
                    grow(pool, own, QF[1][:], KG[1][:], level_T(1, l - 1), level_T(1, l), 1 << (l - 1), False,
                         SEQ).then_inc(lv_up[1], 1)
                windows(h)

            lat_scan(0, False)
            with pool.Fori(1, HEADS) as h:
                own.loop(h - 1, PER["lat_p"])
                lat_scan(h, True)
                own.end(HEADS - 1)

            pool.wait_ge(o_mm[1], HEADS)
            pool.wait_ge(kgT_rdy[1], HEADS)
            pool.wait_ge(pool_rdy, HEADS)
            pool.dma_start(w_pg[:], w_pg_d).then_inc(coef_in, 16)
            pool.wait_ge(pg_mm, HEADS)

            def load_ada(j, q):
                pool.wait_ge(ada2_free, j * 4 + (q + 1))
                pool.dma_start(ada2[:, q % 2], w_ada_d[:, 4 * q:4 * q + 4, ds(j * 512 + 2 * D, 512)]
                               ).then_inc(ada2_in[q % 2], 16)

            def merge(j, last):
                pool.wait_ge(row_rdy, j + 1)
                pool.dma_start(b_row[0:1, :], b_ada[0:1, ds(j * 512 + 2 * D, 512)]).then_inc(b_in, 16)
                if not last:
                    load_ada(j, 2)
                    load_ada(j, 3)
                pool.wait_ge(m_rdy, j + 2)
                pool.dma_start(m_d[ds(j, 1)].rearrange("o p t -> (o p) t"), m_row[:]).then_inc(row_out, 16)
                if not last:
                    load_ada(j + 1, 0)
                    load_ada(j + 1, 1)
                    pool.wait_ge(row_rdy, j + 2)
                    pool.dma_start(mod_d[0:1, ds(j * 512, 512)], mod_row[0:1, :]).then_inc(row_out, 16)

            load_ada(0, 0)
            load_ada(0, 1)
            with pool.Fori(0, KT - 1) as j:
                merge(j, False)
            merge(KT - 1, True)
            load_ada(KT - 1, 2)
            load_ada(KT - 1, 3)

            pool.wait_ge(row_out, 32 * KT)
            pool.wait_ge(m_rdy, KT + 1)
            pool.wait_ge(units_done, 2 + S_W)
            x_all = x[0].rearrange("(t p) d -> p t d", p=P)
            pool.dma_start(m4_row[:], mod_d[0, 2 * D:3 * D].partition_broadcast(P)).then_inc(rows_in, 16)
            pool.dma_start(m3_row[:], mod_d[0, D:2 * D].partition_broadcast(P)).then_inc(rows_in, 16)
            pool.dma_start(w_r[:], w_r_d).then_inc(rows_in, 16)
            pool.dma_start(bias_row[:], router_bias.partition_broadcast(P)).then_inc(rows_in, 16)

            def load_block(cb):
                pool.wait_ge(x2_rdy, cb * 4 + 4)
                pool.wait_ge(m4_rdy, cb + 1)
                pool.dma_start(n2_part[:], norm2_w[0, ds(cb * 512, 512)].partition_broadcast(P)).then_inc(xp_in, 16)
                pool.dma_start(x_part[:], x_all[:, :, ds(cb * 512, 512)]).then_inc(xp_in, 16)
                pool.dma_start(m2_part[:], mod_d[0, ds(cb * 512, 512)].partition_broadcast(P)).then_inc(xp_in, 16)

            load_block(0)
            pool.wait_ge(row_rdy, KT + 1)
            pool.dma_start(mod_d[0:1, (KT - 1) * 512:KT * 512], mod_row[0:1, :]).then_inc(row_out, 16)
            with pool.Fori(1, 4) as cb:
                load_block(cb)

            h2_rows = h2_d.rearrange("(t p) d -> t p d", p=P)
            pool.wait_ge(m4_rdy, 5)
            pool.wait_ge(h2_scaled, 1)
            own.did(tt(h2[:, NTOK - 1, :], h2[:, NTOK - 1, :], m4_row[:], ALU.mult))
            own.wait()
            tt(h2[:, NTOK - 1, :], h2[:, NTOK - 1, :], m3_row[:], ALU.add).then_inc(h2_last, 1)
            pool.wait_ge(h2_last, 1)
            for t in range(NTOK):
                if t < NTOK - 1:
                    pool.wait_ge(h2_rdy, t + 1)
                pool.dma_start(h2_rows[t], h2[:, t, :]).then_inc(y_out, 16)
            pool.wait_ge(row_out, 16 + 32 * KT)
            pool.wait_ge(y_out, 16 * NTOK)
            pool.wait_ge(h2_T, NTOK)
            pool.dma_start(m5_row[:], mod_d[0, 3 * D:4 * D].partition_broadcast(P)).then_inc(rows_in, 16)
            pool.dma_start(fn_row[:], final_norm_w.partition_broadcast(P)).then_inc(rows_in, 16)
            pool.wait_ge(table_rdy, 1)

            def gather(b, column):
                own.wait()
                own.did(pool.tensor_copy(idx_now[:], table_i[:, ds(column, 1)]))
                own.wait()
                own.pass_waits()
                pool.indirect_dma_start(out=xe[:], out_offset=None, in_=h2_d,
                                        in_offset=bass.IndirectOffsetOnAxis(ap=idx_now[:, 0:1], axis=0)
                                        ).then_inc(xe_in, 16)

            def store(b):
                for n in range(2):
                    cols = slice(n * D // 2, (n + 1) * D // 2)
                    pool.wait_ge(y_ev, b * 4 + (6 + 2 * n))
                    own.did(tt(y_sb[:, cols], y_sb[:, cols], m5_row[:, cols], ALU.mult))
                    own.wait()
                    pool.dma_start(y_d[ds(b * BLK, BLK), cols], y_sb[:, cols]).then_inc(y_out, 16)

            pool.wait_ge(rows_in, 6 * 16)
            gather(0, 0)
            pool.wait_ge(xe_in, 16)
            pool.wait_ge(xe_T, 4)
            gather(1, 1)
            with pool.Fori(1, E) as e:
                own.loop(e - 1, 4)
                pool.wait_ge(xe_in, e * 16 + 16)
                pool.wait_ge(xe_T, e * 4 + 4)
                gather(e + 1, e + 1)
                store(e - 1)
                own.end(E - 1)
            store(E - 1)
            pool.wait_ge(y_out, 16 * (2 * E + NTOK))
            pool.wait_ge(xe_in, 16 * (E + 1))
            n_extra = pool.value_load(route_i[0:1, 7:8], min_val=0, max_val=NXTRA)
            with pool.Fori(0, NXTRA) as b:
                with pool.If(b < n_extra):
                    own.loop(b, 4)
                    pool.wait_ge(xe_T, b * 4 + 4 * (E + 1))
                    gather(b + (E + 1), b + E)
                    pool.wait_ge(xe_in, b * 16 + 16 * (E + 2))
                    store(b + E)
                    pool.wait_ge(y_out, b * 32 + 16 * (2 * E + NTOK + 2))
                    own.end(0)
                pool.nop()

            for i in range(NTOK):
                for z, dst in ((0, y0), (1, y1)):
                    pool.indirect_dma_start(out=dst[:, i, :], out_offset=None, in_=y_d,
                                            in_offset=bass.IndirectOffsetOnAxis(ap=dest_i[:, z, i:i + 1], axis=0)
                                            ).then_inc(y_in[i], 16)


PER = dict(ctx_v=17, ctx_p=20, lat_v=39, lat_p=30, merge_v=13)

_INS = ["x", "c", "ctx", "c_ctx", "w_ada", "b_ada", "norm1_w", "norm2_w", "w_in", "w_pool_group", "pool_scale",
        "hg_norm_w", "lb_logits", "w_branch_pool", "w_branch_hgrn", "w_out", "w_router", "router_bias",
        "w_e1", "w_e3", "w_e2", "final_norm_w"]


def shape_constants():
    i = np.arange(P)
    const = np.zeros((P, 3 * P + NTOK), np.float32)
    const[:, 0:P] = np.eye(P)
    const[:, P:2 * P] = i[:, None] < i[None, :]
    const[:, 2 * P:3 * P] = i
    const[:, 3 * P:] = i[:, None] + P * np.arange(NTOK)
    s, t = i[:, None], i[None, :]
    masks = np.zeros((P, 2, LEVELS, P), np.float32)
    for l in range(LEVELS):
        same = (s >> (l + 1)) == (t >> (l + 1))
        masks[:, 0, l] = same & ((t >> l) & 1 == 1) & ((s >> l) & 1 == 0)
        masks[:, 1, l] = same & ((t >> l) & 1 == 0) & ((s >> l) & 1 == 1)
    w = np.arange(GRID_W)
    coefs = np.zeros((HEADS, P, 4, GRID_W), np.float32)
    for h in range(HEADS):
        m = h // 2
        half = WINDOWS[m] // 2
        count = np.minimum(w + half - 1, GRID_W - 1) - np.maximum(w - half, 0) + 1
        coefs[h, :, m, :] = 1.0 / count
    halves = np.zeros((P, 2, LEVELS, P // 2), np.float32)
    for z in range(2):
        for l in range(LEVELS):
            halves[:, z, l] = masks[:, z, l].reshape(P, -1, 2, 1 << l)[:, :, 1 - z].reshape(P, P // 2)
    return const, halves, coefs


def kernel(**inputs):
    import concourse.bacc as _bacc
    from concourse.bass_utils import run_bass_kernel_spmd as _run

    nc = _bacc.Bacc("TRN2", target_bir_lowering=False, num_devices=1)
    arrays, args = {}, []

    def give(name, a):
        a = np.ascontiguousarray(a)
        arrays[f"in_{name}"] = a
        args.append(nc.dram_tensor(f"in_{name}", a.shape, mybir.dt.from_np(a.dtype), kind="ExternalInput").ap())

    for name in _INS:
        give(name, inputs[name])
    for name, a in zip(("consts", "level_masks", "pool_coefs"), shape_constants()):
        give(name, a)
    out = nc.dram_tensor("out_0", (1, SEQ, D), F32, kind="ExternalOutput").ap()
    build(nc, *args, out)
    r = _run(nc, [arrays], core_ids=[0])
    return r.results[0]["out_0"]
```
